# Optimizing a Trainium2 kernel written in Bass

```python
import math
import jax, jax.numpy as jnp
from jax import lax
import numpy as np

D_MODEL = 1024
BATCH = 1
SEQ = 256
DEPTH = 1

NORM_EPS = 1e-6
L2_EPS = 1e-6
ROPE_THETA = 500000.0
NEG_INF = -1e30

GDN_HEADS = 8
GDN_DK = 128
GDN_DV = 128
GDN_CONV = 4
GDN_CHUNK = 64

NSA_HEADS = 8
NSA_GROUPS = 2
NSA_REP = NSA_HEADS // NSA_GROUPS
NSA_DK = 128
NSA_DV = 128
ROT_DIM = NSA_DK // 4
CMP_LEN = 32
CMP_STRIDE = 16
SEL_LEN = 64
SEL_TOPK = 16
WINDOW = 512
Q_BLOCK = 128
SEL_FORCE = 1e4

MEM_LEN = 256
XATTN_HEADS = 4
XATTN_DH = 128

N_EXPERTS = 32
TOP_K = 4
D_EXPERT = D_MODEL
SWIGLU_LIMIT = 7.0
SWIGLU_ALPHA = 1.702
MOE_BLOCK = 256

IN_WIDTHS = (
    GDN_HEADS * GDN_DK,
    GDN_HEADS * GDN_DK,
    GDN_HEADS * GDN_DV,
    GDN_HEADS * GDN_DV,
    GDN_HEADS,
    GDN_HEADS,
    NSA_HEADS * NSA_DK,
    NSA_GROUPS * NSA_DK,
    NSA_GROUPS * NSA_DV,
    NSA_GROUPS * NSA_DK,
    NSA_GROUPS * NSA_DV,
    NSA_GROUPS * NSA_DK,
    NSA_GROUPS * NSA_DV,
    NSA_HEADS * 3,
    D_MODEL,
    D_MODEL,
)
D_IN = sum(IN_WIDTHS)

kernel_name = 'hybrid_gdn_nsa_moe_block'

def rms_norm(x, gain):
    xf = x.astype(jnp.float32)
    y = xf * lax.rsqrt(jnp.mean(xf * xf, axis=-1, keepdims=True) + NORM_EPS)
    return (y * gain.astype(jnp.float32)).astype(x.dtype)

def l2_normalize(x):
    xf = x.astype(jnp.float32)
    return xf * lax.rsqrt(jnp.sum(xf * xf, axis=-1, keepdims=True) + L2_EPS)

def partial_rope(x, pos):
    half = ROT_DIM // 2
    inv_freq = jnp.exp(-math.log(ROPE_THETA) * jnp.arange(half, dtype=jnp.float32) * (2.0 / ROT_DIM))
    ang = pos.astype(jnp.float32)[:, None] * inv_freq[None, :]
    cos = jnp.cos(ang)[None, :, None, :]
    sin = jnp.sin(ang)[None, :, None, :]
    xr = x[..., :ROT_DIM].astype(jnp.float32)
    x1, x2 = xr[..., :half], xr[..., half:]
    rot = jnp.concatenate([x1 * cos - x2 * sin, x2 * cos + x1 * sin], axis=-1)
    return jnp.concatenate([rot.astype(x.dtype), x[..., ROT_DIM:]], axis=-1)

def masked_softmax(s, mask):
    s = jnp.where(mask, s.astype(jnp.float32), NEG_INF)
    m = jnp.max(s, axis=-1, keepdims=True)
    p = jnp.where(mask, jnp.exp(s - m), 0.0)
    return p / jnp.maximum(jnp.sum(p, axis=-1, keepdims=True), 1e-30)

def causal_depthwise_conv_silu(x, w):
    c = x.shape[-1]
    y = lax.conv_general_dilated(
        x, w.astype(x.dtype)[:, None, :], window_strides=(1,),
        padding=[(w.shape[0] - 1, 0)], dimension_numbers=('NWC', 'WIO', 'NWC'),
        feature_group_count=c)
    return jax.nn.silu(y)

def gated_delta_rule(q, k, v, g, beta):
    bsz, seq, nh, dk = q.shape
    dv = v.shape[-1]
    c = GDN_CHUNK
    n = seq // c
    f32 = jnp.float32

    def chunks(a):
        a = jnp.moveaxis(a.astype(f32), 2, 1)
        return a.reshape((bsz, nh, n, c) + a.shape[3:])

    q = chunks(q) * (dk ** -0.5)
    k = chunks(k)
    v = chunks(v)
    beta = chunks(beta)
    g = jnp.cumsum(chunks(g), axis=-1)
    kb = k * beta[..., None]
    vb = v * beta[..., None]
    incl = jnp.tril(jnp.ones((c, c), dtype=bool))
    strict = jnp.tril(jnp.ones((c, c), dtype=bool), -1)
    diff = g[..., :, None] - g[..., None, :]
    decay = jnp.where(incl, jnp.exp(jnp.where(incl, diff, 0.0)), 0.0)
    a_mat = jnp.where(strict, jnp.einsum('bhnid,bhnjd->bhnij', kb, k) * decay, 0.0)
    eye = jnp.eye(c, dtype=f32)
    t_mat = lax.linalg.triangular_solve(a_mat + eye, jnp.broadcast_to(eye, a_mat.shape),
                                        left_side=True, lower=True, unit_diagonal=True)
    u = t_mat @ vb
    w = t_mat @ (kb * jnp.exp(g)[..., None])
    qk = jnp.einsum('bhnid,bhnjd->bhnij', q, k) * decay
    q_dec = q * jnp.exp(g)[..., None]
    k_dec = k * jnp.exp(g[..., -1:] - g)[..., None]
    g_last = jnp.exp(g[..., -1])

    def step(state, xs):
        u_n, w_n, qk_n, qd_n, kd_n, gl_n = xs
        v_new = u_n - jnp.einsum('bhck,bhkv->bhcv', w_n, state)
        o = jnp.einsum('bhck,bhkv->bhcv', qd_n, state) + jnp.einsum('bhij,bhjv->bhiv', qk_n, v_new)
        state = state * gl_n[..., None, None] + jnp.einsum('bhck,bhcv->bhkv', kd_n, v_new)
        return state, o

    xs = (jnp.moveaxis(u, 2, 0), jnp.moveaxis(w, 2, 0), jnp.moveaxis(qk, 2, 0),
          jnp.moveaxis(q_dec, 2, 0), jnp.moveaxis(k_dec, 2, 0), jnp.moveaxis(g_last, 2, 0))
    s0 = jnp.zeros((bsz, nh, dk, dv), f32)
    _, o = lax.scan(step, s0, xs)
    o = jnp.moveaxis(o, 0, 2).reshape(bsz, nh, seq, dv)
    return jnp.moveaxis(o, 1, 2)

def nsa_attention(q, k_cmp, v_cmp, k_slc, v_slc, k_win, v_win, branch_gates,
                  pe_k, w1_k, w2_k, pe_v, w1_v, w2_v):
    bsz, seq = q.shape[0], q.shape[1]
    f32 = jnp.float32
    pos = jnp.arange(seq)
    scale = NSA_DK ** -0.5
    q_rot = partial_rope(q, pos)
    k_slc = partial_rope(k_slc, pos)
    k_win = partial_rope(k_win, pos)

    n_cmp = (seq - CMP_LEN) // CMP_STRIDE + 1
    cmp_idx = jnp.arange(n_cmp)[:, None] * CMP_STRIDE + jnp.arange(CMP_LEN)[None, :]
    cmp_end = jnp.arange(n_cmp) * CMP_STRIDE + (CMP_LEN - 1)

    def compress(a, pe, w1, w2):
        blk = a[:, cmp_idx] + pe[:, None, :]
        blk = jnp.moveaxis(blk, 3, 2).reshape(bsz, n_cmp, NSA_GROUPS, -1)
        return jax.nn.silu(blk @ w1) @ w2

    kc = compress(k_cmp, pe_k, w1_k, w2_k)
    vc = compress(v_cmp, pe_v, w1_v, w2_v)

    n_sel = seq // SEL_LEN
    top_n = min(SEL_TOPK, n_sel)
    r_s = SEL_LEN // CMP_STRIDE
    r_c = CMP_LEN // CMP_STRIDE
    offs = np.array([m - nn for m in range(r_s) for nn in range(r_c)], dtype=np.int32)
    cidx = jnp.arange(n_sel)[:, None] * r_s + offs[None, :]
    ok = ((cidx >= 0) & (cidx < n_cmp)).astype(f32)
    wmap = jnp.sum(jax.nn.one_hot(jnp.clip(cidx, 0, n_cmp - 1), n_cmp, dtype=f32) * ok[..., None], axis=1).T
    sel_ids = jnp.arange(n_sel)
    sel_start = sel_ids * SEL_LEN

    qg = q.reshape(bsz, seq, NSA_GROUPS, NSA_REP, NSA_DK)
    qrg = q_rot.reshape(bsz, seq, NSA_GROUPS, NSA_REP, NSA_DK)
    ks_t = jnp.moveaxis(k_slc, 2, 1)
    vs_t = jnp.moveaxis(v_slc, 2, 1)
    kw_pad = jnp.pad(k_win, ((0, 0), (WINDOW, 0), (0, 0), (0, 0)))
    vw_pad = jnp.pad(v_win, ((0, 0), (WINDOW, 0), (0, 0), (0, 0)))
    b_idx = jnp.arange(bsz)[:, None, None]
    g_idx = jnp.arange(NSA_GROUPS)[None, :, None]
    sel_off = jnp.arange(SEL_LEN)
    win_off = jnp.arange(WINDOW + Q_BLOCK) - WINDOW
    n_keys_sel = top_n * SEL_LEN

    def query_block(i):
        q0 = i * Q_BLOCK
        tq = q0 + jnp.arange(Q_BLOCK)
        qb = lax.dynamic_slice_in_dim(qg, q0, Q_BLOCK, axis=1)
        qrb = lax.dynamic_slice_in_dim(qrg, q0, Q_BLOCK, axis=1)
        s_c = jnp.einsum('bqgrd,bngd->bgrqn', qb, kc) * scale
        p_c = masked_softmax(s_c, cmp_end[None, :] <= tq[:, None])
        o_c = jnp.einsum('bgrqn,bngd->bqgrd', p_c, vc)
        imp = jnp.einsum('bgrqn,ns->bgqs', p_c, wmap)
        cur = tq // SEL_LEN
        forced = (sel_ids[None, :] == 0) | (sel_ids[None, :] == cur[:, None]) | (sel_ids[None, :] == cur[:, None] - 1)
        causal_blk = sel_start[None, :] <= tq[:, None]
        score = jnp.where(causal_blk, imp + jnp.where(forced, SEL_FORCE, 0.0), -SEL_FORCE)
        _, sel = lax.top_k(score, top_n)
        tok = (sel[..., None] * SEL_LEN + sel_off).reshape(bsz, NSA_GROUPS, Q_BLOCK * n_keys_sel)
        ks = ks_t[b_idx, g_idx, tok].reshape(bsz, NSA_GROUPS, Q_BLOCK, n_keys_sel, NSA_DK)
        vs = vs_t[b_idx, g_idx, tok].reshape(bsz, NSA_GROUPS, Q_BLOCK, n_keys_sel, NSA_DV)
        s_s = jnp.einsum('bqgrd,bgqkd->bgrqk', qrb, ks) * scale
        m_s = tok.reshape(bsz, NSA_GROUPS, Q_BLOCK, n_keys_sel) <= tq[None, None, :, None]
        p_s = masked_softmax(s_s, m_s[:, :, None])
        o_s = jnp.einsum('bgrqk,bgqkd->bqgrd', p_s, vs)
        kw = lax.dynamic_slice_in_dim(kw_pad, q0, WINDOW + Q_BLOCK, axis=1)
        vw = lax.dynamic_slice_in_dim(vw_pad, q0, WINDOW + Q_BLOCK, axis=1)
        tk = q0 + win_off
        dlt = tq[:, None] - tk[None, :]
        m_w = (dlt >= 0) & (dlt < WINDOW) & (tk[None, :] >= 0)
        s_w = jnp.einsum('bqgrd,bkgd->bgrqk', qrb, kw) * scale
        p_w = masked_softmax(s_w, m_w)
        o_w = jnp.einsum('bgrqk,bkgd->bqgrd', p_w, vw)
        return o_c, o_s, o_w

    n_qb = seq // Q_BLOCK
    o_c, o_s, o_w = lax.map(query_block, jnp.arange(n_qb))

    def unblock(o):
        return jnp.moveaxis(o, 0, 1).reshape(bsz, seq, NSA_HEADS, NSA_DV)

    gts = jax.nn.sigmoid(branch_gates.astype(f32))
    return gts[..., 0:1] * unblock(o_c) + gts[..., 1:2] * unblock(o_s) + gts[..., 2:3] * unblock(o_w)

def memory_cross_attention(h, m, w_q, w_kv, w_o):
    bsz, seq, _ = h.shape
    q = (h @ w_q).reshape(bsz, seq, XATTN_HEADS, XATTN_DH)
    k, v = jnp.split(m @ w_kv, 2, axis=-1)
    k = k.reshape(bsz, -1, XATTN_HEADS, XATTN_DH)
    v = v.reshape(bsz, -1, XATTN_HEADS, XATTN_DH)
    s = jnp.einsum('bthd,bmhd->bhtm', q, k).astype(jnp.float32) * (XATTN_DH ** -0.5)
    p = jax.nn.softmax(s, axis=-1)
    o = jnp.einsum('bhtm,bmhd->bthd', p, v).reshape(bsz, seq, XATTN_HEADS * XATTN_DH)
    return (o.astype(h.dtype) @ w_o)

def clamped_swiglu(gu):
    gate, up = jnp.split(gu, 2, axis=-1)
    gate = jnp.minimum(gate, SWIGLU_LIMIT)
    up = jnp.clip(up, -SWIGLU_LIMIT, SWIGLU_LIMIT)
    return gate * jax.nn.sigmoid(gate * SWIGLU_ALPHA) * (up + 1.0)

def moe_ffn(h, router_w, router_b, w_gu, b_gu, w_dn, b_dn):
    bsz, seq, d = h.shape
    n_tok = bsz * seq
    hf = h.reshape(n_tok, d)
    logits = (hf @ router_w + router_b).astype(jnp.float32)
    top_v, top_e = lax.top_k(logits, TOP_K)
    gates = jax.nn.softmax(top_v, axis=-1)
    n_pairs = n_tok * TOP_K
    flat_e = top_e.reshape(-1)
    flat_tok = jnp.arange(n_pairs) // TOP_K
    flat_gate = gates.reshape(-1)
    order = jnp.argsort(flat_e)
    e_sorted = flat_e[order]
    counts = jnp.bincount(flat_e, length=N_EXPERTS)
    padded = ((counts + MOE_BLOCK - 1) // MOE_BLOCK) * MOE_BLOCK
    start = jnp.cumsum(counts) - counts
    pstart = jnp.cumsum(padded) - padded
    dest = pstart[e_sorted] + jnp.arange(n_pairs) - start[e_sorted]
    n_rows = n_pairs + N_EXPERTS * MOE_BLOCK
    n_blocks = n_rows // MOE_BLOCK
    row_tok = jnp.zeros((n_rows,), jnp.int32).at[dest].set(flat_tok[order])
    row_gate = jnp.zeros((n_rows,), jnp.float32).at[dest].set(flat_gate[order])
    block_exp = jnp.minimum(
        jnp.searchsorted(jnp.cumsum(padded), jnp.arange(n_blocks) * MOE_BLOCK, side='right'),
        N_EXPERTS - 1)
    xs = hf[row_tok].reshape(n_blocks, MOE_BLOCK, d)

    def expert_block(args):
        xb, e = args
        gu = xb @ w_gu[e] + b_gu[e]
        return clamped_swiglu(gu) @ w_dn[e] + b_dn[e]

    y = lax.map(expert_block, (xs, block_exp)).reshape(n_rows, d)
    out = jax.ops.segment_sum(y.astype(jnp.float32) * row_gate[:, None], row_tok, num_segments=n_tok)
    return out.reshape(bsz, seq, d).astype(h.dtype)

def setup_inputs(seed: int = 0) -> dict:
    key = jax.random.key(seed)
    ks = jax.random.split(key, 32)
    f32 = jnp.float32
    L = DEPTH

    def nrm(k, shape, scale):
        return jax.random.normal(k, shape, f32) * scale

    def gain(k, shape):
        return 1.0 + 0.05 * jax.random.normal(k, shape, f32)

    dt = jnp.exp(jax.random.uniform(ks[6], (L, GDN_HEADS), f32, math.log(1e-3), math.log(1e-1)))
    xd = XATTN_HEADS * XATTN_DH
    return {
        'x': nrm(ks[0], (BATCH, SEQ, D_MODEL), 1.0),
        'mem': nrm(ks[1], (BATCH, MEM_LEN, D_MODEL), 1.0),
        'attn_norm_g': gain(ks[2], (L, D_MODEL)),
        'w_in': nrm(ks[3], (L, D_MODEL, D_IN), D_MODEL ** -0.5),
        'gdn_conv_w': nrm(ks[4], (L, GDN_CONV, 2 * GDN_HEADS * GDN_DK + GDN_HEADS * GDN_DV), GDN_CONV ** -0.5),
        'gdn_a_log': jnp.log(jax.random.uniform(ks[5], (L, GDN_HEADS), f32, 1.0, 16.0)),
        'gdn_dt_bias': dt + jnp.log(-jnp.expm1(-dt)),
        'gdn_norm_g': gain(ks[7], (L, GDN_DV)),
        'cmp_pe_k': nrm(ks[8], (L, CMP_LEN, NSA_DK), 0.1),
        'cmp_w1_k': nrm(ks[9], (L, CMP_LEN * NSA_DK, NSA_DK), (CMP_LEN * NSA_DK) ** -0.5),
        'cmp_w2_k': nrm(ks[10], (L, NSA_DK, NSA_DK), NSA_DK ** -0.5),
        'cmp_pe_v': nrm(ks[11], (L, CMP_LEN, NSA_DV), 0.1),
        'cmp_w1_v': nrm(ks[12], (L, CMP_LEN * NSA_DV, NSA_DV), (CMP_LEN * NSA_DV) ** -0.5),
        'cmp_w2_v': nrm(ks[13], (L, NSA_DV, NSA_DV), NSA_DV ** -0.5),
        'w_branch_a': nrm(ks[14], (L, GDN_HEADS * GDN_DV, D_MODEL), (GDN_HEADS * GDN_DV) ** -0.5),
        'w_branch_b': nrm(ks[15], (L, NSA_HEADS * NSA_DV, D_MODEL), (NSA_HEADS * NSA_DV) ** -0.5),
        'w_mix_out': nrm(ks[16], (L, D_MODEL, D_MODEL), D_MODEL ** -0.5),
        'xattn_norm_g': gain(ks[17], (L, D_MODEL)),
        'mem_norm_g': gain(ks[18], (L, D_MODEL)),
        'xattn_w_q': nrm(ks[19], (L, D_MODEL, xd), D_MODEL ** -0.5),
        'xattn_w_kv': nrm(ks[20], (L, D_MODEL, 2 * xd), D_MODEL ** -0.5),
        'xattn_w_o': nrm(ks[21], (L, xd, D_MODEL), xd ** -0.5),
        'ffn_norm_g': gain(ks[22], (L, D_MODEL)),
        'router_w': nrm(ks[23], (L, D_MODEL, N_EXPERTS), D_MODEL ** -0.5),
        'router_b': nrm(ks[24], (L, N_EXPERTS), 0.01),
        'w_gate_up': nrm(ks[25], (L, N_EXPERTS, D_MODEL, 2 * D_EXPERT), D_MODEL ** -0.5),
        'b_gate_up': nrm(ks[26], (L, N_EXPERTS, 2 * D_EXPERT), 0.01),
        'w_down': nrm(ks[27], (L, N_EXPERTS, D_EXPERT, D_MODEL), D_EXPERT ** -0.5),
        'b_down': nrm(ks[28], (L, N_EXPERTS, D_MODEL), 0.01),
        'final_norm_g': gain(ks[29], (D_MODEL,)),
    }

def reference(x, mem, attn_norm_g, w_in, gdn_conv_w, gdn_a_log, gdn_dt_bias, gdn_norm_g,
              cmp_pe_k, cmp_w1_k, cmp_w2_k, cmp_pe_v, cmp_w1_v, cmp_w2_v,
              w_branch_a, w_branch_b, w_mix_out, xattn_norm_g, mem_norm_g,
              xattn_w_q, xattn_w_kv, xattn_w_o, ffn_norm_g, router_w, router_b,
              w_gate_up, b_gate_up, w_down, b_down, final_norm_g):
    f32 = jnp.float32
    bsz, seq, _ = x.shape
    cuts = [int(c) for c in np.cumsum(IN_WIDTHS)[:-1]]
    gdn_qk = GDN_HEADS * GDN_DK
    for l in range(DEPTH):
        h = rms_norm(x, attn_norm_g[l])
        (g_q, g_k, g_v, g_z, g_b, g_a, n_q, n_kc, n_vc, n_ks, n_vs, n_kw, n_vw,
         n_gate, m_a, m_b) = jnp.split(h @ w_in[l], cuts, axis=-1)

        qkv = causal_depthwise_conv_silu(jnp.concatenate([g_q, g_k, g_v], axis=-1), gdn_conv_w[l])
        c_q, c_k, c_v = jnp.split(qkv, [gdn_qk, 2 * gdn_qk], axis=-1)
        c_q = l2_normalize(c_q.reshape(bsz, seq, GDN_HEADS, GDN_DK))
        c_k = l2_normalize(c_k.reshape(bsz, seq, GDN_HEADS, GDN_DK))
        c_v = c_v.reshape(bsz, seq, GDN_HEADS, GDN_DV)
        beta = jax.nn.sigmoid(g_b.astype(f32))
        log_decay = -jnp.exp(gdn_a_log[l].astype(f32)) * jax.nn.softplus(g_a.astype(f32) + gdn_dt_bias[l].astype(f32))
        o_a = gated_delta_rule(c_q, c_k, c_v, log_decay, beta)
        o_a = rms_norm(o_a, gdn_norm_g[l]) * jax.nn.silu(g_z.reshape(bsz, seq, GDN_HEADS, GDN_DV).astype(f32))
        y_a = o_a.reshape(bsz, seq, -1).astype(x.dtype) @ w_branch_a[l]

        o_b = nsa_attention(
            n_q.reshape(bsz, seq, NSA_HEADS, NSA_DK),
            n_kc.reshape(bsz, seq, NSA_GROUPS, NSA_DK), n_vc.reshape(bsz, seq, NSA_GROUPS, NSA_DV),
            n_ks.reshape(bsz, seq, NSA_GROUPS, NSA_DK), n_vs.reshape(bsz, seq, NSA_GROUPS, NSA_DV),
            n_kw.reshape(bsz, seq, NSA_GROUPS, NSA_DK), n_vw.reshape(bsz, seq, NSA_GROUPS, NSA_DV),
            n_gate.reshape(bsz, seq, NSA_HEADS, 3),
            cmp_pe_k[l], cmp_w1_k[l], cmp_w2_k[l], cmp_pe_v[l], cmp_w1_v[l], cmp_w2_v[l])
        y_b = o_b.reshape(bsz, seq, -1).astype(x.dtype) @ w_branch_b[l]

        mixed = jax.nn.sigmoid(m_a) * y_a + jax.nn.sigmoid(m_b) * y_b
        x = x + mixed @ w_mix_out[l]

        x = x + memory_cross_attention(rms_norm(x, xattn_norm_g[l]), rms_norm(mem, mem_norm_g[l]),
                                       xattn_w_q[l], xattn_w_kv[l], xattn_w_o[l])

        x = x + moe_ffn(rms_norm(x, ffn_norm_g[l]), router_w[l], router_b[l],
                        w_gate_up[l], b_gate_up[l], w_down[l], b_down[l])
    return rms_norm(x, final_norm_g)


_drawn_inputs = setup_inputs


def setup_inputs(seed=0):
    import zlib

    import numpy as np

    out = dict(_drawn_inputs(seed))
    spreads = {}
    factors = {'cmp_pe_k': 3.879, 'b_gate_up': 8.0, 'b_down': 8.0}
    for name, (base, spread) in spreads.items():
        noise = np.random.default_rng([zlib.crc32(name.encode()), seed]).standard_normal(out[name].shape)
        drawn = base * np.exp(spread * noise) if base else spread * noise
        out[name] = __import__('jax').numpy.asarray(drawn.astype(out[name].dtype))
    for name, factor in factors.items():
        out[name] = (out[name] * factor).astype(out[name].dtype)
    return out
```

```python
import math

import numpy as np
import concourse.bass as bass
from concourse import mybir
from contextlib import ExitStack

P = 128
D = 1024
KT = D // P
SEQ = 256
TT = SEQ // P
HEADS = 8
GROUPS = 2
REP = HEADS // GROUPS
DH = 128
CONV = 4
ROT = 32
CMP_LEN, CMP_STRIDE = 32, 16
NCMP = (SEQ - CMP_LEN) // CMP_STRIDE + 1
XH = 4
NE = 32
TOPK = 4
CAP = 64
EPS = 1e-6
NEG = -1e30
LIMIT, ALPHA = 7.0, 1.702
LEVELS = 7
SCALE = DH ** -0.5

C_B = 4 * D
C_NQ = C_B + 2 * HEADS
C_KC = C_NQ + D
KV = GROUPS * DH
C_VC, C_KS, C_VS, C_KW, C_VW = (C_KC + KV * i for i in range(1, 6))
C_NG = C_KC + 6 * KV
C_MA = C_NG + 3 * HEADS
C_MB = C_MA + D

K_ID, K_TRIU, K_STRICT, K_ONES, K_ZERO, K_CAUSAL, K_IOTA, K_LEVEL = (P * i for i in range(8))
K_CMPA = K_LEVEL + LEVELS * P
K_CMPM = K_CMPA + TT * NCMP
K_E = K_CMPM + TT * NCMP
K_SEL = K_E + NE
K_EPS = K_SEL + NE
NK = K_EPS + 1
R_ROT, R_COS, R_SIN = 0, ROT, ROT + SEQ
NR = ROT + 2 * SEQ

SLOT = 256
RING = 4


def constants():
    c = np.zeros((P, NK), np.float32)
    j, i = np.meshgrid(np.arange(P), np.arange(P), indexing="ij")
    c[:, K_ID:K_ID + P] = j == i
    c[:, K_TRIU:K_TRIU + P] = j <= i
    c[:, K_STRICT:K_STRICT + P] = j < i
    c[:, K_ONES:K_ONES + P] = 1
    c[:, K_CAUSAL:K_CAUSAL + P] = np.where(i <= j, 0, NEG)
    c[:, K_IOTA:K_IOTA + P] = i % CAP
    for n in range(LEVELS):
        s = 1 << n
        c[:, K_LEVEL + n * P:K_LEVEL + (n + 1) * P] = (j // (2 * s) == i // (2 * s)) & (j // s % 2 == 0) & (i // s % 2 == 1)
    for t in range(TT):
        q = t * P + np.arange(P)[:, None]
        ok = np.arange(NCMP)[None] * CMP_STRIDE + CMP_LEN - 1 <= q
        c[:, K_CMPA + t * NCMP:K_CMPA + (t + 1) * NCMP] = np.where(ok, 0, NEG)
        c[:, K_CMPM + t * NCMP:K_CMPM + (t + 1) * NCMP] = ok
    c[:, K_E:K_E + NE] = np.arange(NE)
    c[:, K_SEL:K_SEL + NE] = np.arange(P)[:, None] % NE == np.arange(NE)
    c[:, K_EPS] = EPS
    r = np.zeros((ROT, NR), np.float32)
    half = ROT // 2
    for m in range(half):
        r[m + half, R_ROT + m] = -1
        r[m, R_ROT + m + half] = 1
    freq = np.exp(np.float32(-math.log(500000.0)) * np.arange(half, dtype=np.float32) * np.float32(2.0 / ROT))
    ang = np.arange(SEQ, dtype=np.float32)[None] * freq[:, None].astype(np.float32)
    r[:, R_COS:R_COS + SEQ] = np.tile(np.cos(ang), (2, 1))
    r[:, R_SIN:R_SIN + SEQ] = np.tile(np.sin(ang), (2, 1))
    return c, r


def build(nc, a, dbg=None):
    f32, bf16, i32 = mybir.dt.float32, mybir.dt.bfloat16, mybir.dt.int32
    ALU, ACT, AX = mybir.AluOpType, mybir.ActivationFunctionType, mybir.AxisListType

    def cols(w, c0, k=KT, n=SLOT):
        return w[:, c0:c0 + n].rearrange("(k p) n -> p k n", p=P)

    w_in = a["w_in"]
    chunks = [cols(w_in, c) for c in range(0, 4 * D, SLOT)]
    chunks += [cols(w_in, C_NQ + c) for c in range(0, D, SLOT)]
    chunks += [cols(w_in, c) for c in (C_KC, C_VC, C_KS, C_KW)]
    chunks += [cols(w_in, C_MA + c) for c in range(0, D, SLOT)]
    N_LOOP = len(chunks)
    N_MB = len(chunks)
    chunks += [cols(w_in, C_MB + c) for c in range(0, D, SLOT)]
    N_VS = len(chunks)
    chunks += [cols(w_in, c) for c in (C_VS, C_VW)]
    N_XKV = len(chunks)
    chunks += [cols(a["xattn_w_kv"], c) for c in range(0, 2 * XH * DH, SLOT)]
    N_W1 = len(chunks)
    for w in (a["cmp_w1_k"], a["cmp_w1_v"]):
        v = w.rearrange("(l d) f -> d l f", d=DH)
        chunks += [v[:, l:l + CMP_LEN // 2, :] for l in (0, CMP_LEN // 2)]
    N_BA = len(chunks)
    chunks += [cols(a["w_branch_a"], c) for c in range(0, D, SLOT)]
    N_BB = len(chunks)
    chunks += [cols(a["w_branch_b"], c) for c in range(0, D, SLOT)]
    N_MIX = len(chunks)
    chunks += [cols(a["w_mix_out"], c) for c in range(0, D, SLOT)]
    N_XQ = len(chunks)
    chunks += [cols(a["xattn_w_q"], c) for c in range(0, XH * DH, SLOT)]
    N_XO = len(chunks)
    chunks += [cols(a["xattn_w_o"], c) for c in range(0, D, SLOT)]
    N_END = len(chunks)

    ctx = ExitStack()
    with ctx:
        def sb(name, shape, dt=f32):
            return ctx.enter_context(nc.sbuf_tensor(name, shape, dt))

        def sem(name):
            return ctx.enter_context(nc.semaphore(name))

        EXPERT = KT * 2 * D + KT * D
        early = sb("early", [P, EXPERT])
        at = {"early": 0, "mid": 0}

        def part(region, name, *dims, rows=P):
            n = int(np.prod(dims))
            o = at[name]
            at[name] = o + n
            v = region[0:rows, o:o + n]
            if len(dims) == 2:
                v = v.rearrange("p (a b) -> p a b", b=dims[1])
            elif len(dims) == 3:
                v = v.rearrange("p (a b c) -> p a b c", b=dims[1], c=dims[2])
            return v

        def E(*dims, rows=P):
            return part(early, "early", *dims, rows=rows)

        X = sb("X", [P, TT, D])
        hT = sb("hT", [P, KT, SEQ])
        C = sb("C", [P, NK])
        R = sb("R", [ROT, NR])
        ring = sb("ring", [P, RING, KT * SLOT])
        big = sb("big", [P, 32, SEQ])
        mb = sb("mb", [P, KT, SEQ])
        xkT = sb("xkT", [P, XH, SEQ])
        xv = sb("xv", [P, TT, XH * DH])
        colsA = sb("colsA", [P, P])
        colsB = sb("colsB", [P, 2 * CMP_LEN + 1])
        w_ba = sb("w_ba", [P, KT, 2 * HEADS])
        w_ng = sb("w_ng", [P, KT, 3 * HEADS])
        w_rt = sb("w_rt", [P, KT, NE])
        TK = sb("TK", [P, 4, TT, HEADS])
        gates = sb("gates", [P, TT, 3 * HEADS])
        stat = sb("stat", [P, 5, 3, TT])
        small = sb("small", [P, 96])

        STAGE = 2 * P + 2 * TT * D
        MT_END = STAGE + KT * SEQ
        CT_END = MT_END + 3 * HEADS * SEQ
        OA = EXPERT - HEADS * SEQ
        rowsA, rowsB, memx, Xn = E(P), E(P), E(TT, D), E(TT, D)
        mT = E(KT, SEQ)
        cT = E(3 * HEADS, SEQ)
        assert at["early"] == CT_END
        raw = E(2, 2, SEQ + CONV - 1)
        cy, csg = E(2, 2 * SEQ), E(2, 2 * SEQ)
        GB = E(2, SEQ, rows=HEADS)
        TP = E(4, SEQ, rows=HEADS)
        g1 = E(4, SEQ, rows=HEADS)
        abias = E(4, rows=HEADS)
        gates_end = at["early"]
        at["early"] = 0
        sqq, sqk, vst, lnq, lnk = (E(2 * SEQ) for _ in range(5))
        qn, kn = E(2, TT, P), E(2, TT, P)
        vb, qd = E(4, P), E(2, P)
        assert at["early"] <= STAGE
        at["early"] = CT_END
        dd, EDm, QKm, AT, LT, M1s, Tm, Um = (E(4, P) for _ in range(8))
        kd, eG, S1, vn = E(4, P), E(2, P), E(2, P), E(2, P)
        u, wT, sqo, lno = LT, M1s, dd, Tm
        at["early"] = max(at["early"], gates_end)
        GBrow = E(HEADS, 2 * SEQ, rows=1)
        assert at["early"] <= OA
        at["early"] = OA
        oaT = E(HEADS, SEQ)
        at["early"] = 0
        obT = E(HEADS, SEQ)
        qr = E(HEADS, SEQ)
        assert at["early"] <= STAGE
        at["early"] = MT_END
        vtok = E(2, TT, KV)
        blk = E(2, CMP_LEN, GROUPS * NCMP)
        S = [E(REP, SEQ) for _ in range(2)]
        PT = [E(TT, REP, SEQ) for _ in range(2)]
        PcT = E(HEADS, SEQ, rows=NCMP)
        w2 = E(2, DH)
        ccT = E(GROUPS * NCMP)
        vc = E(GROUPS, DH, rows=NCMP)
        s1, s1g = E(2, GROUPS * NCMP), E(2, GROUPS * NCMP)
        sc = E(TT, HEADS, NCMP)
        rt1, rt2 = E(2, SEQ, rows=ROT), E(2, SEQ, rows=ROT)
        zs = E(HEADS, SEQ)
        assert at["early"] <= OA

        yaT, mixT = big[:, 8:16, :], big[:, 16:24, :]

        def tiles(i, *dims):
            v = big[:, i:i + 8, :].rearrange("p a b -> p (a b)")
            return v.rearrange("p (a b) -> p a b", b=dims[-1]) if len(dims) == 2 else v.rearrange("p (a b c) -> p a b c", b=dims[1], c=dims[2])
        x2n = tiles(0, TT, D)
        S2 = [big[:, 8 + 4 * i:12 + 4 * i, :] for i in range(2)]
        PTx = tiles(16, TT, XH, SEQ)
        xqT, xoT = big[:, 24:28, :], big[:, 28:32, :]

        names = """c_in rope_in rows_in x_in mem_in wba_in ab_in w2_in rt_in gbrow_in bias_in fg_in out_out
        cols_tr cols_ok sq_n rinv_n xn_n tr_n hT_n
        ba_mm ba_sig sp_lin sp_exp gc_ok gc_exp tp_ok tp_tr tk_ok pads
        proj_done proj_taken conv_ok sig_ok mul_ok
        body_free sq_ok ss_mm rinv_g qk_ok pre_mm dd_ok ed_ok u0_ok t0_mm t0_ok lt_ok m1_mm m1_ok c_mm tu_ok
        u_mm u_ok w_ok s_mm s_ok ws_mm vn_ok o_mm sqo_ok so_mm lno_ok
        blk_ok w1_act w2_mm w2_ok qcopy rope_mm rope_ok
        sc_mm sc_read mx_ok ex_ok pn_ok tp_mm tp_taken cs_mm cs_max cs_exp cs_ok ct_mm ct_ok pv_mm pv_ok
        zsig z_ok mixed
        lg_mm lg_sub lg_exp lg_ok rk_mm pass_ok prep_ok
        pg_ok gat_mm xg_ok pgt_mm pgt_ok gu_taken act_g act_s h_ok ht_mm ht_ok y_ok scat acc_ok gu_used dn_used
        bsel_ok fin_acc fin_r fin_ok""".split()
        s = {n: sem(n) for n in names}
        ring_in = [sem(f"ring_in{i}") for i in range(RING)]
        gu_in = [sem(f"gu_in{k}") for k in range(KT)]
        dn_in = [sem(f"dn_in{k}") for k in range(KT)]
        psum = ctx.enter_context(nc.psum_tensor("psum", [P, 8 * 512], f32))
        PB = [psum[:, 512 * i:512 * (i + 1)] for i in range(8)]

        ident = C[:, K_ID:K_ID + P]
        ones = C[:, K_ONES:K_ONES + P]
        eps = C[:, K_EPS:K_EPS + 1]
        one = C[:, K_ONES:K_ONES + 1]

        def gain(n):
            return colsA[:, CONV * 24 + 8 * n:CONV * 24 + 8 * n + 8]

        def rw(slot):
            return ring[:, slot, :].rearrange("p (k n) -> p k n", k=KT)

        flat = big[:, :, :].rearrange("p a b -> p (a b)")

        def M(*dims, rows=P):
            return part(flat, "mid", *dims, rows=rows)
        x3n = M(TT, D)
        xg = M(KT, 2, CAP)
        Pg = M(TT, 2, CAP)
        PGd = M(2, TT, P)
        PGT = M(2, TT, P)
        gg, uu, sg, hh = M(512), M(512), M(512), M(512)
        hTt = M(4, P)
        ys = M(512)
        bselb = M(CAP)
        assert at["mid"] <= 32 * SEQ
        rflat = ring[:, :, :].rearrange("p a b -> p (a b)")
        B3 = 3 * NE
        btmp = rflat[0:B3, 0:3 * D]
        bmid = rflat[0:B3, 3 * D:3 * D + 3 * D // 2].bitcast(bf16)
        bspl = rflat[0:B3, 3 * D + 3 * D // 2:6 * D].bitcast(bf16)
        fgb = rflat[:, 6 * D:7 * D]
        bselv = bselb.bitcast(bf16)
        rb = small[0:1, 0:NE]
        mbf = mb[:, :, :].rearrange("p a b -> p (a b)")
        at["rt"] = 0

        def RT(*dims):
            return part(mbf, "rt", *dims)
        PASSES = SEQ // CAP
        NT = PASSES * NE + 2
        lg, lw, msk, oh, eqm, cand, gate = (RT(TT, NE) for _ in range(7))
        rankT, gateT = RT(NT, TT), RT(NT, TT)
        selT = RT(NT)
        mx, m1, rsum = (RT(TT) for _ in range(3))
        cmax = RT(1)
        npass = sb("npass", [1, 1], i32)

        wg = early[:, 0:KT * 2 * D].rearrange("p (k n) -> p k n", k=KT)
        wd = early[:, KT * 2 * D:EXPERT].rearrange("p (k n) -> p k n", k=KT)

        def sparse_step(i):
            g, br, t = i // 4, i // 2 % 2, i % 2
            return dict(q=lambda h: qr[:, g * REP + h, t * P:(t + 1) * P], k=lambda h: big[:, 20 + 2 * br + g, :],
                        n=t + 1, S=S[i % 2], PT=PT[br], t=t, gate=gates[:, t, :].rearrange("p (h b) -> p h b", b=3)[:, g * REP:(g + 1) * REP, 1 + br:2 + br])

        def memory_step(t):
            return dict(q=lambda h: xqT[:, h, t * P:(t + 1) * P], k=lambda h: xkT[:, h, :], n=TT, S=S2[t], PT=PTx, t=t, gate=None)
        steps = [sparse_step(i) for i in range(8)] + [memory_step(t) for t in range(TT)]
        smx, ssum = small[:, 64:72].rearrange("p (a b) -> p a b", a=2), small[:, 72:80].rearrange("p (a b) -> p a b", a=2)

        scope = dict(locals())
        block = ctx.enter_context(nc.Block())

        @block.sync
        def _(sp):
            sp.dma_start(X[:, :, :], a["x"].rearrange("o (t p) d -> p (o t) d", p=P)).then_inc(s["x_in"], 16)
            sp.dma_start(C[:, :], a["tab"]).then_inc(s["c_in"], 16)
            sp.dma_start(rowsA[0:CONV * 24, :], a["gdn_conv_w"].rearrange("t (c d) -> (t c) d", d=P)).then_inc(s["rows_in"], 16)
            for n, g in enumerate(("attn_norm_g", "xattn_norm_g", "mem_norm_g", "ffn_norm_g")):
                sp.dma_start(rowsA[CONV * 24 + 8 * n:CONV * 24 + 8 * n + 8, :], a[g].rearrange("o (c d) -> (o c) d", d=P)).then_inc(s["rows_in"], 16)
            sp.dma_start(rowsB[0:32, :], a["cmp_pe_k"]).then_inc(s["rows_in"], 16)
            sp.dma_start(rowsB[32:64, :], a["cmp_pe_v"]).then_inc(s["rows_in"], 16)
            sp.dma_start(rowsB[64:65, :], a["gdn_norm_g"]).then_inc(s["rows_in"], 16)
            sp.dma_start(w_ba[:, :, :], cols(w_in, C_B, n=2 * HEADS)).then_inc(s["wba_in"], 16)
            sp.dma_start(w_ng[:, :, :], cols(w_in, C_NG, n=3 * HEADS)).then_inc(s["wba_in"], 16)
            sp.dma_start(abias[:, 0:1], a["gdn_a_log"].rearrange("o h -> h o")).then_inc(s["ab_in"], 16)
            sp.dma_start(abias[:, 1:2], a["gdn_dt_bias"].rearrange("o h -> h o")).then_inc(s["ab_in"], 16)
            sp.dma_start(memx, a["mem"].rearrange("o (t p) d -> p (o t) d", p=P)).then_inc(s["mem_in"], 16)
            sp.dma_start(R[:, :], a["rope"]).then_inc(s["rope_in"], 16)
            for n, src in enumerate(chunks):
                if n >= RING:
                    sp.wait_ge(s["proj_done"], n - RING + 1)
                k = src.shape[1]
                dst = ring[:, n % RING, 0:k * src.shape[2]].rearrange("p (k n) -> p k n", k=k)
                sp.dma_start(dst, src).then_inc(ring_in[n % RING], 16)
                if n == N_LOOP:
                    sp.wait_ge(s["body_free"], 5)
                    sp.dma_start(w2[:, 0, :], a["cmp_w2_k"]).then_inc(s["w2_in"], 16)
                    sp.dma_start(w2[:, 1, :], a["cmp_w2_v"]).then_inc(s["w2_in"], 16)
                    sp.dma_start(w_rt[:, :, :], a["router_w"].rearrange("(k p) n -> p k n", p=P)).then_inc(s["rt_in"], 16)
                    sp.dma_start(rb, a["router_b"]).then_inc(s["rt_in"], 16)

            sp.wait_ge(s["pv_ok"], 4)
            sp.wait_ge(s["mixed"], 1)
            for k in range(KT):
                sp.dma_start(wg[:, k, :], a["w_gate_up"][0, k * P:(k + 1) * P, :]).then_inc(gu_in[k], 16)
            for k in range(KT):
                sp.dma_start(wd[:, k, :], a["w_down"][0, k * P:(k + 1) * P, :]).then_inc(dn_in[k], 16)
            sp.wait_ge(s["proj_done"], N_END)
            for i in range(3):
                sp.dma_start(btmp[i * NE:(i + 1) * NE, 0:2 * D], a["b_gate_up"]).then_inc(s["bias_in"], 16)
                sp.dma_start(btmp[i * NE:(i + 1) * NE, 2 * D:3 * D], a["b_down"]).then_inc(s["bias_in"], 16)
            sp.dma_start(fgb, a["final_norm_g"].rearrange("(o d) -> o d", o=1).to_broadcast([P, D])).then_inc(s["fg_in"], 16)

            def expert(n, e):
                for k in range(KT):
                    sp.wait_ge(s["gu_used"], n * KT + (k + 1 - KT))
                    sp.dma_start(wg[:, k, :], a["w_gate_up"][bass.ds(e, 1), k * P:(k + 1) * P, :].rearrange("o p n -> (o p) n")).then_inc(gu_in[k], 16)
                for k in range(KT):
                    sp.wait_ge(s["dn_used"], n * KT + (k + 1 - KT))
                    sp.dma_start(wd[:, k, :], a["w_down"][bass.ds(e, 1), k * P:(k + 1) * P, :].rearrange("o p n -> (o p) n")).then_inc(dn_in[k], 16)

            with sp.Fori(1, NE) as e:
                expert(e, e)
            sp.wait_ge(s["pass_ok"], 1)
            many = sp.value_load(npass[0:1, 0:1], min_val=0, max_val=SEQ)
            with sp.If(many > CAP):
                with sp.Fori(1, SEQ // CAP) as p:
                    with sp.Fori(0, NE) as e:
                        expert(p * NE + e, e)
            sp.wait_ge(s["fin_ok"], 1)
            sp.dma_start(a["out"].rearrange("o (t p) d -> p (o t) d", p=P), X[:, :, :]).then_inc(s["out_out"], 16)
            if dbg:
                for name, ap in dbg(scope):
                    sp.dma_start(a["dbg_" + name], ap).then_inc(s["out_out"], 16)
                sp.wait_ge(s["out_out"], 16 * (1 + len(dbg(scope))))
            else:
                sp.wait_ge(s["out_out"], 16)

        @block.tensor
        def _(pe):
            def mm(out, lhsT, rhs, start=True, stop=True):
                return pe.matmul(out, lhsT, rhs, start=start, stop=stop)

            def tr(out, in_):
                n = in_.shape[0]
                return pe.transpose(out, in_, C[0:n, K_ID:K_ID + n])

            def norm_T(n):
                src = x3n if n == 3 else Xn if n < 2 else x2n
                pe.wait_ge(s["xn_n"], n + 1)
                for b in range(4):
                    for k in range(2):
                        for t in range(TT):
                            last = tr(PB[2 + b][:, k * SEQ + t * P:k * SEQ + (t + 1) * P], src[:, t, (2 * b + k) * P:(2 * b + k + 1) * P])
                    last.then_inc(s["tr_n"], 1)

            pe.wait_ge(s["c_in"], 16)
            pe.wait_ge(s["rows_in"], 16 * 8)
            tr(PB[0][:, 0:P], rowsA)
            tr(PB[0][:, P:P + 65], rowsB[0:65, :]).then_inc(s["cols_tr"], 1)
            norm_T(0)
            pe.wait_ge(s["wba_in"], 32)
            pe.wait_ge(s["hT_n"], 4)
            for j in range(2):
                for k in range(KT):
                    mm(PB[6][0:HEADS, j * SEQ:(j + 1) * SEQ], w_ba[:, k, j * HEADS:(j + 1) * HEADS], hT[:, k, :], k == 0, k == KT - 1)
            for t in range(TT):
                for k in range(KT):
                    last = mm(PB[7][:, t * 24:t * 24 + 24], hT[:, k, t * P:(t + 1) * P], w_ng[:, k, :], k == 0, k == KT - 1)
            last.then_inc(s["ba_mm"], 1)

            def chunk(slot, nth, turn, src, tok=False, tiles=2, half=None, kt=KT):
                bank = PB[slot % 2]
                if half in (None, 0):
                    pe.wait_ge(ring_in[slot], nth)
                    pe.wait_ge(s["proj_taken"], turn)
                w = rw(slot) if kt == KT else ring[:, slot, 0:kt * SLOT].rearrange("p (k n) -> p k n", k=kt)
                for i in range(2):
                    if half is not None and i != half:
                        continue
                    for k in range(kt):
                        if tok:
                            last = mm(bank[:, i * SLOT:(i + 1) * SLOT], src[:, k, i * P:(i + 1) * P], w[:, k, :], k == 0, k == kt - 1)
                        else:
                            last = mm(bank[:, i * SEQ:(i + 1) * SEQ], w[:, k, i * P:(i + 1) * P], src[:, k, :], k == 0, k == kt - 1)
                if half in (None, 1):
                    last.then_inc(s["proj_done"], 1)

            def chunk_n(n, src, **kw):
                chunk(n % RING, 16 * (n // RING + 1), n + 1, src, **kw)

            with pe.Fori(0, 3) as it:
                for j in range(RING):
                    chunk(j, 16 * it + 16, 4 * it + (j + 1), hT)
            norm_T(1)
            pe.wait_ge(s["tp_ok"], 1)
            pe.wait_ge(s["hT_n"], 8)
            for q in range(4):
                for t in range(TT):
                    last = tr(PB[6][:, (q * TT + t) * HEADS:(q * TT + t + 1) * HEADS], TP[:, q, t * P:(t + 1) * P])
            last.then_inc(s["tp_tr"], 1)

            pe.wait_ge(s["gbrow_in"], 16 * HEADS)
            pe.wait_ge(s["tk_ok"], 1)
            with pe.Fori(0, HEADS // 2) as b:
                def fill(i):
                    j, half = divmod(i, 2)
                    chunk(j, 16 * b + 16 * 4, 4 * b + (13 + j), hT, half=half)

                pe.wait_ge(s["sq_ok"], b + 1)
                mm(PB[2][:, :], ones, sqq)
                mm(PB[3][:, :], ones, sqk).then_inc(s["ss_mm"], 1)
                fill(0)
                pe.wait_ge(s["qk_ok"], b + 1)
                for h in range(2):
                    mm(PB[4 + h][:, :], C[0:1, K_ONES:K_ONES + P], GBrow[0:1, bass.ds(2 * b + h, 1), :].rearrange("p a b -> p (a b)"))
                for h in range(2):
                    for t in range(TT):
                        m = slice((2 * h + t) * P, (2 * h + t + 1) * P)
                        mm(PB[6][:, m], kn[:, h, t, :], kn[:, h, t, :])
                        mm(PB[7][:, m], kn[:, h, t, :], qn[:, h, t, :])
                        tr(PB[2][:, m], kn[:, h, t, :])
                        last = tr(PB[3][:, m], vst[:, (2 * h + t) * P:(2 * h + t + 1) * P])
                last.then_inc(s["pre_mm"], 1)
                fill(1)
                pe.wait_ge(s["u0_ok"], b + 1)
                for m in range(4):
                    last = tr(PB[2][:, m * P:(m + 1) * P], Um[:, m, :])
                last.then_inc(s["t0_mm"], 1)
                pe.wait_ge(s["t0_ok"], b + 1)
                for lv in range(1, LEVELS):
                    pe.wait_ge(s["lt_ok"], 6 * b + lv)
                    if lv > 1:
                        pe.wait_ge(s["tu_ok"], 6 * b + (lv - 1))
                    for m in range(4):
                        last = mm(PB[2][:, m * P:(m + 1) * P], LT[:, m, :], Tm[:, m, :])
                    last.then_inc(s["m1_mm"], 1)
                    if 2 <= 1 + lv <= 7:
                        fill(1 + lv)
                    pe.wait_ge(s["m1_ok"], 6 * b + lv)
                    if lv < LEVELS - 1:
                        for m in range(4):
                            mm(PB[3][:, m * P:(m + 1) * P], Um[:, m, :], M1s[:, m, :])
                    for m in range(4):
                        last = mm(PB[4][:, m * P:(m + 1) * P], M1s[:, m, :], Um[:, m, :])
                    last.then_inc(s["c_mm"], 1)
                pe.wait_ge(s["tu_ok"], 6 * b + 6)
                for m in range(4):
                    mm(PB[2][:, m * P:(m + 1) * P], Um[:, m, :], vb[:, m, :])
                for h in range(2):
                    last = mm(PB[3][:, h * P:(h + 1) * P], kd[:, 2 * h + 1, :], Um[:, 2 * h + 1, :])
                last.then_inc(s["u_mm"], 1)
                pe.wait_ge(s["u_ok"], b + 1)
                for h in range(2):
                    last = mm(PB[4][:, h * P:(h + 1) * P], kd[:, 2 * h, :], u[:, 2 * h, :])
                last.then_inc(s["s_mm"], 1)
                pe.wait_ge(s["w_ok"], b + 1)
                pe.wait_ge(s["s_ok"], b + 1)
                for h in range(2):
                    last = mm(PB[5][:, h * P:(h + 1) * P], wT[:, h, :], S1[:, h, :])
                last.then_inc(s["ws_mm"], 1)
                pe.wait_ge(s["vn_ok"], b + 1)
                for h in range(2):
                    o = PB[6][:, h * SEQ:(h + 1) * SEQ]
                    mm(o[:, 0:P], u[:, 2 * h, :], QKm[:, 2 * h, :])
                    mm(o[:, P:SEQ], S1[:, h, :], qd[:, h, :], True, False)
                    last = mm(o[:, P:SEQ], vn[:, h, :], QKm[:, 2 * h + 1, :], False, True)
                last.then_inc(s["o_mm"], 1)
                pe.wait_ge(s["sqo_ok"], b + 1)
                mm(PB[7][:, :], ones, sqo.rearrange("p a b -> p (a b)")).then_inc(s["so_mm"], 1)

            for n in range(N_MB, N_VS):
                chunk_n(n, hT)
            for n in range(N_VS, N_XKV):
                chunk_n(n, hT, tok=True)
            for n in range(N_XKV, N_W1):
                chunk_n(n, mT, tok=n >= N_XKV + 2)

            for v in range(2):
                for l in range(CMP_LEN):
                    n = N_W1 + 2 * v + l // 16
                    if l % 16 == 0:
                        pe.wait_ge(ring_in[n % RING], 16 * (n // RING + 1))
                        if l == 0:
                            pe.wait_ge(s["proj_taken"], n + 1)
                            pe.wait_ge(s["blk_ok"], v + 1)
                    w = ring[:, n % RING, (l % 16) * P:(l % 16 + 1) * P]
                    last = mm(PB[v][:, 0:GROUPS * NCMP], w, blk[:, v, l, :], l == 0, l == CMP_LEN - 1)
                    if l % 16 == 15:
                        last.then_inc(s["proj_done"], 1)
            pe.wait_ge(s["w1_act"], 2)
            pe.wait_ge(s["w2_in"], 32)
            mm(PB[0][:, 0:GROUPS * NCMP], w2[:, 0, :], s1[:, 0, :])
            for g in range(GROUPS):
                last = mm(PB[0][0:NCMP, 64 + g * DH:64 + (g + 1) * DH], s1[:, 1, g * NCMP:(g + 1) * NCMP], w2[:, 1, :])
            last.then_inc(s["w2_mm"], 1)
            pe.wait_ge(s["rope_in"], 16)
            for r in range(6):
                if r >= 2:
                    pe.wait_ge(s["rope_ok"], r - 1)
                src = big[0:ROT, 8 + 2 * r:10 + 2 * r, :] if r < 4 else big[0:ROT, 20 + 2 * (r - 4):22 + 2 * (r - 4), :]
                mm(PB[2 + r % 2][0:ROT, :], R[:, R_ROT:R_ROT + ROT], src.rearrange("p a b -> p (a b)")).then_inc(s["rope_mm"], 1)
            pe.wait_ge(s["w2_ok"], 1)
            for t in range(TT):
                for h in range(HEADS):
                    g = h // REP
                    last = mm(PB[4][:, (t * HEADS + h) * 16:(t * HEADS + h) * 16 + NCMP], big[:, 8 + h, t * P:(t + 1) * P], ccT[:, g * NCMP:(g + 1) * NCMP])
            last.then_inc(s["cs_mm"], 1)
            pe.wait_ge(s["cs_ok"], 1)
            for r in range(4):
                if r >= 2:
                    pe.wait_ge(s["ct_ok"], r - 1)
                for i in range(2):
                    for t in range(TT):
                        last = tr(PB[6 + r % 2][0:NCMP, i * SEQ + t * P:i * SEQ + (t + 1) * P], sc[:, t, 2 * r + i, :])
                last.then_inc(s["ct_mm"], 1)
            pe.wait_ge(s["ct_ok"], 4)
            pe.wait_ge(s["rope_ok"], 6)

            def scores(i):
                st = steps[i]
                w = st["n"] * P
                if i >= 2:
                    pe.wait_ge(s["sc_read"], i - 1)
                for h in range(REP):
                    o = 2 * (i % 2) * 512 + h * w
                    last = mm(psum[:, 1024 + o:1024 + o + w], st["q"](h), st["k"](h)[:, 0:w])
                last.then_inc(s["sc_mm"], 1)

            def turned(i):
                st = steps[i]
                pe.wait_ge(s["pn_ok"], i + 1)
                if i:
                    pe.wait_ge(s["tp_taken"], i)
                for kt in range(st["n"]):
                    for h in range(REP):
                        last = tr(PB[6 + kt][:, h * P:(h + 1) * P], st["S"][:, h, kt * P:(kt + 1) * P])
                last.then_inc(s["tp_mm"], 1)

            scores(0)
            for g in range(GROUPS):
                for j in range(4):
                    i = 4 * g + j
                    if i < 7:
                        scores(i + 1)
                    turned(i)
                pe.wait_ge(s["tp_taken"], 4 * g + 4)
                if g:
                    pe.wait_ge(s["pv_ok"], 2)
                for h in range(REP):
                    o = PB[h // 2][:, (h % 2) * SEQ:(h % 2 + 1) * SEQ]
                    mm(o, vc[:, g, :], PcT[:, g * REP + h, :], True, False)
                    for br in range(2):
                        mm(o, vtok[:, br, 0, g * DH:(g + 1) * DH], PT[br][:, 0, h, :], False, False)
                        last = mm(o[:, P:SEQ], vtok[:, br, 1, g * DH:(g + 1) * DH], PT[br][:, 1, h, P:SEQ], False, br == 1)
                    if h % 2:
                        last.then_inc(s["pv_mm"], 1)

            pe.wait_ge(s["pv_ok"], 4)
            pe.wait_ge(s["z_ok"], 1)
            for n in range(N_BA, N_BB):
                chunk_n(n, oaT)
            for n in range(N_BB, N_MIX):
                chunk_n(n, obT)
            pe.wait_ge(s["mixed"], 1)
            for n in range(N_MIX, N_XQ):
                chunk_n(n, mixT, tok=True)
            norm_T(2)
            pe.wait_ge(s["hT_n"], 12)
            for n in range(N_XQ, N_XO):
                chunk_n(n, hT)
            pe.wait_ge(s["proj_taken"], N_XO + 2)
            scores(8)
            scores(9)
            turned(8)
            turned(9)
            pe.wait_ge(s["tp_taken"], 10)
            for h in range(XH):
                o = PB[h // 2][:, (h % 2) * SEQ:(h % 2 + 1) * SEQ]
                for kt in range(TT):
                    last = mm(o, xv[:, kt, h * DH:(h + 1) * DH], PTx[:, kt, h, :], kt == 0, kt == 1)
                if h % 2:
                    last.then_inc(s["pv_mm"], 1)
            pe.wait_ge(s["pv_ok"], 6)
            for n in range(N_XO, N_END):
                chunk_n(n, xoT, tok=True, kt=XH)

            norm_T(3)
            pe.wait_ge(s["hT_n"], 16)
            pe.wait_ge(s["rt_in"], 32)
            for t in range(TT):
                mm(PB[0][:, t * NE:(t + 1) * NE], C[0:1, K_ONES:K_ONES + P], rb, True, False)
                for k in range(KT):
                    last = mm(PB[0][:, t * NE:(t + 1) * NE], hT[:, k, t * P:(t + 1) * P], w_rt[:, k, :], False, k == KT - 1)
            last.then_inc(s["lg_mm"], 1)
            pe.wait_ge(s["lg_ok"], 1)
            mm(PB[1][:, 0:NE], C[:, K_STRICT:K_STRICT + P], msk[:, 0, :])
            mm(PB[1][:, NE:2 * NE], ones, msk[:, 0, :], True, False)
            mm(PB[1][:, NE:2 * NE], C[:, K_STRICT:K_STRICT + P], msk[:, 1, :], False, True)
            mm(PB[1][:, 2 * NE:3 * NE], ones, msk[:, 0, :], True, False)
            mm(PB[1][:, 2 * NE:3 * NE], ones, msk[:, 1, :], False, True).then_inc(s["rk_mm"], 1)

            def gather(t):
                pe.wait_ge(s["pg_ok"], t + 1)
                for k in range(KT):
                    for tt in range(TT):
                        last = mm(PB[4 + k // 4][:, (k % 4) * P:(k % 4 + 1) * P], x3n[:, tt, k * P:(k + 1) * P], Pg[:, tt, :, :].rearrange("p a b -> p (a b)"), tt == 0, tt == 1)
                last.then_inc(s["gat_mm"], 1)

            def gate_up(t, e):
                pe.wait_ge(s["gu_taken"], 2 * t + (e + 1))
                pe.wait_ge(s["bsel_ok"], t + 1)
                if e == 0:
                    pe.wait_ge(s["xg_ok"], t + 1)
                for c in range(4):
                    mm(PB[c // 2][64 * (c % 2):64 * (c % 2) + CAP, :], bselv[0:3 * NE, e * CAP:(e + 1) * CAP], bspl[:, c * 512:(c + 1) * 512], True, False)
                for k in range(KT):
                    pe.wait_ge(gu_in[k], 32 * t + 16 * (e + 1))
                    for c in range(4):
                        last = mm(PB[c // 2][64 * (c % 2):64 * (c % 2) + CAP, :], xg[:, k, e, :], wg[:, k, c * 512:(c + 1) * 512], False, k == KT - 1)
                    last.then_inc(s["gu_used"], 1)

            def down(t, e):
                pe.wait_ge(s["h_ok"], 2 * t + (e + 1))
                for c in range(4):
                    last = tr(PB[2][:, c * P:(c + 1) * P], hh[:, c * P:(c + 1) * P])
                last.then_inc(s["ht_mm"], 1)
                pe.wait_ge(s["ht_ok"], 2 * t + (e + 1))
                for c in range(2):
                    mm(PB[3][64 * c:64 * c + CAP, :], bselv[0:3 * NE, e * CAP:(e + 1) * CAP], bspl[:, 2 * D + c * 512:2 * D + (c + 1) * 512], True, False)
                for k in range(KT):
                    pe.wait_ge(dn_in[k], 32 * t + 16 * (e + 1))
                    for c in range(2):
                        last = mm(PB[3][64 * c:64 * c + CAP, :], hTt[:, k % 4, (k // 4) * CAP:(k // 4 + 1) * CAP], wd[:, k, c * 512:(c + 1) * 512], False, k == KT - 1)
                    last.then_inc(s["dn_used"], 1)

            def scatter(t, e):
                pe.wait_ge(s["y_ok"], 2 * t + (e + 1))
                pe.wait_ge(s["pgt_ok"], t + 1)
                pe.wait_ge(s["acc_ok"], 2 * t + (e + 1))
                if e == 1:
                    pe.wait_ge(s["xg_ok"], t + 2)
                for tt in range(TT):
                    for c in range(2):
                        last = mm(PB[4 + 2 * tt + c][:, :], PGT[64 * c:64 * c + CAP, e, tt, :], ys[64 * c:64 * c + CAP, :])
                last.then_inc(s["scat"], 1)

            def experts(t):
                pe.wait_ge(s["pg_ok"], t + 1)
                for e in range(2):
                    for tt in range(TT):
                        last = tr(PB[2][:, (2 * e + tt) * P:(2 * e + tt + 1) * P], PGd[:, e, tt, :])
                last.then_inc(s["pgt_mm"], 1)
                gate_up(t, 0)
                pe.wait_ge(s["pgt_ok"], t + 1)
                down(t, 0)
                scatter(t, 0)
                gate_up(t, 1)
                pe.wait_ge(s["acc_ok"], 2 * t + 2)
                gather(t + 1)
                down(t, 1)
                scatter(t, 1)

            pe.wait_ge(s["prep_ok"], 1)
            gather(0)
            with pe.Fori(0, NE // 2) as t:
                experts(t)
            many = pe.value_load(npass[0:1, 0:1], min_val=0, max_val=SEQ)
            with pe.If(many > CAP):
                with pe.Fori(NE // 2, SEQ // CAP * (NE // 2)) as t:
                    experts(t)


        @block.scalar
        def _(act):
            def fn(out, in_, f=ACT.Copy, **kw):
                return act.activation(out, in_, f, **kw)

            def norm(n, src, junk):
                for t in range(TT):
                    fn(junk[:, t, :], src[:, t, :], ACT.Square, accum_out=stat[:, n, 0, t:t + 1])
                act.drain()
                fn(stat[:, n, 1, :], stat[:, n, 0, :], ACT.Ln, scale=1.0 / D, bias=eps)
                act.drain()
                fn(stat[:, n, 2, :], stat[:, n, 1, :], ACT.Exp, scale=-0.5).then_inc(s["rinv_n"], 1)

            act.wait_ge(s["x_in"], 16)
            act.wait_ge(s["c_in"], 16)
            norm(0, X, Xn)

            act.wait_ge(s["ba_mm"], 1)
            fn(GB[:, 1, :], PB[6][0:HEADS, 0:SEQ], ACT.Sigmoid)
            fn(gates[:, :, :], PB[7][:, 0:TT * 3 * HEADS].rearrange("p (t n) -> p t n", t=TT), ACT.Sigmoid).then_inc(s["ba_sig"], 1)
            act.wait_ge(s["sp_lin"], 1)
            fn(g1[:, 2, :], g1[:, 1, :], ACT.Exp, scale=-1.0)
            fn(abias[:, 2:3], abias[:, 0:1], ACT.Exp)
            act.drain()
            fn(g1[:, 3, :], g1[:, 2, :], ACT.Ln, bias=one[0:HEADS, :]).then_inc(s["sp_exp"], 1)
            act.wait_ge(s["gc_ok"], 1)
            fn(TP[:, 2, :], g1[:, 0, :], ACT.Exp)
            fn(g1[:, 2, :], GB[:, 0, :], ACT.Exp).then_inc(s["gc_exp"], 1)
            for h in range(HEADS):
                act.dma_start(GBrow[:, h, :], GB[h:h + 1, :, :].rearrange("p a b -> p (a b)")).then_inc(s["gbrow_in"], 16)

            act.sem_inc(s["proj_taken"], 2)
            act.wait_ge(s["pads"], 1)
            with act.Fori(0, 3) as it:
                for j in range(RING):
                    act.wait_ge(s["proj_done"], 4 * it + (j + 1))
                    act.wait_ge(s["conv_ok"], 4 * it + (j + 1))
                    fn(raw[:, j % 2, :, CONV - 1:], PB[j % 2].rearrange("p (a b) -> p a b", b=SEQ)).then_inc(s["proj_taken"], 1)
                    act.wait_ge(s["conv_ok"], 4 * it + (j + 3))
                    fn(csg[:, j % 2, :], cy[:, j % 2, :], ACT.Sigmoid).then_inc(s["sig_ok"], 1)
            act.wait_ge(s["mem_in"], 16)
            act.wait_ge(s["tr_n"], 4)
            norm(1, memx, Xn)

            with act.Fori(0, HEADS // 2) as b:
                def out(j):
                    act.wait_ge(s["proj_done"], 4 * b + (13 + j))
                    fn(big[:, bass.ds(8 * b + 2 * j, 2), :].rearrange("p a b -> p (a b)"), PB[j % 2]).then_inc(s["proj_taken"], 1)

                act.wait_ge(s["ss_mm"], b + 1)
                fn(lnq, PB[2], ACT.Ln, bias=eps)
                fn(lnk, PB[3], ACT.Ln, bias=eps)
                act.drain()
                fn(lnq, lnq, ACT.Exp, scale=-0.5)
                fn(lnk, lnk, ACT.Exp, scale=-0.5).then_inc(s["rinv_g"], 1)
                act.wait_ge(s["dd_ok"], b + 1)
                fn(EDm.rearrange("p a b -> p (a b)"), dd.rearrange("p a b -> p (a b)"), ACT.Exp)
                for h in range(2):
                    last = fn(eG[:, h, :], PB[4 + h][:, P:SEQ], ACT.Exp)
                last.then_inc(s["ed_ok"], 1)
                out(0)
                act.wait_ge(s["t0_mm"], b + 1)
                fn(Tm.rearrange("p a b -> p (a b)"), PB[2]).then_inc(s["t0_ok"], 1)
                for lv in range(1, LEVELS):
                    act.wait_ge(s["m1_mm"], 6 * b + lv)
                    fn(M1s.rearrange("p a b -> p (a b)"), PB[2]).then_inc(s["m1_ok"], 1)
                    if lv % 2 == 0:
                        out(lv // 2)
                act.wait_ge(s["u_mm"], b + 1)
                fn(u.rearrange("p a b -> p (a b)"), PB[2]).then_inc(s["u_ok"], 1)
                act.wait_ge(s["s_mm"], b + 1)
                fn(S1.rearrange("p a b -> p (a b)"), PB[4][:, 0:SEQ]).then_inc(s["s_ok"], 1)
                act.wait_ge(s["o_mm"], b + 1)
                fn(sqo.rearrange("p a b -> p (a b)"), PB[6], ACT.Square).then_inc(s["sqo_ok"], 1)
                act.wait_ge(s["so_mm"], b + 1)
                fn(lno.rearrange("p a b -> p (a b)"), PB[7], ACT.Ln, scale=1.0 / DH, bias=eps)
                act.drain()
                fn(lno, lno, ACT.Exp, scale=-0.5).then_inc(s["lno_ok"], 1)

            for n in range(N_MB, N_VS):
                act.wait_ge(s["proj_done"], n + 1)
                i = 2 * (n - N_MB)
                fn(mb[:, i:i + 2, :].rearrange("p a b -> p (a b)"), PB[n % 2], ACT.Sigmoid).then_inc(s["proj_taken"], 1)
            fn(big[:, 24:32, :], big[:, 24:32, :], ACT.Sigmoid)
            fn(zs, big[:, 0:8, :], ACT.Sigmoid).then_inc(s["zsig"], 1)
            for n in range(N_VS, N_XKV):
                act.wait_ge(s["proj_done"], n + 1)
                fn(vtok[:, n - N_VS, :, :].rearrange("p a b -> p (a b)"), PB[n % 2]).then_inc(s["proj_taken"], 1)
            for n in range(N_XKV, N_W1):
                act.wait_ge(s["proj_done"], n + 1)
                i = n - N_XKV
                if i < 2:
                    fn(xkT[:, 2 * i:2 * i + 2, :].rearrange("p a b -> p (a b)"), PB[n % 2]).then_inc(s["proj_taken"], 1)
                else:
                    fn(xv[:, :, (i - 2) * SLOT:(i - 1) * SLOT], PB[n % 2].rearrange("p (a b) -> p a b", b=SLOT)).then_inc(s["proj_taken"], 1)
            for v in range(2):
                act.wait_ge(s["proj_done"], N_W1 + 2 * v + 2)
                fn(s1g[:, v, :], PB[v][:, 0:GROUPS * NCMP], ACT.Sigmoid).then_inc(s["proj_taken"], 2)
            act.wait_ge(s["w2_mm"], 1)
            fn(ccT, PB[0][:, 0:GROUPS * NCMP])
            fn(vc, PB[0][0:NCMP, 64:64 + KV].rearrange("p (a b) -> p a b", b=DH)).then_inc(s["w2_ok"], 1)
            act.wait_ge(s["cs_max"], 1)
            fn(sc, sc, ACT.Exp).then_inc(s["cs_exp"], 1)
            for r in range(4):
                act.wait_ge(s["ct_mm"], r + 1)
                fn(PcT[:, 2 * r:2 * r + 2, :].rearrange("p a b -> p (a b)"), PB[6 + r % 2][0:NCMP, :]).then_inc(s["ct_ok"], 1)

            def exps(i):
                st = steps[i]
                act.wait_ge(s["mx_ok"], i + 1)
                w = st["n"] * P
                for h in range(REP):
                    last = fn(st["S"][:, h, 0:w], st["S"][:, h, 0:w], ACT.Exp, bias=smx[:, i % 2, h:h + 1], accum_out=ssum[:, i % 2, h:h + 1])
                last.then_inc(s["ex_ok"], 1)

            def turned(i):
                st = steps[i]
                act.wait_ge(s["tp_mm"], i + 1)
                for kt in range(st["n"]):
                    last = fn(st["PT"][:, kt, :, st["t"] * P:(st["t"] + 1) * P], PB[6 + kt].rearrange("p (a b) -> p a b", b=P))
                last.then_inc(s["tp_taken"], 1)

            exps(0)
            for g in range(GROUPS):
                for j in range(4):
                    i = 4 * g + j
                    if i < 7:
                        exps(i + 1)
                    turned(i)
                for h in range(0, REP, 2):
                    act.wait_ge(s["pv_mm"], 2 * g + h // 2 + 1)
                    fn(obT[:, g * REP + h:g * REP + h + 2, :].rearrange("p a b -> p (a b)"), PB[h // 2]).then_inc(s["pv_ok"], 1)
            for n in range(N_BA, N_MIX):
                act.wait_ge(s["proj_done"], n + 1)
                i = 2 * ((n - N_BA) % 4)
                dst = yaT if n < N_BB else mixT
                fn(dst[:, i:i + 2, :].rearrange("p a b -> p (a b)"), PB[n % 2]).then_inc(s["proj_taken"], 1)
            act.wait_ge(s["proj_taken"], N_XQ + 2)
            norm(2, X, x2n)
            for n in range(N_XQ, N_XO):
                act.wait_ge(s["proj_done"], n + 1)
                i = 2 * (n - N_XQ)
                fn(xqT[:, i:i + 2, :].rearrange("p a b -> p (a b)"), PB[n % 2]).then_inc(s["proj_taken"], 1)
            exps(8)
            exps(9)
            turned(8)
            turned(9)
            for h in range(0, XH, 2):
                act.wait_ge(s["pv_mm"], 5 + h // 2)
                fn(xoT[:, h:h + 2, :].rearrange("p a b -> p (a b)"), PB[h // 2]).then_inc(s["pv_ok"], 1)
            act.wait_ge(s["proj_taken"], N_END + 2)
            norm(3, X, x3n)
            act.wait_ge(s["lg_sub"], 1)
            fn(gate, lw, ACT.Exp).then_inc(s["lg_exp"], 1)

            def experts(t):
                act.wait_ge(s["pgt_mm"], t + 1)
                fn(PGT.rearrange("p a b c -> p (a b c)"), PB[2]).then_inc(s["pgt_ok"], 1)
                for e in range(2):
                    act.wait_ge(s["act_g"], 2 * t + (e + 1))
                    fn(sg, gg, ACT.Sigmoid, scale=ALPHA).then_inc(s["act_s"], 1)
                    act.wait_ge(s["ht_mm"], 2 * t + (e + 1))
                    fn(hTt.rearrange("p a b -> p (a b)"), PB[2]).then_inc(s["ht_ok"], 1)
                    act.wait_ge(s["dn_used"], 16 * t + 8 * (e + 1))
                    fn(ys, PB[3]).then_inc(s["y_ok"], 1)

            with act.Fori(0, NE // 2) as t:
                experts(t)
            act.wait_ge(s["pass_ok"], 1)
            many = act.value_load(npass[0:1, 0:1], min_val=0, max_val=SEQ)
            with act.If(many > CAP):
                with act.Fori(NE // 2, PASSES * (NE // 2)) as t:
                    experts(t)
            act.wait_ge(s["fin_acc"], 1)
            norm(4, X, hT[:, :, :].rearrange("p (t k) n -> p t (k n)", t=TT))

        @block.vector
        def _(dve):
            dr = dve.drain

            def tt(out, a0, a1, op):
                return dve.tensor_tensor(out, a0, a1, op)

            def ts(out, a0, s1, op, s2=None, op2=None):
                return dve.tensor_scalar(out, a0, s1, s2, op) if op2 is None else dve.tensor_scalar(out, a0, s1, s2, op, op2)

            def stt(out, a0, sc_, a1, op, op2):
                return dve.scalar_tensor_tensor(out, a0, sc_, a1, op, op2)

            def bc(v, n):
                return v.unsqueeze(len(v.shape)).to_broadcast([*v.shape, n])

            def mid(v, n):
                return v.unsqueeze(1).to_broadcast([v.shape[0], n, *v.shape[1:]])

            def flat2(v):
                return v.rearrange("p a b -> p (a b)")

            def scale_rows(n, src, dst):
                dve.wait_ge(s["rinv_n"], n + 1)
                for t in range(TT):
                    last = ts(dst[:, t, :], src[:, t, :], stat[:, n, 2, t:t + 1], ALU.mult)
                last.then_inc(s["xn_n"], 1)

            def norm_out(n, dst):
                for b in range(4):
                    dve.wait_ge(s["tr_n"], 4 * n + b + 1)
                    gcol = {0: gain(0), 1: gain(2), 2: gain(1), 3: gain(3)}[n]
                    tt(dst[:, 2 * b:2 * b + 2, :], PB[2 + b].rearrange("p (a b) -> p a b", b=SEQ), bc(gcol[:, 2 * b:2 * b + 2], SEQ), ALU.mult).then_inc(s["hT_n"], 1)

            dve.wait_ge(s["cols_tr"], 1)
            dve.tensor_copy(colsA[:, :], PB[0][:, 0:P])
            dve.tensor_copy(colsB[:, :], PB[0][:, P:P + 65])
            scale_rows(0, X, Xn)
            norm_out(0, hT)

            dve.wait_ge(s["ba_sig"], 1)
            dve.wait_ge(s["ab_in"], 32)
            ts(g1[:, 0, :], PB[6][0:HEADS, SEQ:2 * SEQ], abias[:, 1:2], ALU.add)
            dr()
            stt(g1[:, 1, :], g1[:, 0, :], -1.0, g1[:, 0, :], ALU.mult, ALU.max).then_inc(s["sp_lin"], 1)
            dve.wait_ge(s["sp_exp"], 1)
            stt(g1[:, 2, :], g1[:, 0, :], 0.0, g1[:, 3, :], ALU.max, ALU.add)
            dr()
            ts(g1[:, 1, :], g1[:, 2, :], abias[:, 2:3], ALU.mult, -1.0, ALU.mult)
            dr()
            for t in range(TT):
                q = slice(t * P, (t + 1) * P)
                dve.tensor_tensor_scan(GB[:, 0, q], C[0:HEADS, K_ONES:K_ONES + P], g1[:, 1, q], 0.0, ALU.mult, ALU.add)
            dr()
            for t in range(TT):
                q = slice(t * P, (t + 1) * P)
                ts(g1[:, 0, q], GB[:, 0, q], GB[:, 0, (t + 1) * P - 1:(t + 1) * P], ALU.subtract, -1.0, ALU.mult)
            dve.tensor_copy(TP[:, 0, :], GB[:, 1, :])
            dve.tensor_copy(TP[:, 1, :], GB[:, 0, :]).then_inc(s["gc_ok"], 1)
            dve.wait_ge(s["gc_exp"], 1)
            tt(TP[:, 3, :], g1[:, 2, :], GB[:, 1, :], ALU.mult).then_inc(s["tp_ok"], 1)

            dve.sem_inc(s["conv_ok"], 2)
            with dve.Fori(0, 3) as it:
                for j in range(RING):
                    dve.wait_ge(s["proj_taken"], 4 * it + (j + 3))
                    dve.wait_ge(s["mul_ok"], 4 * it + (j + 1))
                    for tap in range(CONV):
                        for i in range(2):
                            y = cy[:, j % 2, i * SEQ:(i + 1) * SEQ]
                            x = raw[:, j % 2, i, tap:tap + SEQ]
                            w = colsA[:, bass.ds(8 * it + (tap * 24 + 2 * j + i), 1)]
                            last = ts(y, x, w, ALU.mult) if tap == 0 else stt(y, x, w, y, ALU.mult, ALU.add)
                        if tap < CONV - 1:
                            dr()
                    last.then_inc(s["conv_ok"], 1)
            dve.wait_ge(s["mem_in"], 16)
            scale_rows(1, memx, Xn)
            norm_out(1, mT)
            dve.wait_ge(s["tp_tr"], 1)
            dve.tensor_copy(TK[:, :, :, :].rearrange("p a b c -> p (a b c)"), PB[6][:, 0:4 * TT * HEADS]).then_inc(s["tk_ok"], 1)
            dr().then_inc(s["body_free"], 1)

            with dve.Fori(0, HEADS // 2) as b:
                dve.wait_ge(s["rinv_g"], b + 1)
                stt(qn.rearrange("p a b c -> p (a b c)"), flat2(cT[:, bass.ds(2 * b, 2), :]), SCALE, lnq, ALU.mult, ALU.mult)
                tt(kn.rearrange("p a b c -> p (a b c)"), flat2(cT[:, bass.ds(2 * b + HEADS, 2), :]), lnk, ALU.mult).then_inc(s["qk_ok"], 1)
                dve.wait_ge(s["pre_mm"], b + 1)

                def tk(q, t, h):
                    return TK[:, q, t, bass.ds(2 * b + h, 1)]
                for h in range(2):
                    for t in range(TT):
                        last = ts(dd[:, 2 * h + t, :], PB[4 + h][:, t * P:(t + 1) * P], tk(1, t, h), ALU.subtract, 0.0, ALU.min)
                last.then_inc(s["dd_ok"], 1)
                for h in range(2):
                    for t in range(TT):
                        m = 2 * h + t
                        ts(kd[:, m, :], PB[2][:, m * P:(m + 1) * P], tk(2 + t, t, h), ALU.mult)
                        ts(vb[:, m, :], PB[3][:, m * P:(m + 1) * P], tk(0, t, h), ALU.mult)
                dve.wait_ge(s["ed_ok"], b + 1)
                tt(EDm, EDm, mid(C[:, K_TRIU:K_TRIU + P], 4), ALU.mult)
                tt(qd, qn[:, :, 1, :], eG, ALU.mult)
                dr()
                tt(flat2(QKm), flat2(EDm), PB[7], ALU.mult)
                tt(flat2(AT), flat2(EDm), PB[6], ALU.mult)
                dr()
                for h in range(2):
                    v = AT[:, 2 * h:2 * h + 2, :]
                    tt(flat2(v), flat2(v), PB[4 + h][:, SEQ:2 * SEQ], ALU.mult)
                dr()
                tt(dd, AT, mid(C[:, K_LEVEL:K_LEVEL + P], 4), ALU.mult)
                dr()
                tt(Um, mid(ident, 4), dd, ALU.subtract).then_inc(s["u0_ok"], 1)
                for lv in range(1, LEVELS):
                    dve.wait_ge(s["c_mm"], 6 * b + lv)
                    if lv < LEVELS - 1:
                        tt(flat2(Tm), flat2(Tm), PB[3], ALU.subtract)
                    tt(flat2(Um), flat2(Um), PB[4], ALU.subtract).then_inc(s["tu_ok"], 1)
                dve.wait_ge(s["u_mm"], b + 1)
                dve.tensor_copy(flat2(wT)[:, 0:SEQ], PB[3][:, 0:SEQ]).then_inc(s["w_ok"], 1)
                dve.wait_ge(s["ws_mm"], b + 1)
                tt(vn, u[:, 1:4:2, :], PB[5][:, 0:SEQ].rearrange("p (a b) -> p a b", b=P), ALU.subtract).then_inc(s["vn_ok"], 1)
                dve.wait_ge(s["lno_ok"], b + 1)
                tt(flat2(oaT[:, bass.ds(2 * b, 2), :]), flat2(lno), PB[6], ALU.mult)
                dr().then_inc(s["body_free"], 1)

            dve.wait_ge(s["proj_taken"], N_LOOP + 2)
            for v in range(2):
                for g in range(GROUPS):
                    win = big[:, 16 + 2 * v + g, :].rearrange("p (m b) -> p b m", b=CMP_STRIDE)
                    for half in range(2):
                        l = slice(half * CMP_STRIDE, (half + 1) * CMP_STRIDE)
                        pe_cols = colsB[:, CMP_LEN * v + half * CMP_STRIDE:CMP_LEN * v + (half + 1) * CMP_STRIDE]
                        last = tt(blk[:, v, l, g * NCMP:(g + 1) * NCMP], win[:, :, half:half + NCMP], bc(pe_cols, NCMP), ALU.add)
                last.then_inc(s["blk_ok"], 1)
            dve.wait_ge(s["zsig"], 1)
            tt(zs, zs, big[:, 0:8, :], ALU.mult)
            dr()
            stt(flat2(oaT), flat2(oaT), colsB[:, 2 * CMP_LEN:2 * CMP_LEN + 1], flat2(zs), ALU.mult, ALU.mult).then_inc(s["z_ok"], 1)
            for v in range(2):
                dve.wait_ge(s["proj_taken"], N_W1 + 2 * v + 4)
                tt(s1[:, v, :], s1g[:, v, :], PB[v][:, 0:GROUPS * NCMP], ALU.mult).then_inc(s["w1_act"], 1)
            dve.wait_ge(s["qcopy"], 1)
            dve.wait_ge(s["rope_in"], 16)
            cos, sin = R[:, R_COS:R_COS + SEQ], R[:, R_SIN:R_SIN + SEQ]
            for r in range(6):
                i = 8 + 2 * r if r < 4 else 20 + 2 * (r - 4)
                src = big[0:ROT, i:i + 2, :]
                dst = qr[0:ROT, 2 * r:2 * r + 2, :] if r < 4 else src
                dve.wait_ge(s["rope_mm"], r + 1)
                tt(rt1, src, mid(cos, 2), ALU.mult)
                tt(rt2, PB[2 + r % 2][0:ROT, :].rearrange("p (a b) -> p a b", b=SEQ), mid(sin, 2), ALU.mult)
                dr()
                tt(dst, rt1, rt2, ALU.add).then_inc(s["rope_ok"], 1)
                dr()
            dve.wait_ge(s["cs_mm"], 1)
            cps = PB[4][:, 0:TT * HEADS * 16].rearrange("p (t h n) -> p t h n", t=TT, n=16)
            for t in range(TT):
                stt(sc[:, t, :, :], cps[:, t, :, 0:NCMP], SCALE, mid(C[:, K_CMPA + t * NCMP:K_CMPA + (t + 1) * NCMP], HEADS), ALU.mult, ALU.add)
            dr()
            sc2 = sc.rearrange("p t h n -> p (t h) n")
            r1, r2 = small[:, 32:48], small[:, 48:64]
            dve.tensor_reduce(r1, sc2, AX.X, ALU.max)
            dr()
            tt(sc2, sc2, bc(r1, NCMP), ALU.subtract).then_inc(s["cs_max"], 1)
            dve.wait_ge(s["cs_exp"], 1)
            for t in range(TT):
                tt(sc[:, t, :, :], sc[:, t, :, :], mid(C[:, K_CMPM + t * NCMP:K_CMPM + (t + 1) * NCMP], HEADS), ALU.mult)
            dr()
            dve.tensor_reduce(r2, sc2, AX.X, ALU.add)
            dr()
            ts(r2, r2, 1e-30, ALU.max)
            dr()
            dve.reciprocal(r2, r2)
            dr()
            g3 = gates[:, :, :].rearrange("p t (h b) -> p t h b", b=3)
            tt(r2.rearrange("p (t h) -> p t h", t=TT), r2.rearrange("p (t h) -> p t h", t=TT), g3[:, :, :, 0], ALU.mult)
            dr()
            tt(sc2, sc2, bc(r2, NCMP), ALU.mult).then_inc(s["cs_ok"], 1)

            def maxima(i):
                st = steps[i]
                n, w = st["n"], st["n"] * P
                dve.wait_ge(s["sc_mm"], i + 1)
                if i >= 2:
                    dve.wait_ge(s["tp_mm"], i - 1)
                o = 1024 + 2 * (i % 2) * 512
                src = psum[:, o:o + REP * w].rearrange("p (a b) -> p a b", b=w)
                dst = st["S"][:, :, 0:w]
                if i < 8:
                    m = C[:, K_CAUSAL - (n - 1) * P:K_CAUSAL + P]
                    stt(dst, src, SCALE, mid(m, REP), ALU.mult, ALU.add).then_inc(s["sc_read"], 1)
                else:
                    ts(dst, src, SCALE, ALU.mult).then_inc(s["sc_read"], 1)
                dr()
                dve.tensor_reduce(smx[:, i % 2, :], dst, AX.X, ALU.max)
                dr()
                ts(smx[:, i % 2, :], smx[:, i % 2, :], -1.0, ALU.mult).then_inc(s["mx_ok"], 1)

            def weights(i):
                st = steps[i]
                dst = st["S"][:, :, 0:st["n"] * P]
                r = ssum[:, i % 2, :]
                dve.wait_ge(s["ex_ok"], i + 1)
                dve.reciprocal(r, r)
                dr()
                if st["gate"] is not None:
                    tt(r, r, st["gate"][:, :, 0], ALU.mult)
                    dr()
                tt(dst, dst, bc(r, st["n"] * P), ALU.mult).then_inc(s["pn_ok"], 1)

            maxima(0)
            for i in range(8):
                if i < 7:
                    maxima(i + 1)
                weights(i)
            dve.wait_ge(s["proj_taken"], N_MIX + 2)
            tt(yaT, yaT, big[:, 24:32, :], ALU.mult)
            tt(mixT, mixT, mb[:, :, :], ALU.mult)
            dr()
            tt(mixT, mixT, yaT, ALU.add).then_inc(s["mixed"], 1)

            def residual(n0, n1):
                for n in range(n0, n1):
                    dve.wait_ge(s["proj_done"], n + 1)
                    v = X[:, :, (n - n0) * SLOT:(n - n0 + 1) * SLOT]
                    tt(v, v, PB[n % 2].rearrange("p (a b) -> p a b", b=SLOT), ALU.add).then_inc(s["proj_taken"], 1)

            residual(N_MIX, N_XQ)
            scale_rows(2, X, x2n)
            norm_out(2, hT)
            maxima(8)
            maxima(9)
            weights(8)
            weights(9)
            residual(N_XO, N_END)
            scale_rows(3, X, x3n)
            norm_out(3, hT)

            dve.wait_ge(s["lg_mm"], 1)
            lps = PB[0][:, 0:TT * NE].rearrange("p (a b) -> p a b", b=NE)
            dve.tensor_copy(lg, lps)
            dve.tensor_copy(lw, lps)
            dve.memset(msk, 0.0)
            dr()
            for r in range(TOPK):
                dve.tensor_reduce(mx, lw, AX.X, ALU.max)
                dr()
                if r == 0:
                    dve.tensor_copy(m1, mx)
                tt(eqm, lw, bc(mx, NE), ALU.is_equal)
                dr()
                stt(cand, eqm, -1024.0, mid(C[:, K_E:K_E + NE], TT), ALU.mult, ALU.add)
                dr()
                dve.tensor_reduce(rsum, cand, AX.X, ALU.min)
                dr()
                tt(oh, cand, bc(rsum, NE), ALU.is_equal)
                dr()
                tt(msk, msk, oh, ALU.add)
                stt(lw, oh, -3e38, lw, ALU.mult, ALU.add)
                dr()
            tt(lw, lg, bc(m1, NE), ALU.subtract).then_inc(s["lg_sub"], 1)
            dr().then_inc(s["lg_ok"], 1)
            dve.wait_ge(s["lg_exp"], 1)
            tt(gate, gate, msk, ALU.mult)
            dr()
            dve.tensor_reduce(rsum, gate, AX.X, ALU.add)
            dr()
            dve.reciprocal(rsum, rsum)
            dr()
            tt(gate, gate, bc(rsum, NE), ALU.mult)
            dve.wait_ge(s["rk_mm"], 1)
            stt(cand.rearrange("p a b -> p (a b)"), PB[1][:, 0:TT * NE], 1.0, msk.rearrange("p a b -> p (a b)"), ALU.add, ALU.mult)
            dve.tensor_reduce(cmax[0:1, :], PB[1][0:1, 2 * NE:3 * NE], AX.X, ALU.max)
            dve.memset(rankT[:, PASSES * NE:, :], -1.0)
            dve.memset(gateT[:, PASSES * NE:, :], 0.0)
            dve.memset(selT[:, PASSES * NE:], 0.0)
            dr()
            dve.tensor_copy(npass[0:1, 0:1], cmax[0:1, :]).then_inc(s["pass_ok"], 1)
            for p in range(PASSES):
                e = slice(p * NE, (p + 1) * NE)
                ts(rankT[:, e, :].rearrange("p e t -> p t e"), cand, float(1 + p * CAP), ALU.subtract)
                dve.tensor_copy(gateT[:, e, :].rearrange("p e t -> p t e"), gate)
                dve.tensor_copy(selT[:, e], C[:, K_SEL:K_SEL + NE])
            dr()

            def one_hot(t):
                for e in range(2):
                    for k in range(TT):
                        r, g = rankT[:, bass.ds(2 * t + e, 1), k], gateT[:, bass.ds(2 * t + e, 1), k]
                        ts(Pg[:, k, e, :], C[:, K_IOTA:K_IOTA + CAP], r, ALU.is_equal)
                        last = ts(PGd[:, e, k, :], C[:, K_IOTA:K_IOTA + P], r, ALU.is_equal, g, ALU.mult)
                last.then_inc(s["pg_ok"], 1)

            def selectors(t):
                for e in range(2):
                    last = dve.tensor_copy(bselv[0:B3, e * CAP:(e + 1) * CAP], selT[0:B3, bass.ds(2 * t + e, 1)].to_broadcast([B3, CAP]))
                last.then_inc(s["bsel_ok"], 1)

            def tokens(t):
                dve.wait_ge(s["gat_mm"], t + 1)
                g = gain(3)
                for i in range(2):
                    last = tt(xg[:, 4 * i:4 * i + 4, :, :].rearrange("p k e c -> p k (e c)"), PB[4 + i].rearrange("p (a b) -> p a b", b=P), bc(g[:, 4 * i:4 * i + 4], P), ALU.mult)
                last.then_inc(s["xg_ok"], 1)

            def swiglu(t, e):
                dve.wait_ge(s["gu_used"], 16 * t + 8 * (e + 1))
                ts(gg, PB[0], LIMIT, ALU.min).then_inc(s["act_g"], 1)
                ts(uu, PB[1], LIMIT, ALU.min, -LIMIT, ALU.max).then_inc(s["gu_taken"], 1)
                dr()
                stt(uu, uu, 1.0, gg, ALU.add, ALU.mult)
                dr()
                dve.wait_ge(s["act_s"], 2 * t + (e + 1))
                tt(hh, uu, sg, ALU.mult).then_inc(s["h_ok"], 1)

            def add_up(t, e):
                dve.wait_ge(s["scat"], 2 * t + (e + 1))
                for k in range(TT):
                    last = tt(X[:, k, :], X[:, k, :], psum[:, (4 + 2 * k) * 512:(6 + 2 * k) * 512], ALU.add)
                last.then_inc(s["acc_ok"], 1)

            def experts(t):
                swiglu(t, 0)
                add_up(t, 0)
                dve.wait_ge(s["gat_mm"], t + 1)
                dve.wait_ge(s["pgt_mm"], t + 1)
                one_hot(t + 1)
                swiglu(t, 1)
                tokens(t + 1)
                dve.wait_ge(s["dn_used"], 16 * t + 16)
                selectors(t + 1)
                add_up(t, 1)

            dve.sem_inc(s["gu_taken"], 1)
            dve.sem_inc(s["acc_ok"], 1)
            one_hot(0)
            selectors(0)
            tokens(0)
            with dve.Fori(0, NE // 2) as t:
                experts(t)
            dve.wait_ge(s["pass_ok"], 1)
            many = dve.value_load(npass[0:1, 0:1], min_val=0, max_val=SEQ)
            with dve.If(many > CAP):
                with dve.Fori(NE // 2, PASSES * (NE // 2)) as t:
                    experts(t)
            dr().then_inc(s["fin_acc"], 1)
            dve.wait_ge(s["rinv_n"], 5)
            dve.wait_ge(s["fg_in"], 16)
            for t in range(TT):
                last = stt(X[:, t, :], X[:, t, :], stat[:, 4, 2, t:t + 1], fgb, ALU.mult, ALU.mult)
            last.then_inc(s["fin_ok"], 1)

        @block.gpsimd
        def _(pool):
            def tt(out, a0, a1, op=ALU.mult):
                return pool.tensor_tensor(out, a0, a1, op)

            pool.sem_inc(s["mul_ok"], 2)
            pool.memset(raw, 0.0).then_inc(s["pads"], 1)
            with pool.Fori(0, 3) as it:
                for j in range(RING):
                    pool.wait_ge(s["sig_ok"], 4 * it + (j + 1))
                    tt(cT[:, bass.ds(8 * it + 2 * j, 2), :].rearrange("p a b -> p (a b)"), cy[:, j % 2, :], csg[:, j % 2, :]).then_inc(s["mul_ok"], 1)
            pool.drain()
            with pool.Fori(0, HEADS // 2) as b:
                pool.wait_ge(s["body_free"], b + 1)
                q, k, v = (cT[:, bass.ds(2 * b + i * HEADS, 2), :].rearrange("p a b -> p (a b)") for i in range(3))
                tt(sqq, q, q)
                tt(sqk, k, k)
                pool.tensor_copy(vst, v).then_inc(s["sq_ok"], 1)
                pool.wait_ge(s["u0_ok"], b + 1)
                for lv in range(1, LEVELS):
                    if lv > 1:
                        pool.wait_ge(s["m1_mm"], 6 * b + (lv - 1))
                    m = C[:, K_LEVEL + lv * P:K_LEVEL + (lv + 1) * P]
                    tt(LT, AT, m.unsqueeze(1).to_broadcast([P, 4, P])).then_inc(s["lt_ok"], 1)
            pool.wait_ge(s["body_free"], 5)
            pool.wait_ge(s["proj_taken"], N_LOOP + 2)
            pool.tensor_copy(qr, big[:, 8:16, :]).then_inc(s["qcopy"], 1)
            pool.wait_ge(s["bias_in"], 16 * 6)
            pool.tensor_copy(bspl, btmp)
            pool.drain()
            tt(btmp, btmp, bspl, ALU.subtract)
            pool.drain()
            pool.tensor_copy(bmid, btmp)
            pool.drain()
            tt(btmp, btmp, bmid, ALU.subtract)
            pool.drain()
            pool.tensor_copy(bspl[NE:2 * NE, :], bmid[NE:2 * NE, :])
            pool.drain()
            pool.tensor_copy(bspl[2 * NE:3 * NE, :], btmp[2 * NE:3 * NE, :]).then_inc(s["prep_ok"], 1)


_DEPTH = ["attn_norm_g", "w_in", "gdn_conv_w", "gdn_a_log", "gdn_dt_bias", "gdn_norm_g", "cmp_pe_k", "cmp_w1_k",
          "cmp_w2_k", "cmp_pe_v", "cmp_w1_v", "cmp_w2_v", "w_branch_a", "w_branch_b", "w_mix_out", "xattn_norm_g",
          "mem_norm_g", "xattn_w_q", "xattn_w_kv", "xattn_w_o", "ffn_norm_g", "router_w", "router_b", "w_gate_up",
          "b_gate_up", "w_down", "b_down"]
_ROWS = ("attn_norm_g", "xattn_norm_g", "mem_norm_g", "ffn_norm_g", "gdn_a_log", "gdn_dt_bias", "gdn_norm_g", "router_b")


def kernel(**inputs):
    import concourse.bacc as bacc
    from concourse.bass_utils import run_bass_kernel_spmd

    nc = bacc.Bacc("TRN2", target_bir_lowering=False, num_devices=1)
    arrays = {}
    for name in ["x", "mem", "final_norm_g"] + _DEPTH:
        v = np.ascontiguousarray(inputs[name])
        arrays[name] = v[0] if name in _DEPTH and name not in _ROWS else v
    arrays["tab"], arrays["rope"] = constants()
    aps = {n: nc.dram_tensor("in_" + n, v.shape, mybir.dt.from_np(v.dtype), kind="ExternalInput").ap() for n, v in arrays.items()}
    aps["out"] = nc.dram_tensor("out", (1, SEQ, D), mybir.dt.float32, kind="ExternalOutput").ap()
    build(nc, aps)
    r = run_bass_kernel_spmd(nc, [{"in_" + n: v for n, v in arrays.items()}], core_ids=[0])
    return r.results[0]["out"]
```

```python
import math

import numpy as np
import concourse.bass as bass
from concourse import mybir
from contextlib import ExitStack

P = 128
D = 1024
KT = D // P
SEQ = 256
TT = SEQ // P
HEADS = 8
GROUPS = 2
REP = HEADS // GROUPS
DH = 128
CONV = 4
ROT = 32
CMP_LEN, CMP_STRIDE = 32, 16
NCMP = (SEQ - CMP_LEN) // CMP_STRIDE + 1
XH = 4
NE = 32
TOPK = 4
CAP = 64
EPS = 1e-6
NEG = -1e30
LIMIT, ALPHA = 7.0, 1.702
LEVELS = 7
SCALE = DH ** -0.5

C_B = 4 * D
C_NQ = C_B + 2 * HEADS
C_KC = C_NQ + D
KV = GROUPS * DH
C_VC, C_KS, C_VS, C_KW, C_VW = (C_KC + KV * i for i in range(1, 6))
C_NG = C_KC + 6 * KV
C_MA = C_NG + 3 * HEADS
C_MB = C_MA + D

K_ID, K_TRIU, K_STRICT, K_ONES, K_ZERO, K_CAUSAL, K_IOTA, K_CMPA = (P * i for i in range(8))
K_CMPM = K_CMPA + TT * NCMP
K_E = K_CMPM + TT * NCMP
K_SEL = K_E + NE
K_EPS = K_SEL + NE
NK = K_EPS + 1
R_ROT, R_COS, R_SIN = 0, ROT, ROT + SEQ
NR = ROT + 2 * SEQ

SLOT = 256
RING = 4


def constants():
    c = np.zeros((P, NK), np.float32)
    j, i = np.meshgrid(np.arange(P), np.arange(P), indexing="ij")
    c[:, K_ID:K_ID + P] = j == i
    c[:, K_TRIU:K_TRIU + P] = j <= i
    c[:, K_STRICT:K_STRICT + P] = j < i
    c[:, K_ONES:K_ONES + P] = 1
    c[:, K_CAUSAL:K_CAUSAL + P] = np.where(i <= j, 0, NEG)
    c[:, K_IOTA:K_IOTA + P] = i % CAP
    lv = np.zeros((P, LEVELS * P), np.float32)
    for n in range(LEVELS):
        s = 1 << n
        lv[:, n * P:(n + 1) * P] = (j // (2 * s) == i // (2 * s)) & (j // s % 2 == 0) & (i // s % 2 == 1)
    for t in range(TT):
        q = t * P + np.arange(P)[:, None]
        ok = np.arange(NCMP)[None] * CMP_STRIDE + CMP_LEN - 1 <= q
        c[:, K_CMPA + t * NCMP:K_CMPA + (t + 1) * NCMP] = np.where(ok, 0, NEG)
        c[:, K_CMPM + t * NCMP:K_CMPM + (t + 1) * NCMP] = ok
    c[:, K_E:K_E + NE] = np.arange(NE)
    c[:, K_SEL:K_SEL + NE] = np.arange(P)[:, None] % NE == np.arange(NE)
    c[:, K_EPS] = EPS
    r = np.zeros((ROT, NR), np.float32)
    half = ROT // 2
    for m in range(half):
        r[m + half, R_ROT + m] = -1
        r[m, R_ROT + m + half] = 1
    freq = np.exp(np.float32(-math.log(500000.0)) * np.arange(half, dtype=np.float32) * np.float32(2.0 / ROT))
    ang = np.arange(SEQ, dtype=np.float32)[None] * freq[:, None].astype(np.float32)
    r[:, R_COS:R_COS + SEQ] = np.tile(np.cos(ang), (2, 1))
    r[:, R_SIN:R_SIN + SEQ] = np.tile(np.sin(ang), (2, 1))
    return c, lv, r


def build(nc, a, dbg=None):
    f32, bf16, i32 = mybir.dt.float32, mybir.dt.bfloat16, mybir.dt.int32
    ALU, ACT, AX = mybir.AluOpType, mybir.ActivationFunctionType, mybir.AxisListType

    def cols(w, c0, k=KT, n=SLOT):
        return w[:, c0:c0 + n].rearrange("(k p) n -> p k n", p=P)

    w_in = a["w_in"]
    chunks = [cols(w_in, c) for c in range(0, 4 * D, SLOT)]
    chunks += [cols(w_in, C_NQ + c) for c in range(0, D, SLOT)]
    chunks += [cols(w_in, c) for c in (C_KC, C_VC, C_KS, C_KW)]
    chunks += [cols(w_in, C_MA + c) for c in range(0, D, SLOT)]
    N_XKV = len(chunks)
    chunks += [cols(a["xattn_w_kv"], c) for c in range(0, 2 * XH * DH, SLOT)]
    N_VS = len(chunks)
    chunks += [cols(w_in, c) for c in (C_VS, C_VW)]
    N_W1 = len(chunks)
    for w in (a["cmp_w1_k"], a["cmp_w1_v"]):
        v = w.rearrange("(l d) f -> d l f", d=DH)
        chunks += [v[:, l:l + CMP_LEN // 2, :] for l in (0, CMP_LEN // 2)]
    N_MB = len(chunks)
    chunks += [cols(w_in, C_MB + c) for c in range(0, D, SLOT)]
    N_BA = len(chunks)
    chunks += [cols(a["w_branch_a"], c) for c in range(0, D, SLOT)]
    N_BB = len(chunks)
    chunks += [cols(a["w_branch_b"], c) for c in range(0, D, SLOT)]
    N_MIX = len(chunks)
    chunks += [cols(a["w_mix_out"], c) for c in range(0, D, SLOT)]
    N_XQ = len(chunks)
    chunks += [cols(a["xattn_w_q"], c) for c in range(0, XH * DH, SLOT)]
    N_XO = len(chunks)
    chunks += [cols(a["xattn_w_o"], c) for c in range(0, D, SLOT)]
    N_END = len(chunks)

    N_Z = 4 * D // SLOT - 4
    fillers = [*range(N_Z, N_VS), *range(N_MB, N_BB)]
    PRODUCTS = 2 * KT
    table_goal = [8 * (i + 1) for i in range(HEADS)]
    first_goal = [table_goal[-1] + 6, table_goal[-1] + 12]
    start_goal = [first_goal[1] + 50 * b + 2 for b in range(HEADS // 2)]
    gap_goal = [[start_goal[b] + 8 * (g // 2) + (3, 8)[g % 2] for g in range(2 * LEVELS - 2)] for b in range(HEADS // 2)]
    tail_goal = [gap_goal[-1][-1] + 6 * (i + 1) for i in range(5)]
    delta_goal = PRODUCTS * (N_VS - N_Z)
    w1_goal, w2_goal = delta_goal + 4, delta_goal + 8
    rope_goal = [w2_goal + 2 * (i + 1) for i in range(6)]
    cs_goal = rope_goal[-1] + 20
    ct_goal = [cs_goal + 2 * (i + 1) for i in range(4)]
    step_goal = [[ct_goal[-1] + 9 * i + 5, ct_goal[-1] + 9 * i + 9] for i in range(8)]
    all_goal = PRODUCTS * len(fillers)

    ctx = ExitStack()
    with ctx:
        def sb(name, shape, dt=f32):
            return ctx.enter_context(nc.sbuf_tensor(name, shape, dt))

        def sem(name):
            return ctx.enter_context(nc.semaphore(name))

        EXPERT = KT * 2 * D + KT * D
        early = sb("early", [P, EXPERT])
        at = {"early": 0, "mid": 0}

        def part(region, name, *dims, rows=P):
            n = int(np.prod(dims))
            o = at[name]
            at[name] = o + n
            v = region[0:rows, o:o + n]
            if len(dims) == 2:
                v = v.rearrange("p (a b) -> p a b", b=dims[1])
            elif len(dims) == 3:
                v = v.rearrange("p (a b c) -> p a b c", b=dims[1], c=dims[2])
            return v

        def E(*dims, rows=P):
            return part(early, "early", *dims, rows=rows)

        X = sb("X", [P, TT, D])
        hT = sb("hT", [P, KT, SEQ])
        C = sb("C", [P, NK])
        R = sb("R", [ROT, NR])
        ring = sb("ring", [P, RING, KT * SLOT])
        big = sb("big", [P, 32, SEQ])
        mb = sb("mb", [P, KT, SEQ])
        xkT = sb("xkT", [P, XH, SEQ])
        xv = sb("xv", [P, TT, XH * DH])
        colsA = sb("colsA", [P, P])
        colsB = sb("colsB", [P, 2 * CMP_LEN + 1])
        bspl = sb("bspl", [3 * NE, 3 * D], bf16)[:, :]
        w_rt = sb("w_rt", [P, KT, NE])
        TK = sb("TK", [P, 4, TT, HEADS])
        gates = sb("gates", [P, TT, 3 * HEADS])
        stat = sb("stat", [P, 5, 3, TT])
        small = sb("small", [P, 96])

        levels = mb[:, :, :].rearrange("p a b -> p (a b)")[:, 0:LEVELS * P]
        eG = xkT[:, :, :].rearrange("p a b -> p (a b)").rearrange("p (h n) -> p h n", n=P)
        xvf = xv[:, :, :].rearrange("p a b -> p (a b)")
        w_ba = xvf[:, 0:KT * 2 * HEADS].rearrange("p (k n) -> p k n", k=KT)
        w_ng = xvf[:, KT * 2 * HEADS:KT * 5 * HEADS].rearrange("p (k n) -> p k n", k=KT)

        STAGE = 2 * P + 2 * TT * D
        MT_END = STAGE + KT * SEQ
        CT_END = MT_END + 3 * HEADS * SEQ
        OA = EXPERT - HEADS * SEQ
        rowsA, rowsB, memx, Xn = E(P), E(P), E(TT, D), E(TT, D)
        mT = E(KT, SEQ)
        cT = E(3 * HEADS, SEQ)
        assert at["early"] == CT_END
        raw = E(2, 2, SEQ + CONV - 1)
        cy, csg = E(2, 2 * SEQ), E(2, 2 * SEQ)
        GB = E(2, SEQ, rows=HEADS)
        TP = E(4, SEQ, rows=HEADS)
        g1 = E(4, SEQ, rows=HEADS)
        abias = E(4, rows=HEADS)
        at["early"] = 0
        EDm, EDB = E(HEADS, TT, P), E(HEADS, TT, P)
        assert at["early"] <= STAGE
        at["early"] = CT_END
        QKm, AT, kd, vb, Um = ([E(4, P) for _ in range(2)] for _ in range(5))
        qd = [E(2, P) for _ in range(2)]
        LT, M1s, Tm, dd, u, sqo, lno = (E(4, P) for _ in range(7))
        wT, S1, vn = E(2, P), E(2, P), E(2, P)
        assert at["early"] <= OA
        sq, lnr, ddh = QKm, AT, [kd[0][:, 2 * i:2 * i + 2, :] for i in range(2)]
        at["early"] = OA - HEADS * 2 * SEQ - 16
        GBrow = E(HEADS, 2 * SEQ, rows=1)
        assert at["early"] <= OA
        at["early"] = OA
        oaT = E(HEADS, SEQ)
        at["early"] = 0
        obT = E(HEADS, SEQ)
        qr = E(HEADS, SEQ)
        assert at["early"] <= STAGE
        at["early"] = MT_END
        vtok = E(2, TT, KV)
        blk = E(2, CMP_LEN, GROUPS * NCMP)
        S = [E(REP, SEQ) for _ in range(2)]
        PT = [E(TT, REP, SEQ) for _ in range(2)]
        PcT = E(HEADS, SEQ, rows=NCMP)
        w2 = E(2, DH)
        ccT = E(GROUPS * NCMP)
        vc = E(GROUPS, DH, rows=NCMP)
        s1, s1g = E(2, GROUPS * NCMP), E(2, GROUPS * NCMP)
        sc = E(TT, HEADS, NCMP)
        rt1, rt2 = E(2, SEQ, rows=ROT), E(2, SEQ, rows=ROT)
        zs = E(HEADS, SEQ)
        assert at["early"] <= OA

        yaT, mixT = big[:, 8:16, :], big[:, 16:24, :]

        def tiles(i, *dims):
            v = big[:, i:i + 8, :].rearrange("p a b -> p (a b)")
            return v.rearrange("p (a b) -> p a b", b=dims[-1]) if len(dims) == 2 else v.rearrange("p (a b c) -> p a b c", b=dims[1], c=dims[2])
        x2n = tiles(0, TT, D)
        S2 = [big[:, 8 + 4 * i:12 + 4 * i, :] for i in range(2)]
        PTx = tiles(16, TT, XH, SEQ)
        xqT, xoT = big[:, 24:28, :], big[:, 28:32, :]

        names = """c_in rope_in rows_in x_in mem_in wba_in ab_in w2_in rt_in gbrow_in bias_in fg_in out_out
        cols_tr cols_ok sq_n rinv_n xn_n tr_n hT_n
        ba_mm ba_sig sp_lin sp_exp gc_ok gc_exp tp_ok tp_tr tk_ok pads
        proj_done proj_taken conv_ok sig_ok mul_ok
        lv_in sq_ok ss_mm rinv_g qk_ok bc_mm dd_ok ed_ok tab_ok pre_mm qkm_ok kd_ok vt_mm vb_ok u0_ok qd_ok t0_mm t0_ok lt_ok m1_mm m1_ok c_mm tu_ok
        u_mm u_ok w_ok s_mm s_ok ws_mm vn_ok o_mm sqo_ok so_mm lno_ok oa_ok
        blk_ok w1_act w2_mm w2_ok qcopy rope_mm rope_ok
        sc_mm sc_read mx_ok ex_ok pn_ok tp_mm tp_taken cs_mm cs_max cs_exp cs_ok ct_mm ct_ok pv_mm pv_ok
        zsig z_ok mb_ok mixed
        lg_mm lg_sub lg_exp lg_ok rk_mm pass_ok prep_ok
        pg_ok gat_mm xg_ok pgt_mm pgt_ok gu_taken act_g act_s h_ok ht_mm ht_ok y_ok scat acc_ok gu_used dn_used
        bsel_ok fin_acc fin_r fin_ok""".split()
        s = {n: sem(n) for n in names}
        ring_in = [sem(f"ring_in{i}") for i in range(RING)]
        gu_in = [sem(f"gu_in{k}") for k in range(KT)]
        dn_in = [sem(f"dn_in{k}") for k in range(KT)]
        psum = ctx.enter_context(nc.psum_tensor("psum", [P, 8 * 512], f32))
        PB = [psum[:, 512 * i:512 * (i + 1)] for i in range(8)]

        def flat2(v):
            return v.rearrange("p a b -> p (a b)")

        ident = C[:, K_ID:K_ID + P]
        ones = C[:, K_ONES:K_ONES + P]
        eps = C[:, K_EPS:K_EPS + 1]
        one = C[:, K_ONES:K_ONES + 1]

        def gain(n):
            return colsA[:, CONV * 24 + 8 * n:CONV * 24 + 8 * n + 8]

        def rw(slot):
            return ring[:, slot, :].rearrange("p (k n) -> p k n", k=KT)

        flat = big[:, :, :].rearrange("p a b -> p (a b)")

        def M(*dims, rows=P):
            return part(flat, "mid", *dims, rows=rows)
        x3n = M(TT, D)
        xg = M(KT, 2, CAP)
        Pg = M(TT, 2, CAP)
        PGd = M(2, TT, P)
        PGT = M(2, TT, P)
        gg, uu, sg, hh = M(512), M(512), M(512), M(512)
        hTt = M(4, P)
        ys = M(512)
        bselb = M(CAP)
        assert at["mid"] <= 32 * SEQ
        rflat = ring[:, :, :].rearrange("p a b -> p (a b)")
        B3 = 3 * NE
        bt0 = MT_END + 2 * TT * KV
        btmp, bmid = early[0:B3, bt0:bt0 + D], early[0:B3, bt0 + D:bt0 + D + D // 2].bitcast(bf16)
        fgb = rflat[:, 0:D]
        bselv = bselb.bitcast(bf16)
        rb = small[0:1, 0:NE]
        mbf = mb[:, :, :].rearrange("p a b -> p (a b)")
        at["rt"] = 0

        def RT(*dims):
            return part(mbf, "rt", *dims)
        PASSES = SEQ // CAP
        NT = PASSES * NE + 2
        lg, lw, msk, oh, eqm, cand, gate = (RT(TT, NE) for _ in range(7))
        rankT, gateT = RT(NT, TT), RT(NT, TT)
        selT = RT(NT)
        mx, m1, rsum = (RT(TT) for _ in range(3))
        cmax = RT(1)
        npass = sb("npass", [1, 1], i32)

        wg = early[:, 0:KT * 2 * D].rearrange("p (k n) -> p k n", k=KT)
        wd = early[:, KT * 2 * D:EXPERT].rearrange("p (k n) -> p k n", k=KT)

        def sparse_step(i):
            g, br, t = i // 4, i // 2 % 2, i % 2
            return dict(q=lambda h: qr[:, g * REP + h, t * P:(t + 1) * P], k=lambda h: big[:, 20 + 2 * br + g, :],
                        n=t + 1, S=S[i % 2], PT=PT[br], t=t, gate=gates[:, t, :].rearrange("p (h b) -> p h b", b=3)[:, g * REP:(g + 1) * REP, 1 + br:2 + br])

        def memory_step(t):
            return dict(q=lambda h: xqT[:, h, t * P:(t + 1) * P], k=lambda h: xkT[:, h, :], n=TT, S=S2[t], PT=PTx, t=t, gate=None)
        steps = [sparse_step(i) for i in range(8)] + [memory_step(t) for t in range(TT)]
        smx, ssum = small[:, 64:72].rearrange("p (a b) -> p a b", a=2), small[:, 72:80].rearrange("p (a b) -> p a b", a=2)

        scope = dict(locals())
        block = ctx.enter_context(nc.Block())

        @block.sync
        def _(sp):
            sp.dma_start(X[:, :, :], a["x"].rearrange("o (t p) d -> p (o t) d", p=P)).then_inc(s["x_in"], 16)
            sp.dma_start(C[:, :], a["tab"]).then_inc(s["c_in"], 16)
            sp.dma_start(memx, a["mem"].rearrange("o (t p) d -> p (o t) d", p=P)).then_inc(s["mem_in"], 16)
            for n, src in enumerate(chunks):
                if n >= RING:
                    sp.wait_ge(s["proj_done"], n - RING + 1)
                k = src.shape[1]
                dst = ring[:, n % RING, 0:k * src.shape[2]].rearrange("p (k n) -> p k n", k=k)
                sp.dma_start(dst, src).then_inc(ring_in[n % RING], 16)
                if n == RING:
                    sp.dma_start(levels, a["levels"]).then_inc(s["lv_in"], 16)
                    sp.dma_start(R[:, :], a["rope"]).then_inc(s["rope_in"], 16)
                if n == N_VS:
                    sp.wait_ge(s["oa_ok"], 4)
                    sp.dma_start(w2[:, 0, :], a["cmp_w2_k"]).then_inc(s["w2_in"], 16)
                    sp.dma_start(w2[:, 1, :], a["cmp_w2_v"]).then_inc(s["w2_in"], 16)
                    sp.dma_start(w_rt[:, :, :], a["router_w"].rearrange("(k p) n -> p k n", p=P)).then_inc(s["rt_in"], 16)
                    sp.dma_start(rb, a["router_b"]).then_inc(s["rt_in"], 16)

            sp.wait_ge(s["pv_ok"], 4)
            sp.wait_ge(s["prep_ok"], 1)
            sp.wait_ge(s["mixed"], 4)
            for k in range(KT):
                sp.dma_start(wg[:, k, :], a["w_gate_up"][0, k * P:(k + 1) * P, :]).then_inc(gu_in[k], 16)
            for k in range(KT):
                sp.dma_start(wd[:, k, :], a["w_down"][0, k * P:(k + 1) * P, :]).then_inc(dn_in[k], 16)
            sp.wait_ge(s["proj_done"], N_END)
            sp.dma_start(fgb, a["final_norm_g"].rearrange("(o d) -> o d", o=1).to_broadcast([P, D])).then_inc(s["fg_in"], 16)

            def expert(n, e):
                for k in range(KT):
                    sp.wait_ge(s["gu_used"], n * KT + (k + 1 - KT))
                    sp.dma_start(wg[:, k, :], a["w_gate_up"][bass.ds(e, 1), k * P:(k + 1) * P, :].rearrange("o p n -> (o p) n")).then_inc(gu_in[k], 16)
                for k in range(KT):
                    sp.wait_ge(s["dn_used"], n * KT + (k + 1 - KT))
                    sp.dma_start(wd[:, k, :], a["w_down"][bass.ds(e, 1), k * P:(k + 1) * P, :].rearrange("o p n -> (o p) n")).then_inc(dn_in[k], 16)

            with sp.Fori(1, NE) as e:
                expert(e, e)
            sp.wait_ge(s["pass_ok"], 1)
            many = sp.value_load(npass[0:1, 0:1], min_val=0, max_val=SEQ)
            with sp.If(many > CAP):
                with sp.Fori(1, SEQ // CAP) as p:
                    with sp.Fori(0, NE) as e:
                        expert(p * NE + e, e)
            sp.wait_ge(s["fin_ok"], 1)
            sp.dma_start(a["out"].rearrange("o (t p) d -> p (o t) d", p=P), X[:, :, :]).then_inc(s["out_out"], 16)
            if dbg:
                for name, ap in dbg(scope):
                    sp.dma_start(a["dbg_" + name], ap).then_inc(s["out_out"], 16)
                sp.wait_ge(s["out_out"], 16 * (1 + len(dbg(scope))))
            else:
                sp.wait_ge(s["out_out"], 16)

        @block.tensor
        def _(pe):
            def mm(out, lhsT, rhs, start=True, stop=True):
                return pe.matmul(out, lhsT, rhs, start=start, stop=stop)

            def tr(out, in_):
                n = in_.shape[0]
                return pe.transpose(out, in_, C[0:n, K_ID:K_ID + n])

            def norm_T(n):
                src = x3n if n == 3 else Xn if n < 2 else x2n
                pe.wait_ge(s["xn_n"], n + 1)
                for b in range(4):
                    for k in range(2):
                        for t in range(TT):
                            last = tr(PB[2 + b][:, k * SEQ + t * P:k * SEQ + (t + 1) * P], src[:, t, (2 * b + k) * P:(2 * b + k + 1) * P])
                    last.then_inc(s["tr_n"], 1)

            pe.wait_ge(s["c_in"], 16)
            pe.wait_ge(s["rows_in"], 16 * 8)
            tr(PB[0][:, 0:P], rowsA)
            tr(PB[0][:, P:P + 65], rowsB[0:65, :]).then_inc(s["cols_tr"], 1)
            norm_T(0)
            pe.wait_ge(s["wba_in"], 32)
            pe.wait_ge(s["hT_n"], 4)
            for j in range(2):
                for k in range(KT):
                    mm(PB[6][0:HEADS, j * SEQ:(j + 1) * SEQ], w_ba[:, k, j * HEADS:(j + 1) * HEADS], hT[:, k, :], k == 0, k == KT - 1)
            for t in range(TT):
                for k in range(KT):
                    last = mm(PB[7][:, t * 24:t * 24 + 24], hT[:, k, t * P:(t + 1) * P], w_ng[:, k, :], k == 0, k == KT - 1)
            last.then_inc(s["ba_mm"], 1)

            def chunk(slot, nth, turn, src, tok=False, tiles=2, half=None, kt=KT):
                bank = PB[slot % 2]
                if half in (None, 0):
                    pe.wait_ge(ring_in[slot], nth)
                    pe.wait_ge(s["proj_taken"], turn)
                w = rw(slot) if kt == KT else ring[:, slot, 0:kt * SLOT].rearrange("p (k n) -> p k n", k=kt)
                for i in range(2):
                    if half is not None and i != half:
                        continue
                    for k in range(kt):
                        if tok:
                            last = mm(bank[:, i * SLOT:(i + 1) * SLOT], src[:, k, i * P:(i + 1) * P], w[:, k, :], k == 0, k == kt - 1)
                        else:
                            last = mm(bank[:, i * SEQ:(i + 1) * SEQ], w[:, k, i * P:(i + 1) * P], src[:, k, :], k == 0, k == kt - 1)
                if half in (None, 1):
                    last.then_inc(s["proj_done"], 1)

            def chunk_n(n, src, **kw):
                chunk(n % RING, 16 * (n // RING + 1), n + 1, src, **kw)

            with pe.Fori(0, 3) as it:
                for j in range(RING):
                    chunk(j, 16 * it + 16, 4 * it + (j + 1), hT)
            norm_T(1)
            pe.wait_ge(s["tp_ok"], 1)
            pe.wait_ge(s["hT_n"], 8)
            for q in range(4):
                for t in range(TT):
                    last = tr(PB[6][:, (q * TT + t) * HEADS:(q * TT + t + 1) * HEADS], TP[:, q, t * P:(t + 1) * P])
            last.then_inc(s["tp_tr"], 1)

            filled = [0]

            def fill(goal):
                goal = min(goal, all_goal)
                for j in range(filled[0], goal):
                    n, i, k = fillers[j // PRODUCTS], j // KT % 2, j % KT
                    if (i, k) == (0, 0):
                        pe.wait_ge(ring_in[n % RING], 16 * (n // RING + 1))
                        pe.wait_ge(s["proj_taken"], n + 1)
                        if n == N_BA:
                            pe.wait_ge(s["z_ok"], 1)
                    out = PB[n % 2][:, i * SEQ:(i + 1) * SEQ]
                    src = mT if N_XKV <= n < N_VS else oaT if n >= N_BA else hT
                    if N_XKV + 2 <= n < N_VS:
                        last = mm(out, src[:, k, i * P:(i + 1) * P], rw(n % RING)[:, k, :], k == 0, k == KT - 1)
                    else:
                        last = mm(out, rw(n % RING)[:, k, i * P:(i + 1) * P], src[:, k, :], k == 0, k == KT - 1)
                    if (i, k) == (1, KT - 1):
                        last.then_inc(s["proj_done"], 1)
                filled[0] = max(filled[0], goal)

            pe.wait_ge(s["gbrow_in"], 16 * HEADS)
            for i in range(HEADS):
                pe.wait_ge(s["sq_ok"], i + 1)
                if i >= 2:
                    pe.wait_ge(s["rinv_g"], i - 1)
                mm(PB[4 + i % 2], ones, flat2(sq[i % 2])).then_inc(s["ss_mm"], 1)
                if i >= 2:
                    pe.wait_ge(s["tab_ok"], i - 1)
                mm(PB[2 + i % 2], C[0:1, K_ONES:K_ONES + P], GBrow[0:1, i, :]).then_inc(s["bc_mm"], 1)
                fill(table_goal[i])

            def before(b, part):
                if part == 0:
                    if b == 0:
                        pe.wait_ge(s["qk_ok"], HEADS)
                        pe.wait_ge(s["rinv_g"], HEADS)
                    elif b >= 2:
                        pe.wait_ge(s["oa_ok"], b - 1)
                    for h in range(2):
                        for t in range(TT):
                            m, k, q = slice((2 * h + t) * P, (2 * h + t + 1) * P), HEADS + 2 * b + h, 2 * b + h
                            f = slice(t * P, (t + 1) * P)
                            mm(PB[5][:, m], cT[:, k, f], cT[:, k, f])
                            mm(PB[6][:, m], cT[:, k, f], cT[:, q, f])
                            last = tr(PB[7][:, m], cT[:, k, f])
                    last.then_inc(s["pre_mm"], 1)
                else:
                    pe.wait_ge(s["kd_ok"], b + 1)
                    for h in range(2):
                        for t in range(TT):
                            last = tr(PB[7][:, (2 * h + t) * P:(2 * h + t + 1) * P], cT[:, 2 * HEADS + 2 * b + h, t * P:(t + 1) * P])
                    last.then_inc(s["vt_mm"], 1)

            def after(b, part):
                B = b % 2
                if part == 0:
                    pe.wait_ge(s["tu_ok"], 6 * b + 6)
                    if b < 3:
                        pe.wait_ge(s["qkm_ok"], b + 2)
                    for m in range(4):
                        mm(PB[5][:, m * P:(m + 1) * P], Um[B][:, m, :], vb[B][:, m, :])
                    for h in range(2):
                        last = mm(PB[6][:, h * P:(h + 1) * P], kd[B][:, 2 * h + 1, :], Um[B][:, 2 * h + 1, :])
                    last.then_inc(s["u_mm"], 1)
                elif part == 1:
                    pe.wait_ge(s["u_ok"], b + 1)
                    if b < 3:
                        pe.wait_ge(s["vb_ok"], b + 2)
                    for h in range(2):
                        last = mm(PB[7][:, h * P:(h + 1) * P], kd[B][:, 2 * h, :], u[:, 2 * h, :])
                    last.then_inc(s["s_mm"], 1)
                elif part == 2:
                    pe.wait_ge(s["w_ok"], b + 1)
                    pe.wait_ge(s["s_ok"], b + 1)
                    for h in range(2):
                        last = mm(PB[6][:, h * P:(h + 1) * P], wT[:, h, :], S1[:, h, :])
                    last.then_inc(s["ws_mm"], 1)
                elif part == 3:
                    pe.wait_ge(s["vn_ok"], b + 1)
                    for h in range(2):
                        o = PB[5][:, h * SEQ:(h + 1) * SEQ]
                        mm(o[:, 0:P], u[:, 2 * h, :], QKm[B][:, 2 * h, :])
                        mm(o[:, P:SEQ], S1[:, h, :], qd[B][:, h, :], True, False)
                        last = mm(o[:, P:SEQ], vn[:, h, :], QKm[B][:, 2 * h + 1, :], False, True)
                    last.then_inc(s["o_mm"], 1)
                else:
                    pe.wait_ge(s["sqo_ok"], b + 1)
                    mm(PB[7], ones, flat2(sqo)).then_inc(s["so_mm"], 1)

            def side(b, gap):
                if b and gap < 5:
                    after(b - 1, gap)
                if b < 3 and gap in (6, 8):
                    before(b + 1, (gap - 6) // 2)

            before(0, 0)
            fill(first_goal[0])
            before(0, 1)
            fill(first_goal[1])
            for b in range(HEADS // 2):
                B = b % 2
                pe.wait_ge(s["u0_ok"], b + 1)
                for m in range(4):
                    last = tr(PB[2][:, m * P:(m + 1) * P], Um[B][:, m, :])
                last.then_inc(s["t0_mm"], 1)
                fill(start_goal[b])
                pe.wait_ge(s["t0_ok"], b + 1)
                for lv in range(1, LEVELS):
                    pe.wait_ge(s["lt_ok"], 6 * b + lv)
                    if lv > 1:
                        pe.wait_ge(s["tu_ok"], 6 * b + lv - 1)
                    for m in range(4):
                        last = mm(PB[2][:, m * P:(m + 1) * P], LT[:, m, :], Tm[:, m, :])
                    last.then_inc(s["m1_mm"], 1)
                    side(b, 2 * lv - 2)
                    fill(gap_goal[b][2 * lv - 2])
                    pe.wait_ge(s["m1_ok"], 6 * b + lv)
                    if lv < LEVELS - 1:
                        for m in range(4):
                            mm(PB[3][:, m * P:(m + 1) * P], Um[B][:, m, :], M1s[:, m, :])
                    for m in range(4):
                        last = mm(PB[4][:, m * P:(m + 1) * P], M1s[:, m, :], Um[B][:, m, :])
                    last.then_inc(s["c_mm"], 1)
                    side(b, 2 * lv - 1)
                    fill(gap_goal[b][2 * lv - 1])
            for part in range(5):
                after(3, part)
                fill(tail_goal[part])
            fill(delta_goal)

            for n in range(N_VS, N_W1):
                chunk_n(n, hT, tok=True)

            pe.wait_ge(s["oa_ok"], 4)
            pe.wait_ge(s["tu_ok"], 6 * 4)
            for v in range(2):
                pe.wait_ge(s["blk_ok"], v + 1)
                for l in range(CMP_LEN):
                    n = N_W1 + 2 * v + l // 16
                    if l % 16 == 0:
                        pe.wait_ge(ring_in[n % RING], 16 * (n // RING + 1))
                    w = ring[:, n % RING, (l % 16) * P:(l % 16 + 1) * P]
                    last = mm(PB[4 + v][:, 0:GROUPS * NCMP], w, blk[:, v, l, :], l == 0, l == CMP_LEN - 1)
                    if l % 16 == 15:
                        last.then_inc(s["proj_done"], 1)
            fill(w1_goal)
            pe.wait_ge(s["w1_act"], 2)
            pe.wait_ge(s["w2_in"], 32)
            mm(PB[4][:, 0:GROUPS * NCMP], w2[:, 0, :], s1[:, 0, :])
            for g in range(GROUPS):
                last = mm(PB[4][0:NCMP, 64 + g * DH:64 + (g + 1) * DH], s1[:, 1, g * NCMP:(g + 1) * NCMP], w2[:, 1, :])
            last.then_inc(s["w2_mm"], 1)
            fill(w2_goal)
            pe.wait_ge(s["rope_in"], 16)
            for r in range(6):
                if r >= 2:
                    pe.wait_ge(s["rope_ok"], r - 1)
                src = big[0:ROT, 8 + 2 * r:10 + 2 * r, :] if r < 4 else big[0:ROT, 20 + 2 * (r - 4):22 + 2 * (r - 4), :]
                mm(PB[2 + r % 2][0:ROT, :], R[:, R_ROT:R_ROT + ROT], src.rearrange("p a b -> p (a b)")).then_inc(s["rope_mm"], 1)
                fill(rope_goal[r])
            pe.wait_ge(s["w2_ok"], 1)
            for t in range(TT):
                for h in range(HEADS):
                    g = h // REP
                    last = mm(PB[4][:, (t * HEADS + h) * 16:(t * HEADS + h) * 16 + NCMP], big[:, 8 + h, t * P:(t + 1) * P], ccT[:, g * NCMP:(g + 1) * NCMP])
            last.then_inc(s["cs_mm"], 1)
            fill(cs_goal)
            pe.wait_ge(s["cs_ok"], 1)
            for r in range(4):
                if r >= 2:
                    pe.wait_ge(s["ct_ok"], r - 1)
                for i in range(2):
                    for t in range(TT):
                        last = tr(PB[6 + r % 2][0:NCMP, i * SEQ + t * P:i * SEQ + (t + 1) * P], sc[:, t, 2 * r + i, :])
                last.then_inc(s["ct_mm"], 1)
                fill(ct_goal[r])
            pe.wait_ge(s["ct_ok"], 4)
            pe.wait_ge(s["rope_ok"], 6)

            def scores(i):
                st = steps[i]
                w = st["n"] * P
                if i >= 2:
                    pe.wait_ge(s["sc_read"], i - 1)
                for h in range(REP):
                    o = 2 * (i % 2) * 512 + h * w
                    last = mm(psum[:, 1024 + o:1024 + o + w], st["q"](h), st["k"](h)[:, 0:w])
                last.then_inc(s["sc_mm"], 1)

            def turned(i):
                st = steps[i]
                pe.wait_ge(s["pn_ok"], i + 1)
                if i:
                    pe.wait_ge(s["tp_taken"], i)
                if i == 4:
                    pe.wait_ge(s["pv_ok"], 2)
                for kt in range(st["n"]):
                    for h in range(REP):
                        last = tr(PB[6 + kt][:, h * P:(h + 1) * P], st["S"][:, h, kt * P:(kt + 1) * P])
                last.then_inc(s["tp_mm"], 1)

            scores(0)
            for g in range(GROUPS):
                for j in range(4):
                    i = 4 * g + j
                    if i < 7:
                        scores(i + 1)
                    fill(step_goal[i][0])
                    turned(i)
                    fill(step_goal[i][1])
                pe.wait_ge(s["tp_taken"], 4 * g + 4)
                for h in range(REP):
                    o = PB[6 + h // 2][:, (h % 2) * SEQ:(h % 2 + 1) * SEQ]
                    mm(o, vc[:, g, :], PcT[:, g * REP + h, :], True, False)
                    for br in range(2):
                        mm(o, vtok[:, br, 0, g * DH:(g + 1) * DH], PT[br][:, 0, h, :], False, False)
                        last = mm(o[:, P:SEQ], vtok[:, br, 1, g * DH:(g + 1) * DH], PT[br][:, 1, h, P:SEQ], False, br == 1)
                    if h % 2:
                        last.then_inc(s["pv_mm"], 1)

            fill(all_goal)
            pe.wait_ge(s["pv_ok"], 4)
            for n in range(N_BB, N_MIX):
                chunk_n(n, obT)
            pe.wait_ge(s["mixed"], 4)
            for n in range(N_MIX, N_XQ):
                chunk_n(n, mixT, tok=True)
            norm_T(2)
            pe.wait_ge(s["hT_n"], 12)
            for n in range(N_XQ, N_XO):
                chunk_n(n, hT)
            pe.wait_ge(s["proj_taken"], N_XO + 2)
            scores(8)
            scores(9)
            turned(8)
            turned(9)
            pe.wait_ge(s["tp_taken"], 10)
            for h in range(XH):
                o = PB[h // 2][:, (h % 2) * SEQ:(h % 2 + 1) * SEQ]
                for kt in range(TT):
                    last = mm(o, xv[:, kt, h * DH:(h + 1) * DH], PTx[:, kt, h, :], kt == 0, kt == 1)
                if h % 2:
                    last.then_inc(s["pv_mm"], 1)
            pe.wait_ge(s["pv_ok"], 6)
            for n in range(N_XO, N_END):
                chunk_n(n, xoT, tok=True, kt=XH)

            norm_T(3)
            pe.wait_ge(s["hT_n"], 16)
            pe.wait_ge(s["rt_in"], 32)
            for t in range(TT):
                mm(PB[0][:, t * NE:(t + 1) * NE], C[0:1, K_ONES:K_ONES + P], rb, True, False)
                for k in range(KT):
                    last = mm(PB[0][:, t * NE:(t + 1) * NE], hT[:, k, t * P:(t + 1) * P], w_rt[:, k, :], False, k == KT - 1)
            last.then_inc(s["lg_mm"], 1)
            pe.wait_ge(s["lg_ok"], 1)
            mm(PB[1][:, 0:NE], C[:, K_STRICT:K_STRICT + P], msk[:, 0, :])
            mm(PB[1][:, NE:2 * NE], ones, msk[:, 0, :], True, False)
            mm(PB[1][:, NE:2 * NE], C[:, K_STRICT:K_STRICT + P], msk[:, 1, :], False, True)
            mm(PB[1][:, 2 * NE:3 * NE], ones, msk[:, 0, :], True, False)
            mm(PB[1][:, 2 * NE:3 * NE], ones, msk[:, 1, :], False, True).then_inc(s["rk_mm"], 1)

            def gather(t):
                pe.wait_ge(s["pg_ok"], t + 1)
                for k in range(KT):
                    for tt in range(TT):
                        last = mm(PB[4 + k // 4][:, (k % 4) * P:(k % 4 + 1) * P], x3n[:, tt, k * P:(k + 1) * P], Pg[:, tt, :, :].rearrange("p a b -> p (a b)"), tt == 0, tt == 1)
                last.then_inc(s["gat_mm"], 1)

            def gate_up(t, e):
                pe.wait_ge(s["gu_taken"], 2 * t + (e + 1))
                pe.wait_ge(s["bsel_ok"], t + 1)
                if e == 0:
                    pe.wait_ge(s["xg_ok"], t + 1)
                for c in range(4):
                    mm(PB[c // 2][64 * (c % 2):64 * (c % 2) + CAP, :], bselv[0:3 * NE, e * CAP:(e + 1) * CAP], bspl[:, c * 512:(c + 1) * 512], True, False)
                for k in range(KT):
                    pe.wait_ge(gu_in[k], 32 * t + 16 * (e + 1))
                    for c in range(4):
                        last = mm(PB[c // 2][64 * (c % 2):64 * (c % 2) + CAP, :], xg[:, k, e, :], wg[:, k, c * 512:(c + 1) * 512], False, k == KT - 1)
                    last.then_inc(s["gu_used"], 1)

            def down(t, e):
                pe.wait_ge(s["h_ok"], 2 * t + (e + 1))
                for c in range(4):
                    last = tr(PB[2][:, c * P:(c + 1) * P], hh[:, c * P:(c + 1) * P])
                last.then_inc(s["ht_mm"], 1)
                pe.wait_ge(s["ht_ok"], 2 * t + (e + 1))
                for c in range(2):
                    mm(PB[3][64 * c:64 * c + CAP, :], bselv[0:3 * NE, e * CAP:(e + 1) * CAP], bspl[:, 2 * D + c * 512:2 * D + (c + 1) * 512], True, False)
                for k in range(KT):
                    pe.wait_ge(dn_in[k], 32 * t + 16 * (e + 1))
                    for c in range(2):
                        last = mm(PB[3][64 * c:64 * c + CAP, :], hTt[:, k % 4, (k // 4) * CAP:(k // 4 + 1) * CAP], wd[:, k, c * 512:(c + 1) * 512], False, k == KT - 1)
                    last.then_inc(s["dn_used"], 1)

            def scatter(t, e):
                pe.wait_ge(s["y_ok"], 2 * t + (e + 1))
                pe.wait_ge(s["pgt_ok"], t + 1)
                pe.wait_ge(s["acc_ok"], 2 * t + (e + 1))
                if e == 1:
                    pe.wait_ge(s["xg_ok"], t + 2)
                for tt in range(TT):
                    for c in range(2):
                        last = mm(PB[4 + 2 * tt + c][:, :], PGT[64 * c:64 * c + CAP, e, tt, :], ys[64 * c:64 * c + CAP, :])
                last.then_inc(s["scat"], 1)

            def experts(t):
                pe.wait_ge(s["pg_ok"], t + 1)
                for e in range(2):
                    for tt in range(TT):
                        last = tr(PB[2][:, (2 * e + tt) * P:(2 * e + tt + 1) * P], PGd[:, e, tt, :])
                last.then_inc(s["pgt_mm"], 1)
                gate_up(t, 0)
                pe.wait_ge(s["pgt_ok"], t + 1)
                down(t, 0)
                scatter(t, 0)
                gate_up(t, 1)
                pe.wait_ge(s["acc_ok"], 2 * t + 2)
                gather(t + 1)
                down(t, 1)
                scatter(t, 1)

            pe.wait_ge(s["prep_ok"], 1)
            gather(0)
            with pe.Fori(0, NE // 2) as t:
                experts(t)
            many = pe.value_load(npass[0:1, 0:1], min_val=0, max_val=SEQ)
            with pe.If(many > CAP):
                with pe.Fori(NE // 2, SEQ // CAP * (NE // 2)) as t:
                    experts(t)


        @block.scalar
        def _(act):
            def fn(out, in_, f=ACT.Copy, **kw):
                return act.activation(out, in_, f, **kw)

            def norm(n, src, junk):
                for t in range(TT):
                    fn(junk[:, t, :], src[:, t, :], ACT.Square, accum_out=stat[:, n, 0, t:t + 1])
                act.drain()
                if n == 0:
                    act.wait_ge(s["c_in"], 16)
                fn(stat[:, n, 1, :], stat[:, n, 0, :], ACT.Ln, scale=1.0 / D, bias=eps)
                act.drain()
                fn(stat[:, n, 2, :], stat[:, n, 1, :], ACT.Exp, scale=-0.5).then_inc(s["rinv_n"], 1)

            act.sem_inc(s["proj_taken"], 2)
            act.wait_ge(s["x_in"], 16)
            act.preload_act_table_set("natural_log_exp_and_others")
            norm(0, X, Xn)

            act.wait_ge(s["ba_mm"], 1)
            fn(GB[:, 1, :], PB[6][0:HEADS, 0:SEQ], ACT.Sigmoid)
            fn(gates[:, :, :], PB[7][:, 0:TT * 3 * HEADS].rearrange("p (t n) -> p t n", t=TT), ACT.Sigmoid).then_inc(s["ba_sig"], 1)
            act.preload_act_table_set("natural_log_exp_and_others")
            act.wait_ge(s["sp_lin"], 1)
            fn(g1[:, 2, :], g1[:, 1, :], ACT.Exp, scale=-1.0)
            fn(abias[:, 2:3], abias[:, 0:1], ACT.Exp)
            act.drain()
            fn(g1[:, 3, :], g1[:, 2, :], ACT.Ln, bias=one[0:HEADS, :]).then_inc(s["sp_exp"], 1)
            act.wait_ge(s["gc_ok"], 1)
            fn(TP[:, 2, :], g1[:, 0, :], ACT.Exp)
            fn(g1[:, 2, :], GB[:, 0, :], ACT.Exp).then_inc(s["gc_exp"], 1)
            for h in range(HEADS):
                act.dma_start(GBrow[:, h, :], GB[h:h + 1, :, :].rearrange("p a b -> p (a b)")).then_inc(s["gbrow_in"], 16)

            act.wait_ge(s["pads"], 1)
            act.preload_act_table(ACT.Sigmoid)
            with act.Fori(0, 3) as it:
                for j in range(RING):
                    act.wait_ge(s["proj_done"], 4 * it + (j + 1))
                    act.wait_ge(s["conv_ok"], 4 * it + (j + 1))
                    fn(raw[:, j % 2, :, CONV - 1:], PB[j % 2].rearrange("p (a b) -> p a b", b=SEQ)).then_inc(s["proj_taken"], 1)
                    act.wait_ge(s["conv_ok"], 4 * it + (j + 3))
                    fn(csg[:, j % 2, :], cy[:, j % 2, :], ACT.Sigmoid).then_inc(s["sig_ok"], 1)
            act.preload_act_table_set("natural_log_exp_and_others")
            act.wait_ge(s["mem_in"], 16)
            act.wait_ge(s["tr_n"], 4)
            norm(1, memx, Xn)

            drained = [0]

            def out(goal):
                while PRODUCTS * (drained[0] + 1) <= min(goal, all_goal):
                    n = fillers[drained[0]]
                    act.wait_ge(s["proj_done"], n + 1)
                    if n < N_XKV:
                        i = 2 * (n - N_Z)
                        fn(flat2(big[:, i:i + 2, :]), PB[n % 2]).then_inc(s["proj_taken"], 1)
                    elif n < N_XKV + 2:
                        act.wait_ge(s["qd_ok"], 4)
                        i = 2 * (n - N_XKV)
                        fn(flat2(xkT[:, i:i + 2, :]), PB[n % 2]).then_inc(s["proj_taken"], 1)
                    elif n < N_VS:
                        i = SLOT * (n - N_XKV - 2)
                        fn(xv[:, :, i:i + SLOT], PB[n % 2].rearrange("p (a b) -> p a b", b=SLOT)).then_inc(s["proj_taken"], 1)
                    elif n < N_BA:
                        i = 2 * (n - N_MB)
                        fn(flat2(mb[:, i:i + 2, :]), PB[n % 2]).then_inc(s["proj_taken"], 1)
                    else:
                        i = 2 * (n - N_BA)
                        fn(flat2(yaT[:, i:i + 2, :]), PB[n % 2]).then_inc(s["proj_taken"], 1)
                    drained[0] += 1

            for i in range(HEADS):
                act.wait_ge(s["ss_mm"], i + 1)
                if i >= 2:
                    act.wait_ge(s["qk_ok"], i - 1)
                fn(flat2(lnr[i % 2]), PB[4 + i % 2], ACT.Ln, bias=eps)
                act.drain()
                fn(lnr[i % 2], lnr[i % 2], ACT.Exp, scale=-0.5).then_inc(s["rinv_g"], 1)
                act.wait_ge(s["dd_ok"], i + 1)
                fn(EDm[:, i, :, :], ddh[i % 2], ACT.Exp)
                fn(eG[:, i, :], PB[2 + i % 2][:, P:SEQ], ACT.Exp).then_inc(s["ed_ok"], 1)
                out(table_goal[i])

            def after(b, part):
                if part == 0:
                    act.wait_ge(s["u_mm"], b + 1)
                    fn(flat2(u), PB[5]).then_inc(s["u_ok"], 1)
                elif part == 1:
                    act.wait_ge(s["s_mm"], b + 1)
                    fn(flat2(S1), PB[7][:, 0:SEQ]).then_inc(s["s_ok"], 1)
                elif part == 3:
                    act.wait_ge(s["o_mm"], b + 1)
                    fn(flat2(sqo), PB[5], ACT.Square).then_inc(s["sqo_ok"], 1)
                elif part == 4:
                    act.wait_ge(s["so_mm"], b + 1)
                    fn(flat2(lno), PB[7], ACT.Ln, scale=1.0 / DH, bias=eps)
                    act.drain()
                    fn(lno, lno, ACT.Exp, scale=-0.5).then_inc(s["lno_ok"], 1)

            out(first_goal[1])
            for b in range(HEADS // 2):
                act.wait_ge(s["t0_mm"], b + 1)
                fn(flat2(Tm), PB[2]).then_inc(s["t0_ok"], 1)
                out(start_goal[b])
                for lv in range(1, LEVELS):
                    act.wait_ge(s["m1_mm"], 6 * b + lv)
                    fn(flat2(M1s), PB[2]).then_inc(s["m1_ok"], 1)
                    if b and 2 * lv - 2 < 5:
                        after(b - 1, 2 * lv - 2)
                    out(gap_goal[b][2 * lv - 2])
                    if b and 2 * lv - 1 < 5:
                        after(b - 1, 2 * lv - 1)
                    out(gap_goal[b][2 * lv - 1])
            for part in range(5):
                after(3, part)
                out(tail_goal[part])
            out(delta_goal)

            act.preload_act_table(ACT.Sigmoid)
            act.wait_ge(s["oa_ok"], 4)
            fn(zs, big[:, 0:8, :], ACT.Sigmoid).then_inc(s["zsig"], 1)
            for n in range(N_VS, N_W1):
                act.wait_ge(s["proj_done"], n + 1)
                fn(vtok[:, n - N_VS, :, :].rearrange("p a b -> p (a b)"), PB[n % 2]).then_inc(s["proj_taken"], 1)
            fn(big[:, 24:32, :], big[:, 24:32, :], ACT.Sigmoid)
            for v in range(2):
                act.wait_ge(s["proj_done"], N_W1 + 2 * v + 2)
                fn(s1g[:, v, :], PB[4 + v][:, 0:GROUPS * NCMP], ACT.Sigmoid).then_inc(s["proj_taken"], 2)
            act.preload_act_table_set("natural_log_exp_and_others")
            act.wait_ge(s["w2_mm"], 1)
            fn(ccT, PB[4][:, 0:GROUPS * NCMP])
            fn(vc, PB[4][0:NCMP, 64:64 + KV].rearrange("p (a b) -> p a b", b=DH)).then_inc(s["w2_ok"], 1)
            out(cs_goal)
            act.wait_ge(s["cs_max"], 1)
            fn(sc, sc, ACT.Exp).then_inc(s["cs_exp"], 1)
            for r in range(4):
                act.wait_ge(s["ct_mm"], r + 1)
                fn(PcT[:, 2 * r:2 * r + 2, :].rearrange("p a b -> p (a b)"), PB[6 + r % 2][0:NCMP, :]).then_inc(s["ct_ok"], 1)
                out(ct_goal[r])

            def exps(i):
                st = steps[i]
                act.wait_ge(s["mx_ok"], i + 1)
                w = st["n"] * P
                for h in range(REP):
                    last = fn(st["S"][:, h, 0:w], st["S"][:, h, 0:w], ACT.Exp, bias=smx[:, i % 2, h:h + 1], accum_out=ssum[:, i % 2, h:h + 1])
                last.then_inc(s["ex_ok"], 1)

            def turned(i):
                st = steps[i]
                act.wait_ge(s["tp_mm"], i + 1)
                for kt in range(st["n"]):
                    last = fn(st["PT"][:, kt, :, st["t"] * P:(st["t"] + 1) * P], PB[6 + kt].rearrange("p (a b) -> p a b", b=P))
                last.then_inc(s["tp_taken"], 1)

            exps(0)
            for g in range(GROUPS):
                for j in range(4):
                    i = 4 * g + j
                    if i < 7:
                        exps(i + 1)
                    out(step_goal[i][0])
                    turned(i)
                    out(step_goal[i][1])
                for h in range(0, REP, 2):
                    act.wait_ge(s["pv_mm"], 2 * g + h // 2 + 1)
                    fn(obT[:, g * REP + h:g * REP + h + 2, :].rearrange("p a b -> p (a b)"), PB[6 + h // 2]).then_inc(s["pv_ok"], 1)
            out(all_goal)
            act.preload_act_table(ACT.Sigmoid)
            fn(mb[:, :, :], mb[:, :, :], ACT.Sigmoid).then_inc(s["mb_ok"], 1)
            act.preload_act_table_set("natural_log_exp_and_others")
            act.wait_ge(s["proj_taken"], N_XQ + 2)
            norm(2, X, x2n)
            for n in range(N_XQ, N_XO):
                act.wait_ge(s["proj_done"], n + 1)
                i = 2 * (n - N_XQ)
                fn(xqT[:, i:i + 2, :].rearrange("p a b -> p (a b)"), PB[n % 2]).then_inc(s["proj_taken"], 1)
            exps(8)
            exps(9)
            turned(8)
            turned(9)
            for h in range(0, XH, 2):
                act.wait_ge(s["pv_mm"], 5 + h // 2)
                fn(xoT[:, h:h + 2, :].rearrange("p a b -> p (a b)"), PB[h // 2]).then_inc(s["pv_ok"], 1)
            act.wait_ge(s["proj_taken"], N_END + 2)
            norm(3, X, x3n)
            act.wait_ge(s["lg_sub"], 1)
            fn(gate, lw, ACT.Exp).then_inc(s["lg_exp"], 1)

            def experts(t):
                act.wait_ge(s["pgt_mm"], t + 1)
                fn(PGT.rearrange("p a b c -> p (a b c)"), PB[2]).then_inc(s["pgt_ok"], 1)
                for e in range(2):
                    act.wait_ge(s["act_g"], 2 * t + (e + 1))
                    fn(sg, gg, ACT.Sigmoid, scale=ALPHA).then_inc(s["act_s"], 1)
                    act.wait_ge(s["ht_mm"], 2 * t + (e + 1))
                    fn(hTt.rearrange("p a b -> p (a b)"), PB[2]).then_inc(s["ht_ok"], 1)
                    act.wait_ge(s["dn_used"], 16 * t + 8 * (e + 1))
                    fn(ys, PB[3]).then_inc(s["y_ok"], 1)

            act.preload_act_table(ACT.Sigmoid)
            with act.Fori(0, NE // 2) as t:
                experts(t)
            act.wait_ge(s["pass_ok"], 1)
            many = act.value_load(npass[0:1, 0:1], min_val=0, max_val=SEQ)
            with act.If(many > CAP):
                with act.Fori(NE // 2, PASSES * (NE // 2)) as t:
                    experts(t)
            act.wait_ge(s["fin_acc"], 1)
            norm(4, X, hT[:, :, :].rearrange("p (t k) n -> p t (k n)", t=TT))

        @block.vector
        def _(dve):
            dr = dve.drain

            def tt(out, a0, a1, op):
                return dve.tensor_tensor(out, a0, a1, op)

            def ts(out, a0, s1, op, s2=None, op2=None):
                return dve.tensor_scalar(out, a0, s1, s2, op) if op2 is None else dve.tensor_scalar(out, a0, s1, s2, op, op2)

            def stt(out, a0, sc_, a1, op, op2):
                return dve.scalar_tensor_tensor(out, a0, sc_, a1, op, op2)

            def bc(v, n):
                return v.unsqueeze(len(v.shape)).to_broadcast([*v.shape, n])

            def mid(v, n):
                return v.unsqueeze(1).to_broadcast([v.shape[0], n, *v.shape[1:]])

            def scale_rows(n, src, dst):
                dve.wait_ge(s["rinv_n"], n + 1)
                for t in range(TT):
                    last = ts(dst[:, t, :], src[:, t, :], stat[:, n, 2, t:t + 1], ALU.mult)
                last.then_inc(s["xn_n"], 1)

            def norm_out(n, dst):
                for b in range(4):
                    dve.wait_ge(s["tr_n"], 4 * n + b + 1)
                    gcol = {0: gain(0), 1: gain(2), 2: gain(1), 3: gain(3)}[n]
                    tt(dst[:, 2 * b:2 * b + 2, :], PB[2 + b].rearrange("p (a b) -> p a b", b=SEQ), bc(gcol[:, 2 * b:2 * b + 2], SEQ), ALU.mult).then_inc(s["hT_n"], 1)

            dve.wait_ge(s["cols_tr"], 1)
            dve.tensor_copy(colsA[:, :], PB[0][:, 0:P])
            dve.tensor_copy(colsB[:, :], PB[0][:, P:P + 65])
            scale_rows(0, X, Xn)
            norm_out(0, hT)

            dve.wait_ge(s["ba_sig"], 1)
            dve.wait_ge(s["ab_in"], 32)
            ts(g1[:, 0, :], PB[6][0:HEADS, SEQ:2 * SEQ], abias[:, 1:2], ALU.add)
            dr()
            stt(g1[:, 1, :], g1[:, 0, :], -1.0, g1[:, 0, :], ALU.mult, ALU.max).then_inc(s["sp_lin"], 1)
            dve.wait_ge(s["sp_exp"], 1)
            stt(g1[:, 2, :], g1[:, 0, :], 0.0, g1[:, 3, :], ALU.max, ALU.add)
            dr()
            ts(g1[:, 1, :], g1[:, 2, :], abias[:, 2:3], ALU.mult, -1.0, ALU.mult)
            dr()
            for t in range(TT):
                q = slice(t * P, (t + 1) * P)
                dve.tensor_tensor_scan(GB[:, 0, q], C[0:HEADS, K_ONES:K_ONES + P], g1[:, 1, q], 0.0, ALU.mult, ALU.add)
            dr()
            for t in range(TT):
                q = slice(t * P, (t + 1) * P)
                ts(g1[:, 0, q], GB[:, 0, q], GB[:, 0, (t + 1) * P - 1:(t + 1) * P], ALU.subtract, -1.0, ALU.mult)
            dve.tensor_copy(TP[:, 0, :], GB[:, 1, :])
            dve.tensor_copy(TP[:, 1, :], GB[:, 0, :]).then_inc(s["gc_ok"], 1)
            dve.wait_ge(s["gc_exp"], 1)
            tt(TP[:, 3, :], g1[:, 2, :], GB[:, 1, :], ALU.mult).then_inc(s["tp_ok"], 1)

            dve.sem_inc(s["conv_ok"], 2)
            with dve.Fori(0, 3) as it:
                for j in range(RING):
                    dve.wait_ge(s["proj_taken"], 4 * it + (j + 3))
                    dve.wait_ge(s["mul_ok"], 4 * it + (j + 1))
                    for tap in range(CONV):
                        for i in range(2):
                            y = cy[:, j % 2, i * SEQ:(i + 1) * SEQ]
                            x = raw[:, j % 2, i, tap:tap + SEQ]
                            w = colsA[:, bass.ds(8 * it + (tap * 24 + 2 * j + i), 1)]
                            last = ts(y, x, w, ALU.mult) if tap == 0 else stt(y, x, w, y, ALU.mult, ALU.add)
                        if tap < CONV - 1:
                            dr()
                    last.then_inc(s["conv_ok"], 1)
            dve.wait_ge(s["mem_in"], 16)
            scale_rows(1, memx, Xn)
            norm_out(1, mT)
            dve.wait_ge(s["tp_tr"], 1)
            dve.tensor_copy(TK[:, :, :, :].rearrange("p a b c -> p (a b c)"), PB[6][:, 0:4 * TT * HEADS]).then_inc(s["tk_ok"], 1)

            dr()
            for i in range(HEADS):
                dve.wait_ge(s["bc_mm"], i + 1)
                if i >= 2:
                    dve.wait_ge(s["ed_ok"], i - 1)
                for t in range(TT):
                    last = ts(ddh[i % 2][:, t, :], PB[2 + i % 2][:, t * P:(t + 1) * P], TK[:, 1, t, i:i + 1], ALU.subtract, 0.0, ALU.min)
                last.then_inc(s["dd_ok"], 1)
                dve.wait_ge(s["rinv_g"], i + 1)
                f = flat2(cT[:, 2 * i:2 * i + 2, :])
                if i < 4:
                    stt(f, f, SCALE, flat2(lnr[i % 2]), ALU.mult, ALU.mult).then_inc(s["qk_ok"], 1)
                else:
                    tt(f, f, flat2(lnr[i % 2]), ALU.mult).then_inc(s["qk_ok"], 1)
                dve.wait_ge(s["ed_ok"], i + 1)
                tt(EDm[:, i, :, :], EDm[:, i, :, :], mid(C[:, K_TRIU:K_TRIU + P], TT), ALU.mult)
                dr()
                tt(flat2(EDB[:, i, :, :]), flat2(EDm[:, i, :, :]), PB[2 + i % 2][:, SEQ:2 * SEQ], ALU.mult).then_inc(s["tab_ok"], 1)

            def before(b, part):
                B = b % 2
                e = slice(2 * b, 2 * b + 2)
                if part == 0:
                    dve.wait_ge(s["pre_mm"], b + 1)
                    tt(flat2(AT[B]), EDB[:, e, :, :].rearrange("p a b c -> p (a b c)"), PB[5], ALU.mult)
                    tt(flat2(QKm[B]), EDm[:, e, :, :].rearrange("p a b c -> p (a b c)"), PB[6], ALU.mult).then_inc(s["qkm_ok"], 1)
                elif part == 1:
                    for h in range(2):
                        for t in range(TT):
                            m = 2 * h + t
                            last = ts(kd[B][:, m, :], PB[7][:, m * P:(m + 1) * P], TK[:, 2 + t, t, 2 * b + h:2 * b + h + 1], ALU.mult)
                    last.then_inc(s["kd_ok"], 1)
                elif part == 2:
                    dve.wait_ge(s["vt_mm"], b + 1)
                    for h in range(2):
                        for t in range(TT):
                            m = 2 * h + t
                            last = ts(vb[B][:, m, :], PB[7][:, m * P:(m + 1) * P], TK[:, 0, t, 2 * b + h:2 * b + h + 1], ALU.mult)
                    last.then_inc(s["vb_ok"], 1)
                    tt(dd, AT[B], mid(levels[:, 0:P], 4), ALU.mult)
                elif part == 3:
                    dr()
                    tt(Um[B], mid(ident, 4), dd, ALU.subtract).then_inc(s["u0_ok"], 1)
                elif part == 4:
                    tt(qd[B], cT[:, e, P:SEQ], eG[:, e, :], ALU.mult).then_inc(s["qd_ok"], 1)

            def after(b, part):
                if part == 0:
                    dve.wait_ge(s["u_mm"], b + 1)
                    dve.tensor_copy(flat2(wT), PB[6][:, 0:SEQ]).then_inc(s["w_ok"], 1)
                elif part == 2:
                    dve.wait_ge(s["ws_mm"], b + 1)
                    tt(vn, u[:, 1:4:2, :], PB[6][:, 0:SEQ].rearrange("p (a b) -> p a b", b=P), ALU.subtract).then_inc(s["vn_ok"], 1)
                elif part == 4:
                    dve.wait_ge(s["lno_ok"], b + 1)
                    tt(flat2(oaT[:, 2 * b:2 * b + 2, :]), flat2(lno), PB[5], ALU.mult).then_inc(s["oa_ok"], 1)

            dve.wait_ge(s["lv_in"], 16)
            for part in range(5):
                before(0, part)
            for b in range(HEADS // 2):
                B = b % 2
                for lv in range(1, LEVELS):
                    for half in range(2):
                        gap = 2 * lv - 2 + half
                        if half:
                            dve.wait_ge(s["c_mm"], 6 * b + lv)
                            if lv < LEVELS - 1:
                                tt(flat2(Tm), flat2(Tm), PB[3], ALU.subtract)
                            tt(flat2(Um[B]), flat2(Um[B]), PB[4], ALU.subtract).then_inc(s["tu_ok"], 1)
                        if b and gap < 5:
                            after(b - 1, gap)
                        if b < 3 and gap >= 7:
                            before(b + 1, gap - 7)
            for part in range(5):
                after(3, part)

            dve.wait_ge(s["proj_taken"], N_XKV + 2)
            for v in range(2):
                for g in range(GROUPS):
                    win = big[:, 16 + 2 * v + g, :].rearrange("p (m b) -> p b m", b=CMP_STRIDE)
                    for half in range(2):
                        l = slice(half * CMP_STRIDE, (half + 1) * CMP_STRIDE)
                        pe_cols = colsB[:, CMP_LEN * v + half * CMP_STRIDE:CMP_LEN * v + (half + 1) * CMP_STRIDE]
                        last = tt(blk[:, v, l, g * NCMP:(g + 1) * NCMP], win[:, :, half:half + NCMP], bc(pe_cols, NCMP), ALU.add)
                last.then_inc(s["blk_ok"], 1)
            dve.wait_ge(s["zsig"], 1)
            tt(zs, zs, big[:, 0:8, :], ALU.mult)
            dr()
            stt(flat2(oaT), flat2(oaT), colsB[:, 2 * CMP_LEN:2 * CMP_LEN + 1], flat2(zs), ALU.mult, ALU.mult).then_inc(s["z_ok"], 1)
            for v in range(2):
                dve.wait_ge(s["proj_taken"], N_W1 + 2 * v + 4)
                tt(s1[:, v, :], s1g[:, v, :], PB[4 + v][:, 0:GROUPS * NCMP], ALU.mult).then_inc(s["w1_act"], 1)
            dve.wait_ge(s["qcopy"], 1)
            dve.wait_ge(s["rope_in"], 16)
            cos, sin = R[:, R_COS:R_COS + SEQ], R[:, R_SIN:R_SIN + SEQ]
            for r in range(6):
                i = 8 + 2 * r if r < 4 else 20 + 2 * (r - 4)
                src = big[0:ROT, i:i + 2, :]
                dst = qr[0:ROT, 2 * r:2 * r + 2, :] if r < 4 else src
                dve.wait_ge(s["rope_mm"], r + 1)
                tt(rt1, src, mid(cos, 2), ALU.mult)
                tt(rt2, PB[2 + r % 2][0:ROT, :].rearrange("p (a b) -> p a b", b=SEQ), mid(sin, 2), ALU.mult)
                dr()
                tt(dst, rt1, rt2, ALU.add).then_inc(s["rope_ok"], 1)
                dr()
            dve.wait_ge(s["cs_mm"], 1)
            cps = PB[4][:, 0:TT * HEADS * 16].rearrange("p (t h n) -> p t h n", t=TT, n=16)
            for t in range(TT):
                stt(sc[:, t, :, :], cps[:, t, :, 0:NCMP], SCALE, mid(C[:, K_CMPA + t * NCMP:K_CMPA + (t + 1) * NCMP], HEADS), ALU.mult, ALU.add)
            dr()
            sc2 = sc.rearrange("p t h n -> p (t h) n")
            r1, r2 = small[:, 32:48], small[:, 48:64]
            dve.tensor_reduce(r1, sc2, AX.X, ALU.max)
            dr()
            tt(sc2, sc2, bc(r1, NCMP), ALU.subtract).then_inc(s["cs_max"], 1)
            dve.wait_ge(s["cs_exp"], 1)
            for t in range(TT):
                tt(sc[:, t, :, :], sc[:, t, :, :], mid(C[:, K_CMPM + t * NCMP:K_CMPM + (t + 1) * NCMP], HEADS), ALU.mult)
            dr()
            dve.tensor_reduce(r2, sc2, AX.X, ALU.add)
            dr()
            ts(r2, r2, 1e-30, ALU.max)
            dr()
            dve.reciprocal(r2, r2)
            dr()
            g3 = gates[:, :, :].rearrange("p t (h b) -> p t h b", b=3)
            tt(r2.rearrange("p (t h) -> p t h", t=TT), r2.rearrange("p (t h) -> p t h", t=TT), g3[:, :, :, 0], ALU.mult)
            dr()
            tt(sc2, sc2, bc(r2, NCMP), ALU.mult).then_inc(s["cs_ok"], 1)

            def maxima(i):
                st = steps[i]
                n, w = st["n"], st["n"] * P
                dve.wait_ge(s["sc_mm"], i + 1)
                if i >= 2:
                    dve.wait_ge(s["tp_mm"], i - 1)
                o = 1024 + 2 * (i % 2) * 512
                src = psum[:, o:o + REP * w].rearrange("p (a b) -> p a b", b=w)
                dst = st["S"][:, :, 0:w]
                if i < 8:
                    m = C[:, K_CAUSAL - (n - 1) * P:K_CAUSAL + P]
                    stt(dst, src, SCALE, mid(m, REP), ALU.mult, ALU.add).then_inc(s["sc_read"], 1)
                else:
                    ts(dst, src, SCALE, ALU.mult).then_inc(s["sc_read"], 1)
                dr()
                dve.tensor_reduce(smx[:, i % 2, :], dst, AX.X, ALU.max)
                dr()
                ts(smx[:, i % 2, :], smx[:, i % 2, :], -1.0, ALU.mult).then_inc(s["mx_ok"], 1)

            def weights(i):
                st = steps[i]
                dst = st["S"][:, :, 0:st["n"] * P]
                r = ssum[:, i % 2, :]
                dve.wait_ge(s["ex_ok"], i + 1)
                dve.reciprocal(r, r)
                dr()
                if st["gate"] is not None:
                    tt(r, r, st["gate"][:, :, 0], ALU.mult)
                    dr()
                tt(dst, dst, bc(r, st["n"] * P), ALU.mult).then_inc(s["pn_ok"], 1)

            maxima(0)
            for i in range(8):
                if i < 7:
                    maxima(i + 1)
                weights(i)
            dve.wait_ge(s["mb_ok"], 1)
            tt(yaT, yaT, big[:, 24:32, :], ALU.mult)
            dve.wait_ge(s["proj_taken"], N_BB + 2)
            for n in range(N_BB, N_MIX):
                f = slice(2 * (n - N_BB), 2 * (n - N_BB) + 2)
                dve.wait_ge(s["proj_done"], n + 1)
                tt(flat2(mixT[:, f, :]), flat2(mb[:, f, :]), PB[n % 2], ALU.mult).then_inc(s["proj_taken"], 1)
                dr()
                tt(mixT[:, f, :], mixT[:, f, :], yaT[:, f, :], ALU.add).then_inc(s["mixed"], 1)

            def residual(n0, n1):
                for n in range(n0, n1):
                    dve.wait_ge(s["proj_done"], n + 1)
                    v = X[:, :, (n - n0) * SLOT:(n - n0 + 1) * SLOT]
                    tt(v, v, PB[n % 2].rearrange("p (a b) -> p a b", b=SLOT), ALU.add).then_inc(s["proj_taken"], 1)

            residual(N_MIX, N_XQ)
            scale_rows(2, X, x2n)
            norm_out(2, hT)
            maxima(8)
            maxima(9)
            weights(8)
            weights(9)
            residual(N_XO, N_END)
            scale_rows(3, X, x3n)
            norm_out(3, hT)

            dve.wait_ge(s["lg_mm"], 1)
            lps = PB[0][:, 0:TT * NE].rearrange("p (a b) -> p a b", b=NE)
            dve.tensor_copy(lg, lps)
            dve.tensor_copy(lw, lps)
            dve.memset(msk, 0.0)
            dr()
            for r in range(TOPK):
                dve.tensor_reduce(mx, lw, AX.X, ALU.max)
                dr()
                if r == 0:
                    dve.tensor_copy(m1, mx)
                tt(eqm, lw, bc(mx, NE), ALU.is_equal)
                dr()
                stt(cand, eqm, -1024.0, mid(C[:, K_E:K_E + NE], TT), ALU.mult, ALU.add)
                dr()
                dve.tensor_reduce(rsum, cand, AX.X, ALU.min)
                dr()
                tt(oh, cand, bc(rsum, NE), ALU.is_equal)
                dr()
                tt(msk, msk, oh, ALU.add)
                stt(lw, oh, -3e38, lw, ALU.mult, ALU.add)
                dr()
            tt(lw, lg, bc(m1, NE), ALU.subtract).then_inc(s["lg_sub"], 1)
            dr().then_inc(s["lg_ok"], 1)
            dve.wait_ge(s["lg_exp"], 1)
            tt(gate, gate, msk, ALU.mult)
            dr()
            dve.tensor_reduce(rsum, gate, AX.X, ALU.add)
            dr()
            dve.reciprocal(rsum, rsum)
            dr()
            tt(gate, gate, bc(rsum, NE), ALU.mult)
            dve.wait_ge(s["rk_mm"], 1)
            stt(cand.rearrange("p a b -> p (a b)"), PB[1][:, 0:TT * NE], 1.0, msk.rearrange("p a b -> p (a b)"), ALU.add, ALU.mult)
            dve.tensor_reduce(cmax[0:1, :], PB[1][0:1, 2 * NE:3 * NE], AX.X, ALU.max)
            dve.memset(rankT[:, PASSES * NE:, :], -1.0)
            dve.memset(gateT[:, PASSES * NE:, :], 0.0)
            dve.memset(selT[:, PASSES * NE:], 0.0)
            dr()
            dve.tensor_copy(npass[0:1, 0:1], cmax[0:1, :]).then_inc(s["pass_ok"], 1)
            for p in range(PASSES):
                e = slice(p * NE, (p + 1) * NE)
                ts(rankT[:, e, :].rearrange("p e t -> p t e"), cand, float(1 + p * CAP), ALU.subtract)
                dve.tensor_copy(gateT[:, e, :].rearrange("p e t -> p t e"), gate)
                dve.tensor_copy(selT[:, e], C[:, K_SEL:K_SEL + NE])
            dr()

            def one_hot(t):
                for e in range(2):
                    for k in range(TT):
                        r, g = rankT[:, bass.ds(2 * t + e, 1), k], gateT[:, bass.ds(2 * t + e, 1), k]
                        ts(Pg[:, k, e, :], C[:, K_IOTA:K_IOTA + CAP], r, ALU.is_equal)
                        last = ts(PGd[:, e, k, :], C[:, K_IOTA:K_IOTA + P], r, ALU.is_equal, g, ALU.mult)
                last.then_inc(s["pg_ok"], 1)

            def selectors(t):
                for e in range(2):
                    last = dve.tensor_copy(bselv[0:B3, e * CAP:(e + 1) * CAP], selT[0:B3, bass.ds(2 * t + e, 1)].to_broadcast([B3, CAP]))
                last.then_inc(s["bsel_ok"], 1)

            def tokens(t):
                dve.wait_ge(s["gat_mm"], t + 1)
                g = gain(3)
                for i in range(2):
                    last = tt(xg[:, 4 * i:4 * i + 4, :, :].rearrange("p k e c -> p k (e c)"), PB[4 + i].rearrange("p (a b) -> p a b", b=P), bc(g[:, 4 * i:4 * i + 4], P), ALU.mult)
                last.then_inc(s["xg_ok"], 1)

            def swiglu(t, e):
                dve.wait_ge(s["gu_used"], 16 * t + 8 * (e + 1))
                ts(gg, PB[0], LIMIT, ALU.min).then_inc(s["act_g"], 1)
                ts(uu, PB[1], LIMIT, ALU.min, -LIMIT, ALU.max).then_inc(s["gu_taken"], 1)
                dr()
                stt(uu, uu, 1.0, gg, ALU.add, ALU.mult)
                dr()
                dve.wait_ge(s["act_s"], 2 * t + (e + 1))
                tt(hh, uu, sg, ALU.mult).then_inc(s["h_ok"], 1)

            def add_up(t, e):
                dve.wait_ge(s["scat"], 2 * t + (e + 1))
                for k in range(TT):
                    last = tt(X[:, k, :], X[:, k, :], psum[:, (4 + 2 * k) * 512:(6 + 2 * k) * 512], ALU.add)
                last.then_inc(s["acc_ok"], 1)

            def experts(t):
                swiglu(t, 0)
                add_up(t, 0)
                dve.wait_ge(s["gat_mm"], t + 1)
                dve.wait_ge(s["pgt_mm"], t + 1)
                one_hot(t + 1)
                swiglu(t, 1)
                tokens(t + 1)
                dve.wait_ge(s["dn_used"], 16 * t + 16)
                selectors(t + 1)
                add_up(t, 1)

            dve.sem_inc(s["gu_taken"], 1)
            dve.sem_inc(s["acc_ok"], 1)
            one_hot(0)
            selectors(0)
            tokens(0)
            with dve.Fori(0, NE // 2) as t:
                experts(t)
            dve.wait_ge(s["pass_ok"], 1)
            many = dve.value_load(npass[0:1, 0:1], min_val=0, max_val=SEQ)
            with dve.If(many > CAP):
                with dve.Fori(NE // 2, PASSES * (NE // 2)) as t:
                    experts(t)
            dr().then_inc(s["fin_acc"], 1)
            dve.wait_ge(s["rinv_n"], 5)
            dve.wait_ge(s["fg_in"], 16)
            for t in range(TT):
                last = stt(X[:, t, :], X[:, t, :], stat[:, 4, 2, t:t + 1], fgb, ALU.mult, ALU.mult)
            last.then_inc(s["fin_ok"], 1)

        @block.gpsimd
        def _(pool):
            def tt(out, a0, a1, op=ALU.mult):
                return pool.tensor_tensor(out, a0, a1, op)

            for n, src in ((0, "gdn_conv_w"), *enumerate(("attn_norm_g", "xattn_norm_g", "mem_norm_g", "ffn_norm_g"), 1)):
                r0, r1 = (0, CONV * 24) if n == 0 else (CONV * 24 + 8 * n - 8, CONV * 24 + 8 * n)
                v = a[src].rearrange("t (c d) -> (t c) d", d=P)
                pool.dma_start(rowsA[r0:r1, :], v).then_inc(s["rows_in"], 16)
            pool.dma_start(rowsB[0:32, :], a["cmp_pe_k"]).then_inc(s["rows_in"], 16)
            pool.dma_start(rowsB[32:64, :], a["cmp_pe_v"]).then_inc(s["rows_in"], 16)
            pool.dma_start(rowsB[64:65, :], a["gdn_norm_g"]).then_inc(s["rows_in"], 16)
            pool.dma_start(w_ba, cols(w_in, C_B, n=2 * HEADS)).then_inc(s["wba_in"], 16)
            pool.dma_start(w_ng, cols(w_in, C_NG, n=3 * HEADS)).then_inc(s["wba_in"], 16)
            pool.dma_start(abias[:, 0:1], a["gdn_a_log"].rearrange("o h -> h o")).then_inc(s["ab_in"], 16)
            pool.dma_start(abias[:, 1:2], a["gdn_dt_bias"].rearrange("o h -> h o")).then_inc(s["ab_in"], 16)
            pool.sem_inc(s["mul_ok"], 2)
            pool.memset(raw, 0.0).then_inc(s["pads"], 1)
            with pool.Fori(0, 3) as it:
                for j in range(RING):
                    pool.wait_ge(s["sig_ok"], 4 * it + (j + 1))
                    tt(cT[:, bass.ds(8 * it + 2 * j, 2), :].rearrange("p a b -> p (a b)"), cy[:, j % 2, :], csg[:, j % 2, :]).then_inc(s["mul_ok"], 1)
            pool.drain()
            for i in range(HEADS):
                if i >= 2:
                    pool.wait_ge(s["ss_mm"], i - 1)
                f = flat2(cT[:, 2 * i:2 * i + 2, :])
                tt(flat2(sq[i % 2]), f, f).then_inc(s["sq_ok"], 1)
            pool.wait_ge(s["lv_in"], 16)
            for b in range(HEADS // 2):
                pool.wait_ge(s["u0_ok"], b + 1)
                for lv in range(1, LEVELS):
                    if lv > 1 or b:
                        pool.wait_ge(s["m1_mm"], 6 * b + lv - 1)
                    m = levels[:, lv * P:(lv + 1) * P]
                    tt(LT, AT[b % 2], m.unsqueeze(1).to_broadcast([P, 4, P])).then_inc(s["lt_ok"], 1)
            pool.wait_ge(s["oa_ok"], 4)
            pool.wait_ge(s["proj_taken"], N_XKV + 2)
            pool.tensor_copy(qr, big[:, 8:16, :]).then_inc(s["qcopy"], 1)
            pool.wait_ge(s["w1_act"], 2)
            for c in range(3):
                src = a["b_gate_up"][:, c * D:(c + 1) * D] if c < 2 else a["b_down"]
                bs = bspl[:, c * D:(c + 1) * D]
                for i in range(3):
                    pool.dma_start(btmp[i * NE:(i + 1) * NE, :], src).then_inc(s["bias_in"], 16)
                pool.wait_ge(s["bias_in"], 48 * (c + 1))
                pool.tensor_copy(bs, btmp)
                pool.drain()
                tt(btmp, btmp, bs, ALU.subtract)
                pool.drain()
                pool.tensor_copy(bmid, btmp)
                pool.drain()
                tt(btmp, btmp, bmid, ALU.subtract)
                pool.drain()
                pool.tensor_copy(bs[NE:2 * NE, :], bmid[NE:2 * NE, :])
                pool.drain()
                pool.tensor_copy(bs[2 * NE:3 * NE, :], btmp[2 * NE:3 * NE, :])
                pool.drain()
            pool.drain().then_inc(s["prep_ok"], 1)


_DEPTH = ["attn_norm_g", "w_in", "gdn_conv_w", "gdn_a_log", "gdn_dt_bias", "gdn_norm_g", "cmp_pe_k", "cmp_w1_k",
          "cmp_w2_k", "cmp_pe_v", "cmp_w1_v", "cmp_w2_v", "w_branch_a", "w_branch_b", "w_mix_out", "xattn_norm_g",
          "mem_norm_g", "xattn_w_q", "xattn_w_kv", "xattn_w_o", "ffn_norm_g", "router_w", "router_b", "w_gate_up",
          "b_gate_up", "w_down", "b_down"]
_ROWS = ("attn_norm_g", "xattn_norm_g", "mem_norm_g", "ffn_norm_g", "gdn_a_log", "gdn_dt_bias", "gdn_norm_g", "router_b")


def kernel(**inputs):
    import concourse.bacc as bacc
    from concourse.bass_utils import run_bass_kernel_spmd

    nc = bacc.Bacc("TRN2", target_bir_lowering=False, num_devices=1)
    arrays = {}
    for name in ["x", "mem", "final_norm_g"] + _DEPTH:
        v = np.ascontiguousarray(inputs[name])
        arrays[name] = v[0] if name in _DEPTH and name not in _ROWS else v
    arrays["tab"], arrays["levels"], arrays["rope"] = constants()
    aps = {n: nc.dram_tensor("in_" + n, v.shape, mybir.dt.from_np(v.dtype), kind="ExternalInput").ap() for n, v in arrays.items()}
    aps["out"] = nc.dram_tensor("out", (1, SEQ, D), mybir.dt.float32, kind="ExternalOutput").ap()
    build(nc, aps)
    r = run_bass_kernel_spmd(nc, [{"in_" + n: v for n, v in arrays.items()}], core_ids=[0])
    return r.results[0]["out"]
```

```python
import math

import numpy as np
import concourse.bass as bass
from concourse import mybir
from contextlib import ExitStack

P = 128
D = 1024
KT = D // P
SEQ = 256
TT = SEQ // P
HEADS = 8
GROUPS = 2
REP = HEADS // GROUPS
DH = 128
CONV = 4
ROT = 32
CMP_LEN, CMP_STRIDE = 32, 16
NCMP = (SEQ - CMP_LEN) // CMP_STRIDE + 1
XH = 4
NE = 32
TOPK = 4
CAP = 64
EPS = 1e-6
NEG = -1e30
LIMIT, ALPHA = 7.0, 1.702
WARM_FIRST, WARM_STEP = 12, (4, 4)
LEVELS = 7
SCALE = DH ** -0.5

C_B = 4 * D
C_NQ = C_B + 2 * HEADS
C_KC = C_NQ + D
KV = GROUPS * DH
C_VC, C_KS, C_VS, C_KW, C_VW = (C_KC + KV * i for i in range(1, 6))
C_NG = C_KC + 6 * KV
C_MA = C_NG + 3 * HEADS
C_MB = C_MA + D

K_ID, K_TRIU, K_STRICT, K_ONES, K_ZERO, K_CAUSAL, K_IOTA, K_CMPA = (P * i for i in range(8))
K_CMPM = K_CMPA + TT * NCMP
K_E = K_CMPM + TT * NCMP
K_SEL = K_E + NE
K_EPS = K_SEL + NE
NK = K_EPS + 1
R_ROT, R_COS, R_SIN = 0, ROT, ROT + SEQ
NR = ROT + 2 * SEQ

SLOT = 256
RING = 4


def constants():
    c = np.zeros((P, NK), np.float32)
    j, i = np.meshgrid(np.arange(P), np.arange(P), indexing="ij")
    c[:, K_ID:K_ID + P] = j == i
    c[:, K_TRIU:K_TRIU + P] = j <= i
    c[:, K_STRICT:K_STRICT + P] = j < i
    c[:, K_ONES:K_ONES + P] = 1
    c[:, K_CAUSAL:K_CAUSAL + P] = np.where(i <= j, 0, NEG)
    c[:, K_IOTA:K_IOTA + P] = i % CAP
    lv = np.zeros((P, LEVELS * P), np.float32)
    for n in range(LEVELS):
        s = 1 << n
        lv[:, n * P:(n + 1) * P] = (j // (2 * s) == i // (2 * s)) & (j // s % 2 == 0) & (i // s % 2 == 1)
    for t in range(TT):
        q = t * P + np.arange(P)[:, None]
        ok = np.arange(NCMP)[None] * CMP_STRIDE + CMP_LEN - 1 <= q
        c[:, K_CMPA + t * NCMP:K_CMPA + (t + 1) * NCMP] = np.where(ok, 0, NEG)
        c[:, K_CMPM + t * NCMP:K_CMPM + (t + 1) * NCMP] = ok
    c[:, K_E:K_E + NE] = np.arange(NE)
    c[:, K_SEL:K_SEL + NE] = np.arange(P)[:, None] % NE == np.arange(NE)
    c[:, K_EPS] = EPS
    r = np.zeros((ROT, NR), np.float32)
    half = ROT // 2
    for m in range(half):
        r[m + half, R_ROT + m] = -1
        r[m, R_ROT + m + half] = 1
    freq = np.exp(np.float32(-math.log(500000.0)) * np.arange(half, dtype=np.float32) * np.float32(2.0 / ROT))
    ang = np.arange(SEQ, dtype=np.float32)[None] * freq[:, None].astype(np.float32)
    r[:, R_COS:R_COS + SEQ] = np.tile(np.cos(ang), (2, 1))
    r[:, R_SIN:R_SIN + SEQ] = np.tile(np.sin(ang), (2, 1))
    return c, lv, r


def build(nc, a):
    f32, bf16, i32 = mybir.dt.float32, mybir.dt.bfloat16, mybir.dt.int32
    ALU, ACT, AX = mybir.AluOpType, mybir.ActivationFunctionType, mybir.AxisListType

    def cols(w, c0, k=KT, n=SLOT):
        return w[:, c0:c0 + n].rearrange("(k p) n -> p k n", p=P)

    w_in = a["w_in"]
    chunks = [cols(w_in, c) for c in range(0, 4 * D, SLOT)]
    chunks += [cols(w_in, C_NQ + c) for c in range(0, D, SLOT)]
    chunks += [cols(w_in, c) for c in (C_KC, C_VC, C_KS, C_KW)]
    chunks += [cols(w_in, C_MA + c) for c in range(0, D, SLOT)]
    N_XKV = len(chunks)
    chunks += [cols(a["xattn_w_kv"], c) for c in range(0, 2 * XH * DH, SLOT)]
    N_VS = len(chunks)
    w1 = []
    for w in (a["cmp_w1_k"], a["cmp_w1_v"]):
        v = w.rearrange("(l d) f -> d l f", d=DH)
        w1 += [v[:, l:l + CMP_LEN // 2, :] for l in (0, CMP_LEN // 2)]
    w_mb = [cols(w_in, C_MB + c) for c in range(0, D, SLOT)]
    chunks += [w1[0], cols(w_in, C_VS), w1[1], cols(w_in, C_VW), w1[2], w_mb[0], w1[3], *w_mb[1:]]
    W1_AT, V_AT, MB_AT = ([N_VS + i for i in l] for l in ((0, 2, 4, 6), (1, 3), (5, 7, 8, 9)))
    N_BA = len(chunks)
    chunks += [cols(a["w_branch_a"], c) for c in range(0, D, SLOT)]
    N_BB = len(chunks)
    chunks += [cols(a["w_branch_b"], c) for c in range(0, D, SLOT)]
    N_MIX = len(chunks)
    chunks += [cols(a["w_mix_out"], c) for c in range(0, D, SLOT)]
    N_XQ = len(chunks)
    chunks += [cols(a["xattn_w_q"], c) for c in range(0, XH * DH, SLOT)]
    N_XO = len(chunks)
    chunks += [cols(a["xattn_w_o"], c) for c in range(0, D, SLOT)]
    N_END = len(chunks)
    GU_BEFORE, DN_BEFORE = N_XQ, N_XO + 2

    N_Z = 4 * D // SLOT - 4
    fillers = [*range(N_Z, N_VS), *MB_AT, *range(N_BA, N_BB)]
    PRODUCTS = 2 * KT
    lead_goal = PRODUCTS
    table_goal = [lead_goal + 7 * (i + 1) for i in range(HEADS)]
    first_goal = [table_goal[-1] + 6, table_goal[-1] + 12]
    start_goal = [first_goal[1] + 50 * b + 2 for b in range(HEADS // 2)]
    gap_goal = [[start_goal[b] + 8 * (g // 2) + (3, 8)[g % 2] for g in range(2 * LEVELS - 2)] for b in range(HEADS // 2)]
    tail_goal = [gap_goal[-1][-1] + 6 * (i + 1) for i in range(5)]
    delta_goal = PRODUCTS * (N_VS - N_Z)
    mb_goal = delta_goal + PRODUCTS
    w1_goal, w2_goal = mb_goal + PRODUCTS + 4, mb_goal + PRODUCTS + 8
    cs_goal = w2_goal + 14
    ct_goal = [cs_goal + 2 * (i + 1) for i in range(4)]
    step_goal = [[ct_goal[-1] + 8 * i + 6, ct_goal[-1] + 8 * i + 8] for i in range(8)]
    all_goal = PRODUCTS * len(fillers)

    ctx = ExitStack()
    with ctx:
        def sb(name, shape, dt=f32):
            return ctx.enter_context(nc.sbuf_tensor(name, shape, dt))

        def sem(name):
            return ctx.enter_context(nc.semaphore(name))

        EXPERT = KT * 2 * D + KT * D
        early = sb("early", [P, EXPERT])
        at = {"early": 0, "mid": 0}

        def part(region, name, *dims, rows=P):
            n = int(np.prod(dims))
            o = at[name]
            at[name] = o + n
            v = region[0:rows, o:o + n]
            if len(dims) == 2:
                v = v.rearrange("p (a b) -> p a b", b=dims[1])
            elif len(dims) == 3:
                v = v.rearrange("p (a b c) -> p a b c", b=dims[1], c=dims[2])
            return v

        def E(*dims, rows=P):
            return part(early, "early", *dims, rows=rows)

        X = sb("X", [P, TT, D])
        hT = sb("hT", [P, KT, SEQ])
        C = sb("C", [P, NK])
        R = sb("R", [ROT, NR])
        ring = sb("ring", [P, RING, KT * SLOT])
        big = sb("big", [P, 32, SEQ])
        mb = sb("mb", [P, KT, SEQ])
        xkT = sb("xkT", [P, XH, SEQ])
        xv = sb("xv", [P, TT, XH * DH])
        colsA = sb("colsA", [P, P])
        colsB = sb("colsB", [P, 2 * CMP_LEN + 1])
        bspl = sb("bspl", [3 * NE, 3 * D], bf16)[:, :]
        w_rt = sb("w_rt", [P, KT, NE])
        TK = sb("TK", [P, 4, TT, HEADS])
        gates = sb("gates", [P, TT, 3 * HEADS])
        stat = sb("stat", [P, 5, 3, TT])
        small = sb("small", [P, 96])

        levels = mb[:, :, :].rearrange("p a b -> p (a b)")[:, 0:LEVELS * P]
        zeros = mb[:, KT - 1, :]
        eG = xkT[:, :, :].rearrange("p a b -> p (a b)").rearrange("p (h n) -> p h n", n=P)
        xvf = xv[:, :, :].rearrange("p a b -> p (a b)")
        w_bn = xvf[:, 0:KT * 5 * HEADS].rearrange("p (k n) -> p k n", k=KT)
        ba = small[:, 0:2 * TT * HEADS].rearrange("p (t n) -> p t n", t=TT)

        STAGE = 2 * P + 2 * TT * D
        MT_END = STAGE + KT * SEQ
        CT_END = MT_END + 3 * HEADS * SEQ
        OA = EXPERT - HEADS * SEQ
        rowsA, rowsB, memx, Xn = E(P), E(P), E(TT, D), E(TT, D)
        mT = E(KT, SEQ)
        cT = E(3 * HEADS, SEQ)
        assert at["early"] == CT_END
        raw = E(2, 2, SEQ + CONV - 1)
        cy, csg = E(2, 2 * SEQ), E(2, 2 * SEQ)
        GB = E(2, SEQ, rows=HEADS)
        TP = E(4, SEQ, rows=HEADS)
        g1 = E(4, SEQ, rows=HEADS)
        abias = E(4, rows=HEADS)
        at["early"] = 0
        EDm, EDB = E(HEADS, TT, P), E(HEADS, TT, P)
        assert at["early"] <= STAGE
        at["early"] = CT_END
        QKm, AT, kd, vb, Um = ([E(4, P) for _ in range(2)] for _ in range(5))
        qd = [E(2, P) for _ in range(2)]
        LT, M1s, Tm, dd, u, sqo, lno = (E(4, P) for _ in range(7))
        wT, S1, vn = E(2, P), E(2, P), E(2, P)
        assert at["early"] <= OA
        sq, lnr, ddh = QKm, AT, [kd[0][:, 2 * i:2 * i + 2, :] for i in range(2)]
        at["early"] = OA - HEADS * 2 * SEQ - 16
        G3 = E(HEADS * SEQ, rows=3).bitcast(bf16).rearrange("p (h n) -> p h n", h=HEADS)
        Gp = E(3 * SEQ, rows=HEADS).bitcast(bf16).rearrange("p (i n) -> p i n", i=3)
        Gr = E(2 * SEQ, rows=HEADS)
        ones3 = E(P // 2, rows=3).bitcast(bf16)
        assert at["early"] <= OA
        at["early"] = OA
        oaT = E(HEADS, SEQ)
        at["early"] = 0
        obT = E(HEADS, SEQ)
        qr = E(HEADS, SEQ)
        assert at["early"] <= STAGE
        at["early"] = MT_END
        vtok = E(2, TT, KV)
        blk = E(2, CMP_LEN, GROUPS * NCMP)
        S = [E(REP, SEQ) for _ in range(2)]
        PT = [E(TT, REP, SEQ) for _ in range(2)]
        PcT = E(HEADS, SEQ, rows=NCMP)
        w2 = E(2, DH)
        ccT = E(GROUPS * NCMP)
        vc = E(GROUPS, DH, rows=NCMP)
        s1, s1g = E(2, GROUPS * NCMP), E(2, GROUPS * NCMP)
        sc = E(TT, HEADS, NCMP)
        rt1, rt2 = E(2, SEQ, rows=ROT), E(2, SEQ, rows=ROT)
        zs = E(HEADS, SEQ)
        assert at["early"] <= OA

        yaT, mixT = big[:, 8:16, :], big[:, 16:24, :]

        def tiles(i, *dims):
            v = big[:, i:i + 8, :].rearrange("p a b -> p (a b)")
            return v.rearrange("p (a b) -> p a b", b=dims[-1]) if len(dims) == 2 else v.rearrange("p (a b c) -> p a b c", b=dims[1], c=dims[2])
        x2n = tiles(0, TT, D)
        S2 = [big[:, 8 + 4 * i:12 + 4 * i, :] for i in range(2)]
        PTx = tiles(16, TT, XH, SEQ)
        xqT, xoT = big[:, 24:28, :], big[:, 28:32, :]

        names = """zeros_ok gsplit x1_in rows1_in c_in rope_in rows_in x_in mem_in wba_in ab_in w2_in rt_in gbrow_in bias_in fg_in out_out
        cols_tr rinv_n xn_n tr_n hT_n
        res_mm res_ok ba_mm ba_ok ba_tr ba_sig sp_lin sp_exp gc_ok gc_exp tp_ok tp_tr pads
        proj_done proj_taken conv_ok sig_ok mul_ok
        lv_in sq_ok ss_mm rinv_g qk_ok bc_mm dd_ok ed_ok tab_ok pre_mm qkm_ok kd_ok vt_mm vb_ok u0_ok qd_ok t0_mm t0_ok lt_ok m1_mm m1_ok c_mm tu_ok
        u_mm u_ok w_ok s_mm s_ok ws_mm vn_ok o_mm sqo_ok so_mm lno_ok oa_ok
        blk_ok w1_act w2_mm w2_ok qcopy rope_mm rope_ok
        sc_mm sc_read mx_ok ex_ok pn_ok tp_mm tp_taken cs_mm cs_max cs_exp cs_ok ct_mm ct_ok pv_mm pv_ok
        zsig z_ok mb_ok mixed
        lg_mm lg_sub lg_exp lg_ok rk_mm pass_ok prep_ok
        pg_ok pgd_ok gat_mm xg_ok pgt_mm pgt_ok gu_taken act_g act_s h_ok ht_mm ht_ok y_ok scat acc_ok gu_used dn_used
        bsel_ok fin_acc fin_ok""".split()
        s = {n: sem(n) for n in names}
        ring_in = [sem(f"ring_in{i}") for i in range(RING)]
        gu_in = [sem(f"gu_in{k}") for k in range(KT)]
        dn_in = [sem(f"dn_in{k}") for k in range(KT)]
        pre_g_in = [sem(f"pre_g_in{k}") for k in range(4)]
        pre_d_in = [sem(f"pre_d_in{k}") for k in range(3)]
        psum = ctx.enter_context(nc.psum_tensor("psum", [P, 8 * 512], f32))
        PB = [psum[:, 512 * i:512 * (i + 1)] for i in range(8)]

        def flat2(v):
            return v.rearrange("p a b -> p (a b)")

        ident = C[:, K_ID:K_ID + P]
        ones = C[:, K_ONES:K_ONES + P]
        eps = C[:, K_EPS:K_EPS + 1]
        one = C[:, K_ONES:K_ONES + 1]

        def gain(n):
            return colsA[:, CONV * 24 + 8 * n:CONV * 24 + 8 * n + 8]

        def rw(slot):
            return ring[:, slot, :].rearrange("p (k n) -> p k n", k=KT)

        flat = big[:, :, :].rearrange("p a b -> p (a b)")

        def M(*dims, rows=P):
            return part(flat, "mid", *dims, rows=rows)
        x3n = M(TT, D)
        xg = M(KT, 2, CAP)
        Pg = M(TT, 2, CAP)
        PGd = M(2, TT, P)
        PGT = M(2, TT, P)
        gg, uu, sg, hh = M(512), M(512), M(512), M(512)
        hTt = M(4, P)
        ys = M(512)
        bselb = M(CAP)
        assert at["mid"] <= 32 * SEQ
        rflat = ring[:, :, :].rearrange("p a b -> p (a b)")
        B3 = 3 * NE
        bt0 = MT_END + 2 * TT * KV
        btmp, bmid = early[0:B3, bt0:bt0 + D], early[0:B3, bt0 + D:bt0 + D + D // 2].bitcast(bf16)
        hTf, xkf = hT[:, :, :].rearrange("p a b -> p (a b)"), xkT[:, :, :].rearrange("p a b -> p (a b)")
        pre_g = [rflat[:, 2 * D * i:2 * D * (i + 1)] for i in range(3)] + [hTf]
        pre_d = [rflat[:, 6 * D:7 * D], xkf, xvf]
        fgb = rflat[:, 7 * D:8 * D]
        bselv = bselb.bitcast(bf16)
        rb = small[0:1, 0:NE]
        mbf = mb[:, :, :].rearrange("p a b -> p (a b)")
        at["rt"] = 0

        def RT(*dims):
            return part(mbf, "rt", *dims)
        PASSES = SEQ // CAP
        NT = PASSES * NE + 2
        lg, lw, msk, cand, gate = (RT(TT, NE) for _ in range(5))
        lwp, left = RT(TT, NE + 4), RT(TT, NE + 4)
        top = RT(TT, 8)
        rankT, gateT = RT(NT, TT), RT(NT, TT)
        selT = RT(NT)
        rsum = RT(TT)
        cmax = RT(1)
        npass = sb("npass", [1, 1], i32)

        wg = early[:, 0:KT * 2 * D].rearrange("p (k n) -> p k n", k=KT)
        wd = early[:, KT * 2 * D:EXPERT].rearrange("p (k n) -> p k n", k=KT)

        def sparse_step(i):
            g, br, t = i // 4, i // 2 % 2, i % 2
            return dict(q=lambda h: qr[:, g * REP + h, t * P:(t + 1) * P], k=lambda h: big[:, 20 + 2 * br + g, :],
                        n=t + 1, S=S[i % 2], PT=lambda kt: PT[br][:, kt, :, t * P:(t + 1) * P], gate=gates[:, t, :].rearrange("p (h b) -> p h b", b=3)[:, g * REP:(g + 1) * REP, 1 + br:2 + br])

        def memory_step(j):
            return dict(q=lambda m: xqT[:, 2 * j + m // 2, m % 2 * P:(m % 2 + 1) * P], k=lambda m: xkT[:, 2 * j + m // 2, :],
                        n=TT, S=S2[j], PT=lambda kt: PTx[:, kt, 2 * j:2 * j + 2, :].rearrange("p h (t n) -> p (h t) n", n=P), gate=None)
        steps = [sparse_step(i) for i in range(8)] + [memory_step(t) for t in range(2)]
        smx, ssum = small[:, 64:72].rearrange("p (a b) -> p a b", a=2), small[:, 72:80].rearrange("p (a b) -> p a b", a=2)

        block = ctx.enter_context(nc.Block())

        def gains_in(eng, names, landed):
            for n, src in enumerate(("gdn_conv_w", "attn_norm_g", "xattn_norm_g", "mem_norm_g", "ffn_norm_g")):
                r0, r1 = (0, CONV * 24) if n == 0 else (CONV * 24 + 8 * n - 8, CONV * 24 + 8 * n)
                if src in names:
                    eng.dma_start(rowsA[r0:r1, :], a[src].rearrange("t (c d) -> (t c) d", d=P)).then_inc(landed, 16)

        @block.sync
        def _(sp):
            for t in range(TT):
                sp.dma_start(X[:, t, :], a["x"][0, t * P:(t + 1) * P, :]).then_inc(s[("x_in", "x1_in")[t]], 16)
                if t == 0:
                    sp.dma_start(C[:, :], a["tab"]).then_inc(s["c_in"], 16)
            gains_in(sp, ("mem_norm_g", "ffn_norm_g"), s["rows1_in"])
            sp.dma_start(rowsB[64:65, :], a["gdn_norm_g"]).then_inc(s["rows1_in"], 16)
            for n, src in enumerate(chunks):
                if n == 1:
                    sp.wait_ge(s["rows_in"], 16 * 5)
                    sp.wait_ge(s["wba_in"], 32)
                if n == 2:
                    sp.dma_start(memx, a["mem"].rearrange("o (t p) d -> p (o t) d", p=P)).then_inc(s["mem_in"], 16)
                if n == GU_BEFORE:
                    sp.wait_ge(s["pv_ok"], 4)
                    sp.wait_ge(s["prep_ok"], 1)
                    sp.wait_ge(s["mixed"], 4)
                    for k in range(KT):
                        sp.dma_start(wg[:, k, :], a["w_gate_up"][0, k * P:(k + 1) * P, :]).then_inc(gu_in[k], 16)
                if n == DN_BEFORE:
                    for k in range(KT):
                        sp.dma_start(wd[:, k, :], a["w_down"][0, k * P:(k + 1) * P, :]).then_inc(dn_in[k], 16)
                if n >= RING:
                    sp.wait_ge(s["proj_done"], n - RING + 1)
                k = src.shape[1]
                dst = ring[:, n % RING, 0:k * src.shape[2]].rearrange("p (k n) -> p k n", k=k)
                sp.dma_start(dst, src).then_inc(ring_in[n % RING], 16)
                if n == RING:
                    sp.dma_start(levels, a["levels"]).then_inc(s["lv_in"], 16)
                    sp.dma_start(R[:, :], a["rope"]).then_inc(s["rope_in"], 16)
                if n == W1_AT[3]:
                    sp.wait_ge(s["oa_ok"], 4)
                    sp.dma_start(w2[:, 0, :], a["cmp_w2_k"]).then_inc(s["w2_in"], 16)
                    sp.dma_start(w2[:, 1, :], a["cmp_w2_v"]).then_inc(s["w2_in"], 16)
                    sp.dma_start(w_rt[:, :, :], a["router_w"].rearrange("(k p) n -> p k n", p=P)).then_inc(s["rt_in"], 16)
                    sp.dma_start(rb, a["router_b"]).then_inc(s["rt_in"], 16)

            sp.wait_ge(s["proj_done"], N_END)
            sp.dma_start(fgb, a["final_norm_g"].rearrange("(o d) -> o d", o=1).to_broadcast([P, D])).then_inc(s["fg_in"], 16)

            for i, v in enumerate(pre_g):
                k = KT - len(pre_g) + i
                if i == 3:
                    sp.wait_ge(s["lg_mm"], 2)
                sp.dma_start(v, a["w_gate_up"][1, k * P:(k + 1) * P, :]).then_inc(pre_g_in[i], 16)
            for i, v in enumerate(pre_d):
                k = KT - len(pre_d) + i
                sp.dma_start(v, a["w_down"][1, k * P:(k + 1) * P, :]).then_inc(pre_d_in[i], 16)
            for w, dst, landed, used, early_from in ((a["w_gate_up"], wg, gu_in, s["gu_used"], KT - len(pre_g)), (a["w_down"], wd, dn_in, s["dn_used"], KT - len(pre_d))):
                for k in range(KT):
                    sp.wait_ge(used, k + 1)
                    if k >= early_from:
                        sp.sem_inc(landed[k], 16)
                    sp.dma_start(dst[:, k, :], w[2 if k >= early_from else 1, k * P:(k + 1) * P, :]).then_inc(landed[k], 16)
            for w, dst, landed, used, early_from in ((a["w_gate_up"], wg, gu_in, s["gu_used"], KT - len(pre_g)), (a["w_down"], wd, dn_in, s["dn_used"], KT - len(pre_d))):
                for k in range(early_from):
                    sp.wait_ge(used, KT + k + 1)
                    sp.dma_start(dst[:, k, :], w[2, k * P:(k + 1) * P, :]).then_inc(landed[k], 16)

            def expert(n, e):
                for k in range(KT):
                    sp.wait_ge(s["gu_used"], n * KT + (k + 1 - KT))
                    sp.dma_start(wg[:, k, :], a["w_gate_up"][bass.ds(e, 1), k * P:(k + 1) * P, :].rearrange("o p n -> (o p) n")).then_inc(gu_in[k], 16)
                for k in range(KT):
                    sp.wait_ge(s["dn_used"], n * KT + (k + 1 - KT))
                    sp.dma_start(wd[:, k, :], a["w_down"][bass.ds(e, 1), k * P:(k + 1) * P, :].rearrange("o p n -> (o p) n")).then_inc(dn_in[k], 16)

            with sp.Fori(3, NE) as e:
                expert(e, e)
            sp.wait_ge(s["pass_ok"], 1)
            many = sp.value_load(npass[0:1, 0:1], min_val=0, max_val=SEQ)
            with sp.If(many > CAP):
                with sp.Fori(1, SEQ // CAP) as p:
                    with sp.Fori(0, NE) as e:
                        expert(p * NE + e, e)
            for t in range(TT):
                sp.wait_ge(s["fin_ok"], t + 1)
                sp.dma_start(a["out"][0, t * P:(t + 1) * P, :], X[:, t, :]).then_inc(s["out_out"], 16)
            sp.wait_ge(s["out_out"], 16 * TT)

        @block.tensor
        def _(pe):
            def mm(out, lhsT, rhs, start=True, stop=True):
                return pe.matmul(out, lhsT, rhs, start=start, stop=stop)

            def tr(out, in_):
                n = in_.shape[0]
                return pe.transpose(out, in_, C[0:n, K_ID:K_ID + n])

            def warm(n, v=C[:, 0:SEQ], bank=1):
                for _ in range(n):
                    mm(PB[bank][:, 0:SEQ], v[:, 0:P], v)

            def norm_T(n):
                for t in range(TT):
                    turn_tile(n, t)

            def turn_tile(n, t):
                src = x3n if n == 3 else Xn if n < 2 else x2n
                pe.wait_ge(s["xn_n"], 2 * n + t + 1)
                for j in range(2):
                    for k in range(4):
                        last = tr(PB[2 + 2 * t + j][:, k * P:(k + 1) * P], src[:, t, (4 * j + k) * P:(4 * j + k + 1) * P])
                    last.then_inc(s["tr_n"], 1)

            pe.wait_ge(s["zeros_ok"], 1)
            warm(WARM_FIRST, zeros)
            pe.wait_ge(s["c_in"], 16)
            turn_tile(0, 0)
            pe.wait_ge(s["rows_in"], 16 * 5)
            pe.wait_ge(s["rows1_in"], 16 * 3)
            tr(PB[0][:, 0:P], rowsA)
            tr(PB[0][:, P:P + 65], rowsB[0:65, :]).then_inc(s["cols_tr"], 1)
            warm(2, zeros)
            turn_tile(0, 1)
            pe.wait_ge(s["wba_in"], 32)
            for t in range(TT):
                pe.wait_ge(s["hT_n"], 2 * t + 2)
                for k in range(KT):
                    last = mm(PB[7][:, t * 5 * HEADS:(t + 1) * 5 * HEADS], hT[:, k, t * P:(t + 1) * P], w_bn[:, k, :], k == 0, k == KT - 1)
            last.then_inc(s["ba_mm"], 1)
            pe.wait_ge(s["ba_ok"], 1)
            for j in range(2):
                for t in range(TT):
                    last = tr(PB[6][0:HEADS, j * SEQ + t * P:j * SEQ + (t + 1) * P], ba[:, t, j * HEADS:(j + 1) * HEADS])
            last.then_inc(s["ba_tr"], 1)

            def chunk(slot, nth, turn, src, tok=False, tiles=2, half=None, kt=KT):
                bank = PB[slot % 2]
                if half in (None, 0):
                    pe.wait_ge(ring_in[slot], nth)
                    pe.wait_ge(s["proj_taken"], turn)
                w = rw(slot) if kt == KT else ring[:, slot, 0:kt * SLOT].rearrange("p (k n) -> p k n", k=kt)
                for i in range(2):
                    if half is not None and i != half:
                        continue
                    for k in range(kt):
                        if tok:
                            last = mm(bank[:, i * SLOT:(i + 1) * SLOT], src[:, k, i * P:(i + 1) * P], w[:, k, :], k == 0, k == kt - 1)
                        else:
                            last = mm(bank[:, i * SEQ:(i + 1) * SEQ], w[:, k, i * P:(i + 1) * P], src[:, k, :], k == 0, k == kt - 1)
                if half in (None, 1):
                    last.then_inc(s["proj_done"], 1)

            def chunk_n(n, src, **kw):
                chunk(n % RING, 16 * (n // RING + 1), n + 1, src, **kw)

            with pe.Fori(0, 3) as it:
                for j in range(RING):
                    chunk(j, 16 * it + 16, 4 * it + (j + 1), hT)
            norm_T(1)
            pe.wait_ge(s["tp_ok"], 1)
            for q in range(4):
                for t in range(TT):
                    last = tr(PB[6][:, (q * TT + t) * HEADS:(q * TT + t + 1) * HEADS], TP[:, q, t * P:(t + 1) * P])
            last.then_inc(s["tp_tr"], 1)

            filled = [0]

            def fill(goal):
                goal = min(goal, all_goal)
                for j in range(filled[0], goal):
                    n, i, k = fillers[j // PRODUCTS], j // KT % 2, j % KT
                    if (i, k) == (0, 0):
                        pe.wait_ge(ring_in[n % RING], 16 * (n // RING + 1))
                        pe.wait_ge(s["proj_taken"], n + 1)
                        if n == N_BA:
                            pe.wait_ge(s["z_ok"], 1)
                    out = PB[n % 2][:, i * SEQ:(i + 1) * SEQ]
                    src = mT if N_XKV <= n < N_VS else oaT if n >= N_BA else hT
                    if N_XKV + 2 <= n < N_VS:
                        last = mm(out, src[:, k, i * P:(i + 1) * P], rw(n % RING)[:, k, :], k == 0, k == KT - 1)
                    else:
                        last = mm(out, rw(n % RING)[:, k, i * P:(i + 1) * P], src[:, k, :], k == 0, k == KT - 1)
                    if (i, k) == (1, KT - 1):
                        last.then_inc(s["proj_done"], 1)
                filled[0] = max(filled[0], goal)

            fill(lead_goal)
            pe.wait_ge(s["gbrow_in"], 16 * 3)
            pe.wait_ge(s["hT_n"], 8)
            for i in range(HEADS):
                pe.wait_ge(s["sq_ok"], i + 1)
                if i >= 2:
                    pe.wait_ge(s["rinv_g"], i - 1)
                mm(PB[4 + i % 2], ones, flat2(sq[i % 2])).then_inc(s["ss_mm"], 1)
                if i >= 2:
                    pe.wait_ge(s["tab_ok"], i - 1)
                mm(PB[2 + i % 2], ones3, G3[:, i, :]).then_inc(s["bc_mm"], 1)
                fill(table_goal[i])

            def before(b, part):
                if part == 0:
                    if b == 0:
                        pe.wait_ge(s["qk_ok"], HEADS)
                        pe.wait_ge(s["rinv_g"], HEADS)
                    elif b >= 2:
                        pe.wait_ge(s["oa_ok"], b - 1)
                    for h in range(2):
                        for t in range(TT):
                            m, k, q = slice((2 * h + t) * P, (2 * h + t + 1) * P), HEADS + 2 * b + h, 2 * b + h
                            f = slice(t * P, (t + 1) * P)
                            mm(PB[5][:, m], cT[:, k, f], cT[:, k, f])
                            mm(PB[6][:, m], cT[:, k, f], cT[:, q, f])
                            last = tr(PB[7][:, m], cT[:, k, f])
                    last.then_inc(s["pre_mm"], 1)
                else:
                    pe.wait_ge(s["kd_ok"], b + 1)
                    for h in range(2):
                        for t in range(TT):
                            last = tr(PB[7][:, (2 * h + t) * P:(2 * h + t + 1) * P], cT[:, 2 * HEADS + 2 * b + h, t * P:(t + 1) * P])
                    last.then_inc(s["vt_mm"], 1)

            def after(b, part):
                B = b % 2
                if part == 0:
                    pe.wait_ge(s["tu_ok"], 6 * b + 6)
                    if b < 3:
                        pe.wait_ge(s["qkm_ok"], b + 2)
                    for m in range(4):
                        mm(PB[5][:, m * P:(m + 1) * P], Um[B][:, m, :], vb[B][:, m, :])
                    for h in range(2):
                        last = mm(PB[6][:, h * P:(h + 1) * P], kd[B][:, 2 * h + 1, :], Um[B][:, 2 * h + 1, :])
                    last.then_inc(s["u_mm"], 1)
                elif part == 1:
                    pe.wait_ge(s["u_ok"], b + 1)
                    if b < 3:
                        pe.wait_ge(s["vb_ok"], b + 2)
                    for h in range(2):
                        last = mm(PB[7][:, h * P:(h + 1) * P], kd[B][:, 2 * h, :], u[:, 2 * h, :])
                    last.then_inc(s["s_mm"], 1)
                elif part == 2:
                    pe.wait_ge(s["w_ok"], b + 1)
                    pe.wait_ge(s["s_ok"], b + 1)
                    for h in range(2):
                        last = mm(PB[6][:, h * P:(h + 1) * P], wT[:, h, :], S1[:, h, :])
                    last.then_inc(s["ws_mm"], 1)
                elif part == 3:
                    pe.wait_ge(s["vn_ok"], b + 1)
                    for h in range(2):
                        o = PB[5][:, h * SEQ:(h + 1) * SEQ]
                        mm(o[:, 0:P], u[:, 2 * h, :], QKm[B][:, 2 * h, :])
                        mm(o[:, P:SEQ], S1[:, h, :], qd[B][:, h, :], True, False)
                        last = mm(o[:, P:SEQ], vn[:, h, :], QKm[B][:, 2 * h + 1, :], False, True)
                    last.then_inc(s["o_mm"], 1)
                else:
                    pe.wait_ge(s["sqo_ok"], b + 1)
                    mm(PB[7], ones, flat2(sqo)).then_inc(s["so_mm"], 1)

            def side(b, gap):
                if b and gap < 5:
                    after(b - 1, gap)
                if b < 3 and gap in (6, 8):
                    before(b + 1, (gap - 6) // 2)

            before(0, 0)
            fill(first_goal[0])
            before(0, 1)
            fill(first_goal[1])
            for b in range(HEADS // 2):
                B = b % 2
                pe.wait_ge(s["u0_ok"], b + 1)
                for m in range(4):
                    last = tr(PB[2][:, m * P:(m + 1) * P], Um[B][:, m, :])
                last.then_inc(s["t0_mm"], 1)
                fill(start_goal[b])
                pe.wait_ge(s["t0_ok"], b + 1)
                for lv in range(1, LEVELS):
                    pe.wait_ge(s["lt_ok"], 6 * b + lv)
                    if lv > 1:
                        pe.wait_ge(s["tu_ok"], 6 * b + lv - 1)
                    for m in range(4):
                        last = mm(PB[2][:, m * P:(m + 1) * P], LT[:, m, :], Tm[:, m, :])
                    last.then_inc(s["m1_mm"], 1)
                    side(b, 2 * lv - 2)
                    fill(gap_goal[b][2 * lv - 2])
                    pe.wait_ge(s["m1_ok"], 6 * b + lv)
                    if lv < LEVELS - 1:
                        for m in range(4):
                            mm(PB[3][:, m * P:(m + 1) * P], Um[B][:, m, :], M1s[:, m, :])
                    for m in range(4):
                        last = mm(PB[4][:, m * P:(m + 1) * P], M1s[:, m, :], Um[B][:, m, :])
                    last.then_inc(s["c_mm"], 1)
                    side(b, 2 * lv - 1)
                    fill(gap_goal[b][2 * lv - 1])
            for part in range(5):
                after(3, part)
                fill(tail_goal[part])
            fill(delta_goal)

            def compress(i):
                n, v = W1_AT[i], i // 2
                pe.wait_ge(ring_in[n % RING], 16 * (n // RING + 1))
                if i % 2 == 0:
                    pe.wait_ge(s["blk_ok"], v + 1)
                if i < 2:
                    pe.wait_ge(ring_in[V_AT[i] % RING], 16 * (V_AT[i] // RING + 1))
                    pe.wait_ge(s["proj_taken"], V_AT[i] + 1)
                for l in range(16):
                    last = mm(PB[4 + v][:, 0:GROUPS * NCMP], ring[:, n % RING, l * P:(l + 1) * P], blk[:, v, 16 * (i % 2) + l, :], i % 2 == 0 and l == 0, i % 2 == 1 and l == 15)
                    if l == 15:
                        last.then_inc(s["proj_done"], 1)
                    if i < 2:
                        t, k = l // KT, l % KT
                        last = mm(PB[V_AT[i] % 2][:, t * SLOT:(t + 1) * SLOT], hT[:, k, t * P:(t + 1) * P], rw(V_AT[i] % RING)[:, k, :], k == 0, k == KT - 1)
                        if l == 15:
                            last.then_inc(s["proj_done"], 1)
                    else:
                        fill(delta_goal + (i - 2) * PRODUCTS + l + 1)

            def rotate(r):
                if r >= 2:
                    pe.wait_ge(s["rope_ok"], r - 1)
                src = big[0:ROT, 8 + 2 * r:10 + 2 * r, :] if r < 4 else big[0:ROT, 20 + 2 * (r - 4):22 + 2 * (r - 4), :]
                mm(PB[2 + r % 2][0:ROT, :], R[:, R_ROT:R_ROT + ROT], src.rearrange("p a b -> p (a b)")).then_inc(s["rope_mm"], 1)

            pe.wait_ge(s["oa_ok"], 4)
            pe.wait_ge(s["tu_ok"], 6 * 4)
            pe.wait_ge(s["rope_in"], 16)
            compress(0)
            for r in range(2):
                rotate(r)
            compress(1)
            for r in range(2, 4):
                rotate(r)
            compress(2)
            for r in range(4, 6):
                rotate(r)
            compress(3)
            fill(w1_goal)
            pe.wait_ge(s["w1_act"], 2)
            pe.wait_ge(s["w2_in"], 32)
            mm(PB[4][:, 0:GROUPS * NCMP], w2[:, 0, :], s1[:, 0, :])
            for g in range(GROUPS):
                last = mm(PB[4][0:NCMP, 64 + g * DH:64 + (g + 1) * DH], s1[:, 1, g * NCMP:(g + 1) * NCMP], w2[:, 1, :])
            last.then_inc(s["w2_mm"], 1)
            fill(w2_goal)
            pe.wait_ge(s["w2_ok"], 1)
            for t in range(TT):
                for h in range(HEADS):
                    g = h // REP
                    last = mm(PB[4][:, (t * HEADS + h) * 16:(t * HEADS + h) * 16 + NCMP], big[:, 8 + h, t * P:(t + 1) * P], ccT[:, g * NCMP:(g + 1) * NCMP])
            last.then_inc(s["cs_mm"], 1)
            fill(cs_goal)
            pe.wait_ge(s["cs_ok"], 1)
            for r in range(4):
                if r >= 2:
                    pe.wait_ge(s["ct_ok"], r - 1)
                for i in range(2):
                    for t in range(TT):
                        last = tr(PB[6 + r % 2][0:NCMP, i * SEQ + t * P:i * SEQ + (t + 1) * P], sc[:, t, 2 * r + i, :])
                last.then_inc(s["ct_mm"], 1)
                fill(ct_goal[r])
            pe.wait_ge(s["ct_ok"], 4)
            pe.wait_ge(s["rope_ok"], 6)

            def scores(i):
                st = steps[i]
                w = st["n"] * P
                if i >= 2:
                    pe.wait_ge(s["sc_read"], i - 1)
                for h in range(REP):
                    o = 2 * (i % 2) * 512 + h * w
                    last = mm(psum[:, 1024 + o:1024 + o + w], st["q"](h), st["k"](h)[:, 0:w])
                last.then_inc(s["sc_mm"], 1)

            def turned(i):
                st = steps[i]
                pe.wait_ge(s["pn_ok"], i + 1)
                if i:
                    pe.wait_ge(s["tp_taken"], i)
                if i == 4:
                    pe.wait_ge(s["pv_ok"], 2)
                for kt in range(st["n"]):
                    for h in range(REP):
                        last = tr(PB[6 + kt][:, h * P:(h + 1) * P], st["S"][:, h, kt * P:(kt + 1) * P])
                last.then_inc(s["tp_mm"], 1)

            scores(0)
            for g in range(GROUPS):
                for j in range(4):
                    i = 4 * g + j
                    if i < 7:
                        scores(i + 1)
                    fill(step_goal[i][0])
                    turned(i)
                    fill(step_goal[i][1])
                pe.wait_ge(s["tp_taken"], 4 * g + 4)
                for h in range(REP):
                    o = PB[6 + h // 2][:, (h % 2) * SEQ:(h % 2 + 1) * SEQ]
                    mm(o, vc[:, g, :], PcT[:, g * REP + h, :], True, False)
                    for br in range(2):
                        mm(o, vtok[:, br, 0, g * DH:(g + 1) * DH], PT[br][:, 0, h, :], False, False)
                        last = mm(o[:, P:SEQ], vtok[:, br, 1, g * DH:(g + 1) * DH], PT[br][:, 1, h, P:SEQ], False, br == 1)
                    if h % 2:
                        last.then_inc(s["pv_mm"], 1)

            def into_stream(n0, src, kt, n):
                pe.wait_ge(s["proj_taken"], n0 + 2)
                for t in range(TT):
                    for c in range(4):
                        slot = (n0 + c) % RING
                        w = ring[:, slot, 0:kt * SLOT].rearrange("p (k n) -> p k n", k=kt)
                        if t == 0:
                            pe.wait_ge(ring_in[slot], 16 * ((n0 + c) // RING + 1))
                        for k in range(kt):
                            last = mm(PB[6 * t + c // 2][:, (c % 2) * SLOT:(c % 2 + 1) * SLOT], src[:, k, t * P:(t + 1) * P], w[:, k, :], k == 0, k == kt - 1)
                        if t == 1:
                            last.then_inc(s["proj_done"], 1)
                        elif c % 2:
                            last.then_inc(s["res_mm"], 1)
                        if t == 1 and c == (1 if kt == KT else 2):
                            turn_tile(n, 0)

            fill(all_goal)
            pe.wait_ge(s["pv_ok"], 4)
            for n in range(N_BB, N_MIX):
                chunk_n(n, obT)
            pe.wait_ge(s["mixed"], 4)
            into_stream(N_MIX, mixT, KT, 2)
            pe.wait_ge(s["proj_taken"], N_XQ + 2)
            warm(6, bank=0)
            turn_tile(2, 1)
            pe.wait_ge(s["hT_n"], 12)
            chunk_n(N_XQ, hT)
            pe.wait_ge(s["proj_taken"], N_XQ + 3)
            scores(8)
            chunk_n(N_XQ + 1, hT)
            pe.wait_ge(s["proj_taken"], N_XQ + 4)
            scores(9)
            pe.wait_ge(s["ex_ok"], 9)
            for j in range(2):
                warm(WARM_STEP[j], bank=2)
                turned(8 + j)
                pe.wait_ge(s["tp_taken"], 9 + j)
                for h in range(2 * j, 2 * j + 2):
                    o = PB[j][:, (h % 2) * SEQ:(h % 2 + 1) * SEQ]
                    for kt in range(TT):
                        last = mm(o, xv[:, kt, h * DH:(h + 1) * DH], PTx[:, kt, h, :], kt == 0, kt == 1)
                last.then_inc(s["pv_mm"], 1)
            warm(2, bank=2)
            pe.wait_ge(s["pv_ok"], 6)
            into_stream(N_XO, xoT, XH, 3)

            pe.wait_ge(s["rt_in"], 32)
            pe.wait_ge(s["proj_taken"], N_END + 2)
            for t in range(TT):
                if t:
                    warm(3)
                    turn_tile(3, 1)
                mm(PB[t][:, 0:NE], C[0:1, K_ONES:K_ONES + P], rb, True, False)
                for k in range(KT):
                    if k % 4 == 0:
                        pe.wait_ge(s["hT_n"], 13 + 2 * t + k // 4)
                    last = mm(PB[t][:, 0:NE], hT[:, k, t * P:(t + 1) * P], w_rt[:, k, :], False, k == KT - 1)
                last.then_inc(s["lg_mm"], 1)
            warm(4, bank=3)
            pe.wait_ge(s["lg_ok"], 1)
            mm(PB[2][:, 0:NE], C[:, K_STRICT:K_STRICT + P], msk[:, 0, :])
            mm(PB[2][:, NE:2 * NE], ones, msk[:, 0, :], True, False)
            mm(PB[2][:, NE:2 * NE], C[:, K_STRICT:K_STRICT + P], msk[:, 1, :], False, True)
            mm(PB[2][:, 2 * NE:3 * NE], ones, msk[:, 0, :], True, False)
            mm(PB[2][:, 2 * NE:3 * NE], ones, msk[:, 1, :], False, True).then_inc(s["rk_mm"], 1)

            def gather(t):
                pe.wait_ge(s["pg_ok"], t + 1)
                for k in range(KT):
                    for tt in range(TT):
                        last = mm(PB[4 + k // 4][:, (k % 4) * P:(k % 4 + 1) * P], x3n[:, tt, k * P:(k + 1) * P], Pg[:, tt, :, :].rearrange("p a b -> p (a b)"), tt == 0, tt == 1)
                last.then_inc(s["gat_mm"], 1)

            def gate_up(t, e, early_loads=False):
                pe.wait_ge(s["gu_taken"], 2 * t + (e + 1))
                pe.wait_ge(s["bsel_ok"], t + 1)
                if e == 0:
                    pe.wait_ge(s["xg_ok"], t + 1)
                for c in range(4):
                    mm(PB[c // 2][64 * (c % 2):64 * (c % 2) + CAP, :], bselv[0:3 * NE, e * CAP:(e + 1) * CAP], bspl[:, c * 512:(c + 1) * 512], True, False)
                for k in range(KT):
                    w, i = wg[:, k, :], k - (KT - len(pre_g))
                    if early_loads and i >= 0:
                        pe.wait_ge(pre_g_in[i], 16)
                        w = pre_g[i]
                    else:
                        pe.wait_ge(gu_in[k], 32 * t + 16 * (e + 1))
                    for c in range(4):
                        last = mm(PB[c // 2][64 * (c % 2):64 * (c % 2) + CAP, :], xg[:, k, e, :], w[:, c * 512:(c + 1) * 512], False, k == KT - 1)
                    last.then_inc(s["gu_used"], 1)

            def down(t, e, early_loads=False):
                pe.wait_ge(s["h_ok"], 2 * t + (e + 1))
                for c in range(4):
                    last = tr(PB[2][:, c * P:(c + 1) * P], hh[:, c * P:(c + 1) * P])
                last.then_inc(s["ht_mm"], 1)
                pe.wait_ge(s["ht_ok"], 2 * t + (e + 1))
                if e == 0:
                    pe.wait_ge(s["pgt_ok"], t + 1)
                for c in range(2):
                    mm(PB[3][64 * c:64 * c + CAP, :], bselv[0:3 * NE, e * CAP:(e + 1) * CAP], bspl[:, 2 * D + c * 512:2 * D + (c + 1) * 512], True, False)
                for k in range(KT):
                    w, i = wd[:, k, :], k - (KT - len(pre_d))
                    if early_loads and i >= 0:
                        pe.wait_ge(pre_d_in[i], 16)
                        w = pre_d[i]
                    else:
                        pe.wait_ge(dn_in[k], 32 * t + 16 * (e + 1))
                    for c in range(2):
                        last = mm(PB[3][64 * c:64 * c + CAP, :], hTt[:, k % 4, (k // 4) * CAP:(k // 4 + 1) * CAP], w[:, c * 512:(c + 1) * 512], False, k == KT - 1)
                    last.then_inc(s["dn_used"], 1)

            def scatter(t, e):
                pe.wait_ge(s["y_ok"], 2 * t + (e + 1))
                pe.wait_ge(s["pgt_ok"], t + 1)
                pe.wait_ge(s["acc_ok"], 2 * t + (e + 1))
                if e == 1:
                    pe.wait_ge(s["xg_ok"], t + 2)
                for tt in range(TT):
                    for c in range(2):
                        last = mm(PB[4 + 2 * tt + c][:, :], PGT[64 * c:64 * c + CAP, e, tt, :], ys[64 * c:64 * c + CAP, :])
                    last.then_inc(s["scat"], 1)

            def experts(t, first=False, carry=True):
                gate_up(t, 0)
                if carry and not first:
                    scatter(t - 1, 1)
                pe.wait_ge(s["pgd_ok"], t + 1)
                if not first:
                    pe.wait_ge(s["y_ok"], 2 * t)
                for e in range(2):
                    for tt in range(TT):
                        last = tr(PB[3][:, (2 * e + tt) * P:(2 * e + tt + 1) * P], PGd[:, e, tt, :])
                last.then_inc(s["pgt_mm"], 1)
                down(t, 0)
                scatter(t, 0)
                gate_up(t, 1, first)
                pe.wait_ge(s["acc_ok"], 2 * t + 2)
                gather(t + 1)
                down(t, 1, first)
                if not carry:
                    scatter(t, 1)

            pe.wait_ge(s["prep_ok"], 1)
            warm(4, bank=3)
            gather(0)
            experts(0, True)
            with pe.Fori(1, NE // 2) as t:
                experts(t)
            scatter(NE // 2 - 1, 1)
            many = pe.value_load(npass[0:1, 0:1], min_val=0, max_val=SEQ)
            with pe.If(many > CAP):
                with pe.Fori(NE // 2, SEQ // CAP * (NE // 2)) as t:
                    experts(t, carry=False)

        @block.scalar
        def _(act):
            def fn(out, in_, f=ACT.Copy, **kw):
                return act.activation(out, in_, f, **kw)

            def norm(n, t, src, junk):
                fn(junk[:, t, :], src[:, t, :], ACT.Square, accum_out=stat[:, n, 0, t:t + 1])
                act.drain()
                if n == 0:
                    act.wait_ge(s["c_in"], 16)
                fn(stat[:, n, 1, t:t + 1], stat[:, n, 0, t:t + 1], ACT.Ln, scale=1.0 / D, bias=eps)
                act.drain()
                fn(stat[:, n, 2, t:t + 1], stat[:, n, 1, t:t + 1], ACT.Exp, scale=-0.5).then_inc(s["rinv_n"], 1)

            act.sem_inc(s["proj_taken"], 2)
            act.preload_act_table_set("natural_log_exp_and_others")
            act.dma_start(w_bn[:, :, 0:2 * HEADS], cols(w_in, C_B, n=2 * HEADS)).then_inc(s["wba_in"], 16)
            act.dma_start(w_bn[:, :, 2 * HEADS:], cols(w_in, C_NG, n=3 * HEADS)).then_inc(s["wba_in"], 16)
            for t in range(TT):
                act.wait_ge(s[("x_in", "x1_in")[t]], 16)
                norm(0, t, X, Xn)

            act.wait_ge(s["ba_mm"], 1)
            logits = PB[7][:, 0:TT * 5 * HEADS].rearrange("p (t n) -> p t n", t=TT)
            fn(ba, logits[:, :, 0:2 * HEADS]).then_inc(s["ba_ok"], 1)
            act.wait_ge(s["mem_in"], 16)
            act.wait_ge(s["tr_n"], 4)
            for t in range(TT):
                norm(1, t, memx, Xn)

            fn(gates[:, :, :], logits[:, :, 2 * HEADS:], ACT.Sigmoid)
            act.wait_ge(s["ba_tr"], 1)
            fn(GB[:, 1, :], PB[6][0:HEADS, 0:SEQ], ACT.Sigmoid).then_inc(s["ba_sig"], 1)
            act.preload_act_table_set("natural_log_exp_and_others")
            act.wait_ge(s["sp_lin"], 1)
            fn(g1[:, 2, :], g1[:, 1, :], ACT.Exp, scale=-1.0)
            fn(abias[:, 2:3], abias[:, 0:1], ACT.Exp)
            act.drain()
            fn(g1[:, 3, :], g1[:, 2, :], ACT.Ln, bias=one[0:HEADS, :]).then_inc(s["sp_exp"], 1)
            act.wait_ge(s["gc_ok"], 1)
            fn(TP[:, 2, :], g1[:, 0, :], ACT.Exp)
            fn(g1[:, 2, :], GB[:, 0, :], ACT.Exp).then_inc(s["gc_exp"], 1)
            act.wait_ge(s["gsplit"], 1)
            for i in range(3):
                act.dma_start(G3[i:i + 1, :, :], Gp[:, i, :]).then_inc(s["gbrow_in"], 16)

            act.wait_ge(s["pads"], 1)
            act.preload_act_table(ACT.Sigmoid)
            with act.Fori(0, 3) as it:
                for j in range(RING):
                    act.wait_ge(s["proj_done"], 4 * it + (j + 1))
                    act.wait_ge(s["conv_ok"], 4 * it + (j + 1))
                    fn(raw[:, j % 2, :, CONV - 1:], PB[j % 2].rearrange("p (a b) -> p a b", b=SEQ)).then_inc(s["proj_taken"], 1)
                    act.wait_ge(s["conv_ok"], 4 * it + (j + 3))
                    fn(csg[:, j % 2, :], cy[:, j % 2, :], ACT.Sigmoid).then_inc(s["sig_ok"], 1)
            act.preload_act_table_set("natural_log_exp_and_others")
            drained = [0]

            def out(goal):
                while PRODUCTS * (drained[0] + 1) <= min(goal, all_goal):
                    n = fillers[drained[0]]
                    act.wait_ge(s["proj_done"], n + 1)
                    if n < N_XKV:
                        i = 2 * (n - N_Z)
                        fn(flat2(big[:, i:i + 2, :]), PB[n % 2]).then_inc(s["proj_taken"], 1)
                    elif n < N_XKV + 2:
                        act.wait_ge(s["qd_ok"], 4)
                        i = 2 * (n - N_XKV)
                        fn(flat2(xkT[:, i:i + 2, :]), PB[n % 2]).then_inc(s["proj_taken"], 1)
                    elif n < N_VS:
                        i = SLOT * (n - N_XKV - 2)
                        fn(xv[:, :, i:i + SLOT], PB[n % 2].rearrange("p (a b) -> p a b", b=SLOT)).then_inc(s["proj_taken"], 1)
                    elif n < N_BA:
                        i = 2 * MB_AT.index(n)
                        fn(flat2(mb[:, i:i + 2, :]), PB[n % 2]).then_inc(s["proj_taken"], 1)
                    else:
                        i = 2 * (n - N_BA)
                        fn(flat2(yaT[:, i:i + 2, :]), PB[n % 2]).then_inc(s["proj_taken"], 1)
                    drained[0] += 1

            out(lead_goal)
            for i in range(HEADS):
                act.wait_ge(s["ss_mm"], i + 1)
                if i >= 2:
                    act.wait_ge(s["qk_ok"], i - 1)
                fn(flat2(lnr[i % 2]), PB[4 + i % 2], ACT.Ln, bias=eps)
                act.drain()
                fn(lnr[i % 2], lnr[i % 2], ACT.Exp, scale=-0.5).then_inc(s["rinv_g"], 1)
                act.wait_ge(s["dd_ok"], i + 1)
                fn(EDm[:, i, :, :], ddh[i % 2], ACT.Exp)
                fn(eG[:, i, :], PB[2 + i % 2][:, P:SEQ], ACT.Exp).then_inc(s["ed_ok"], 1)
                out(table_goal[i])

            def after(b, part):
                if part == 0:
                    act.wait_ge(s["u_mm"], b + 1)
                    fn(flat2(u), PB[5]).then_inc(s["u_ok"], 1)
                elif part == 1:
                    act.wait_ge(s["s_mm"], b + 1)
                    fn(flat2(S1), PB[7][:, 0:SEQ]).then_inc(s["s_ok"], 1)
                elif part == 3:
                    act.wait_ge(s["o_mm"], b + 1)
                    fn(flat2(sqo), PB[5], ACT.Square).then_inc(s["sqo_ok"], 1)
                elif part == 4:
                    act.wait_ge(s["so_mm"], b + 1)
                    fn(flat2(lno), PB[7], ACT.Ln, scale=1.0 / DH, bias=eps)
                    act.drain()
                    fn(lno, lno, ACT.Exp, scale=-0.5).then_inc(s["lno_ok"], 1)

            out(first_goal[1])
            for b in range(HEADS // 2):
                act.wait_ge(s["t0_mm"], b + 1)
                fn(flat2(Tm), PB[2]).then_inc(s["t0_ok"], 1)
                out(start_goal[b])
                for lv in range(1, LEVELS):
                    act.wait_ge(s["m1_mm"], 6 * b + lv)
                    fn(flat2(M1s), PB[2]).then_inc(s["m1_ok"], 1)
                    if b and 2 * lv - 2 < 5:
                        after(b - 1, 2 * lv - 2)
                    out(gap_goal[b][2 * lv - 2])
                    if b and 2 * lv - 1 < 5:
                        after(b - 1, 2 * lv - 1)
                    out(gap_goal[b][2 * lv - 1])
            for part in range(5):
                after(3, part)
                out(tail_goal[part])
            out(delta_goal)

            act.preload_act_table(ACT.Sigmoid)
            act.wait_ge(s["oa_ok"], 4)
            fn(zs, big[:, 0:8, :], ACT.Sigmoid).then_inc(s["zsig"], 1)
            for i in range(2):
                act.wait_ge(s["proj_done"], W1_AT[i] + 1)
                if i == 0:
                    act.drain().then_inc(s["proj_taken"], 1)
                else:
                    fn(s1g[:, 0, :], PB[4][:, 0:GROUPS * NCMP], ACT.Sigmoid).then_inc(s["proj_taken"], 1)
                act.wait_ge(s["proj_done"], V_AT[i] + 1)
                fn(vtok[:, i, :, :].rearrange("p a b -> p (a b)"), PB[V_AT[i] % 2]).then_inc(s["proj_taken"], 1)
            fn(big[:, 24:32, :], big[:, 24:32, :], ACT.Sigmoid)
            act.wait_ge(s["proj_done"], W1_AT[2] + 1)
            act.drain().then_inc(s["proj_taken"], 1)
            out(mb_goal)
            act.wait_ge(s["proj_done"], W1_AT[3] + 1)
            fn(s1g[:, 1, :], PB[5][:, 0:GROUPS * NCMP], ACT.Sigmoid).then_inc(s["proj_taken"], 1)
            act.preload_act_table_set("natural_log_exp_and_others")
            act.wait_ge(s["w2_mm"], 1)
            fn(ccT, PB[4][:, 0:GROUPS * NCMP])
            fn(vc, PB[4][0:NCMP, 64:64 + KV].rearrange("p (a b) -> p a b", b=DH)).then_inc(s["w2_ok"], 1)
            out(cs_goal)
            act.wait_ge(s["cs_max"], 1)
            fn(sc, sc, ACT.Exp).then_inc(s["cs_exp"], 1)
            for r in range(4):
                act.wait_ge(s["ct_mm"], r + 1)
                fn(PcT[:, 2 * r:2 * r + 2, :].rearrange("p a b -> p (a b)"), PB[6 + r % 2][0:NCMP, :]).then_inc(s["ct_ok"], 1)
                out(ct_goal[r])

            def exps(i):
                st = steps[i]
                act.wait_ge(s["mx_ok"], i + 1)
                w = st["n"] * P
                for h in range(REP):
                    o = 1024 + 2 * (i % 2) * 512 + h * w
                    src, scale = (st["S"][:, h, 0:w], 1.0) if i < 8 else (psum[:, o:o + w], SCALE)
                    last = fn(st["S"][:, h, 0:w], src, ACT.Exp, scale=scale, bias=smx[:, i % 2, h:h + 1], accum_out=ssum[:, i % 2, h:h + 1])
                last.then_inc(s["ex_ok"], 1)

            def turned(i):
                st = steps[i]
                act.wait_ge(s["tp_mm"], i + 1)
                for kt in range(st["n"]):
                    last = fn(st["PT"](kt), PB[6 + kt].rearrange("p (a b) -> p a b", b=P))
                last.then_inc(s["tp_taken"], 1)

            exps(0)
            for g in range(GROUPS):
                for j in range(4):
                    i = 4 * g + j
                    if i < 7:
                        exps(i + 1)
                    out(step_goal[i][0])
                    turned(i)
                    out(step_goal[i][1])
                for h in range(0, REP, 2):
                    act.wait_ge(s["pv_mm"], 2 * g + h // 2 + 1)
                    fn(obT[:, g * REP + h:g * REP + h + 2, :].rearrange("p a b -> p (a b)"), PB[6 + h // 2]).then_inc(s["pv_ok"], 1)
            out(all_goal)
            act.preload_act_table(ACT.Sigmoid)
            fn(mb[:, :, :], mb[:, :, :], ACT.Sigmoid).then_inc(s["mb_ok"], 1)
            act.preload_act_table_set("natural_log_exp_and_others")
            act.wait_ge(s["proj_taken"], N_XQ + 2)
            norm(2, 0, X, x2n)
            act.wait_ge(s["res_ok"], 1)
            norm(2, 1, X, x2n)
            for j in range(2):
                act.wait_ge(s["proj_done"], N_XQ + j + 1)
                fn(flat2(xqT[:, 2 * j:2 * j + 2, :]), PB[(N_XQ + j) % 2]).then_inc(s["proj_taken"], 1)
                exps(8 + j)
            for j in range(2):
                turned(8 + j)
                act.wait_ge(s["pv_mm"], 5 + j)
                fn(flat2(xoT[:, 2 * j:2 * j + 2, :]), PB[j]).then_inc(s["pv_ok"], 1)
            act.wait_ge(s["proj_taken"], N_END + 2)
            norm(3, 0, X, x3n)
            act.wait_ge(s["res_ok"], 2)
            norm(3, 1, X, x3n)
            act.wait_ge(s["lg_sub"], 1)
            fn(gate, lw, ACT.Exp).then_inc(s["lg_exp"], 1)

            def experts(t):
                for e in range(2):
                    act.wait_ge(s["act_g"], 2 * t + (e + 1))
                    fn(sg, gg, ACT.Sigmoid, scale=ALPHA).then_inc(s["act_s"], 1)
                    if e == 0:
                        act.wait_ge(s["pgt_mm"], t + 1)
                        fn(PGT.rearrange("p a b c -> p (a b c)"), PB[3]).then_inc(s["pgt_ok"], 1)
                    act.wait_ge(s["ht_mm"], 2 * t + (e + 1))
                    fn(hTt.rearrange("p a b -> p (a b)"), PB[2]).then_inc(s["ht_ok"], 1)
                    act.wait_ge(s["dn_used"], 16 * t + 8 * (e + 1))
                    fn(ys, PB[3]).then_inc(s["y_ok"], 1)

            act.preload_act_table(ACT.Sigmoid)
            with act.Fori(0, NE // 2) as t:
                experts(t)
            act.wait_ge(s["pass_ok"], 1)
            many = act.value_load(npass[0:1, 0:1], min_val=0, max_val=SEQ)
            with act.If(many > CAP):
                with act.Fori(NE // 2, PASSES * (NE // 2)) as t:
                    experts(t)
            act.preload_act_table_set("natural_log_exp_and_others")
            act.wait_ge(s["fin_acc"], 1)
            for t in range(TT):
                norm(4, t, X, hT[:, :, :].rearrange("p (t k) n -> p t (k n)", t=TT))

        @block.vector
        def _(dve):
            dr = dve.drain

            def tt(out, a0, a1, op):
                return dve.tensor_tensor(out, a0, a1, op)

            def ts(out, a0, s1, op, s2=None, op2=None):
                return dve.tensor_scalar(out, a0, s1, s2, op) if op2 is None else dve.tensor_scalar(out, a0, s1, s2, op, op2)

            def stt(out, a0, sc_, a1, op, op2):
                return dve.scalar_tensor_tensor(out, a0, sc_, a1, op, op2)

            def bc(v, n):
                return v.unsqueeze(len(v.shape)).to_broadcast([*v.shape, n])

            def mid(v, n):
                return v.unsqueeze(1).to_broadcast([v.shape[0], n, *v.shape[1:]])

            def scale_rows(n, t, src, dst):
                dve.wait_ge(s["rinv_n"], 2 * n + t + 1)
                ts(dst[:, t, :], src[:, t, :], stat[:, n, 2, t:t + 1], ALU.mult).then_inc(s["xn_n"], 1)

            def norm_out(n, t, dst):
                gcol = {0: gain(0), 1: gain(2), 2: gain(1), 3: gain(3)}[n]
                for j in range(2):
                    dve.wait_ge(s["tr_n"], 4 * n + 2 * t + j + 1)
                    f = slice(4 * j, 4 * j + 4)
                    tt(dst[:, f, t * P:(t + 1) * P], PB[2 + 2 * t + j].rearrange("p (a b) -> p a b", b=P), bc(gcol[:, f], P), ALU.mult).then_inc(s["hT_n"], 1)

            dve.memset(zeros, 0.0).then_inc(s["zeros_ok"], 1)
            scale_rows(0, 0, X, Xn)
            dve.wait_ge(s["cols_tr"], 1)
            dve.tensor_copy(colsA[:, :], PB[0][:, 0:P])
            dve.tensor_copy(colsB[:, :], PB[0][:, P:P + 65])
            scale_rows(0, 1, X, Xn)
            dr()
            for t in range(TT):
                norm_out(0, t, hT)
            dve.wait_ge(s["mem_in"], 16)
            for t in range(TT):
                scale_rows(1, t, memx, Xn)

            dve.wait_ge(s["ba_sig"], 1)
            dve.wait_ge(s["ab_in"], 32)
            ts(g1[:, 0, :], PB[6][0:HEADS, SEQ:2 * SEQ], abias[:, 1:2], ALU.add)
            dr()
            stt(g1[:, 1, :], g1[:, 0, :], -1.0, g1[:, 0, :], ALU.mult, ALU.max).then_inc(s["sp_lin"], 1)
            dve.wait_ge(s["sp_exp"], 1)
            stt(g1[:, 2, :], g1[:, 0, :], 0.0, g1[:, 3, :], ALU.max, ALU.add)
            dr()
            ts(g1[:, 1, :], g1[:, 2, :], abias[:, 2:3], ALU.mult, -1.0, ALU.mult)
            dr()
            for t in range(TT):
                q = slice(t * P, (t + 1) * P)
                dve.tensor_tensor_scan(GB[:, 0, q], C[0:HEADS, K_ONES:K_ONES + P], g1[:, 1, q], 0.0, ALU.mult, ALU.add)
            dr()
            for t in range(TT):
                q = slice(t * P, (t + 1) * P)
                ts(g1[:, 0, q], GB[:, 0, q], GB[:, 0, (t + 1) * P - 1:(t + 1) * P], ALU.subtract, -1.0, ALU.mult)
            dve.tensor_copy(TP[:, 0, :], GB[:, 1, :])
            dve.tensor_copy(TP[:, 1, :], GB[:, 0, :]).then_inc(s["gc_ok"], 1)
            dve.wait_ge(s["gc_exp"], 1)
            tt(TP[:, 3, :], g1[:, 2, :], GB[:, 1, :], ALU.mult).then_inc(s["tp_ok"], 1)
            dve.memset(ones3, 1.0)
            dve.tensor_copy(Gp[:, 0, :], flat2(GB))
            dr()
            tt(Gr, flat2(GB), Gp[:, 0, :], ALU.subtract)
            dr()
            dve.tensor_copy(Gp[:, 1, :], Gr)
            dr()
            tt(Gr, Gr, Gp[:, 1, :], ALU.subtract)
            dr()
            dve.tensor_copy(Gp[:, 2, :], Gr).then_inc(s["gsplit"], 1)

            dve.sem_inc(s["conv_ok"], 2)
            with dve.Fori(0, 3) as it:
                for j in range(RING):
                    dve.wait_ge(s["proj_taken"], 4 * it + (j + 3))
                    dve.wait_ge(s["mul_ok"], 4 * it + (j + 1))
                    for tap in range(CONV):
                        for i in range(2):
                            y = cy[:, j % 2, i * SEQ:(i + 1) * SEQ]
                            x = raw[:, j % 2, i, tap:tap + SEQ]
                            w = colsA[:, bass.ds(8 * it + (tap * 24 + 2 * j + i), 1)]
                            last = ts(y, x, w, ALU.mult) if tap == 0 else stt(y, x, w, y, ALU.mult, ALU.add)
                        if tap < CONV - 1:
                            dr()
                    last.then_inc(s["conv_ok"], 1)
            for t in range(TT):
                norm_out(1, t, mT)
            dve.wait_ge(s["tp_tr"], 1)
            dve.tensor_copy(TK[:, :, :, :].rearrange("p a b c -> p (a b c)"), PB[6][:, 0:4 * TT * HEADS])

            dr()
            for i in range(HEADS):
                dve.wait_ge(s["bc_mm"], i + 1)
                if i >= 2:
                    dve.wait_ge(s["ed_ok"], i - 1)
                for t in range(TT):
                    last = ts(ddh[i % 2][:, t, :], PB[2 + i % 2][:, t * P:(t + 1) * P], TK[:, 1, t, i:i + 1], ALU.subtract, 0.0, ALU.min)
                last.then_inc(s["dd_ok"], 1)
                dve.wait_ge(s["rinv_g"], i + 1)
                f = flat2(cT[:, 2 * i:2 * i + 2, :])
                if i < 4:
                    stt(f, f, SCALE, flat2(lnr[i % 2]), ALU.mult, ALU.mult).then_inc(s["qk_ok"], 1)
                else:
                    tt(f, f, flat2(lnr[i % 2]), ALU.mult).then_inc(s["qk_ok"], 1)
                dve.wait_ge(s["ed_ok"], i + 1)
                tt(EDm[:, i, :, :], EDm[:, i, :, :], mid(C[:, K_TRIU:K_TRIU + P], TT), ALU.mult)
                dr()
                tt(flat2(EDB[:, i, :, :]), flat2(EDm[:, i, :, :]), PB[2 + i % 2][:, SEQ:2 * SEQ], ALU.mult).then_inc(s["tab_ok"], 1)

            def before(b, part):
                B = b % 2
                e = slice(2 * b, 2 * b + 2)
                if part == 0:
                    dve.wait_ge(s["pre_mm"], b + 1)
                    tt(flat2(AT[B]), EDB[:, e, :, :].rearrange("p a b c -> p (a b c)"), PB[5], ALU.mult)
                    tt(flat2(QKm[B]), EDm[:, e, :, :].rearrange("p a b c -> p (a b c)"), PB[6], ALU.mult).then_inc(s["qkm_ok"], 1)
                elif part == 1:
                    for h in range(2):
                        for t in range(TT):
                            m = 2 * h + t
                            last = ts(kd[B][:, m, :], PB[7][:, m * P:(m + 1) * P], TK[:, 2 + t, t, 2 * b + h:2 * b + h + 1], ALU.mult)
                    last.then_inc(s["kd_ok"], 1)
                elif part == 2:
                    dve.wait_ge(s["vt_mm"], b + 1)
                    for h in range(2):
                        for t in range(TT):
                            m = 2 * h + t
                            last = ts(vb[B][:, m, :], PB[7][:, m * P:(m + 1) * P], TK[:, 0, t, 2 * b + h:2 * b + h + 1], ALU.mult)
                    last.then_inc(s["vb_ok"], 1)
                    tt(dd, AT[B], mid(levels[:, 0:P], 4), ALU.mult)
                elif part == 3:
                    dr()
                    tt(Um[B], mid(ident, 4), dd, ALU.subtract).then_inc(s["u0_ok"], 1)
                elif part == 4:
                    tt(qd[B], cT[:, e, P:SEQ], eG[:, e, :], ALU.mult).then_inc(s["qd_ok"], 1)

            def after(b, part):
                if part == 0:
                    dve.wait_ge(s["u_mm"], b + 1)
                    dve.tensor_copy(flat2(wT), PB[6][:, 0:SEQ]).then_inc(s["w_ok"], 1)
                elif part == 2:
                    dve.wait_ge(s["ws_mm"], b + 1)
                    tt(vn, u[:, 1:4:2, :], PB[6][:, 0:SEQ].rearrange("p (a b) -> p a b", b=P), ALU.subtract).then_inc(s["vn_ok"], 1)
                elif part == 4:
                    dve.wait_ge(s["lno_ok"], b + 1)
                    tt(flat2(oaT[:, 2 * b:2 * b + 2, :]), flat2(lno), PB[5], ALU.mult).then_inc(s["oa_ok"], 1)

            dve.wait_ge(s["lv_in"], 16)
            for part in range(5):
                before(0, part)
            for b in range(HEADS // 2):
                B = b % 2
                for lv in range(1, LEVELS):
                    for half in range(2):
                        gap = 2 * lv - 2 + half
                        if half:
                            dve.wait_ge(s["c_mm"], 6 * b + lv)
                            if lv < LEVELS - 1:
                                tt(flat2(Tm), flat2(Tm), PB[3], ALU.subtract)
                            tt(flat2(Um[B]), flat2(Um[B]), PB[4], ALU.subtract).then_inc(s["tu_ok"], 1)
                        if b and gap < 5:
                            after(b - 1, gap)
                        if b < 3 and gap >= 7:
                            before(b + 1, gap - 7)
            for part in range(5):
                after(3, part)

            dve.wait_ge(s["proj_taken"], N_XKV + 2)
            for v in range(2):
                for g in range(GROUPS):
                    win = big[:, 16 + 2 * v + g, :].rearrange("p (m b) -> p b m", b=CMP_STRIDE)
                    for half in range(2):
                        l = slice(half * CMP_STRIDE, (half + 1) * CMP_STRIDE)
                        pe_cols = colsB[:, CMP_LEN * v + half * CMP_STRIDE:CMP_LEN * v + (half + 1) * CMP_STRIDE]
                        last = tt(blk[:, v, l, g * NCMP:(g + 1) * NCMP], win[:, :, half:half + NCMP], bc(pe_cols, NCMP), ALU.add)
                last.then_inc(s["blk_ok"], 1)
            dve.wait_ge(s["zsig"], 1)
            tt(zs, zs, big[:, 0:8, :], ALU.mult)
            dr()
            stt(flat2(oaT), flat2(oaT), colsB[:, 2 * CMP_LEN:2 * CMP_LEN + 1], flat2(zs), ALU.mult, ALU.mult).then_inc(s["z_ok"], 1)
            dve.wait_ge(s["qcopy"], 1)
            dve.wait_ge(s["rope_in"], 16)
            cos, sin = R[:, R_COS:R_COS + SEQ], R[:, R_SIN:R_SIN + SEQ]
            for r in range(6):
                i = 8 + 2 * r if r < 4 else 20 + 2 * (r - 4)
                src = big[0:ROT, i:i + 2, :]
                dst = qr[0:ROT, 2 * r:2 * r + 2, :] if r < 4 else src
                dve.wait_ge(s["rope_mm"], r + 1)
                tt(rt1, src, mid(cos, 2), ALU.mult)
                tt(rt2, PB[2 + r % 2][0:ROT, :].rearrange("p (a b) -> p a b", b=SEQ), mid(sin, 2), ALU.mult)
                dr()
                tt(dst, rt1, rt2, ALU.add).then_inc(s["rope_ok"], 1)
                dr()
            for v in range(2):
                dve.wait_ge(s["proj_taken"], W1_AT[2 * v + 1] + 3)
                tt(s1[:, v, :], s1g[:, v, :], PB[4 + v][:, 0:GROUPS * NCMP], ALU.mult).then_inc(s["w1_act"], 1)
            dve.wait_ge(s["cs_mm"], 1)
            cps = PB[4][:, 0:TT * HEADS * 16].rearrange("p (t h n) -> p t h n", t=TT, n=16)
            for t in range(TT):
                stt(sc[:, t, :, :], cps[:, t, :, 0:NCMP], SCALE, mid(C[:, K_CMPA + t * NCMP:K_CMPA + (t + 1) * NCMP], HEADS), ALU.mult, ALU.add)
            dr()
            sc2 = sc.rearrange("p t h n -> p (t h) n")
            r1, r2 = small[:, 32:48], small[:, 48:64]
            dve.tensor_reduce(r1, sc2, AX.X, ALU.max)
            dr()
            tt(sc2, sc2, bc(r1, NCMP), ALU.subtract).then_inc(s["cs_max"], 1)
            dve.wait_ge(s["cs_exp"], 1)
            for t in range(TT):
                tt(sc[:, t, :, :], sc[:, t, :, :], mid(C[:, K_CMPM + t * NCMP:K_CMPM + (t + 1) * NCMP], HEADS), ALU.mult)
            dr()
            dve.tensor_reduce(r2, sc2, AX.X, ALU.add)
            dr()
            ts(r2, r2, 1e-30, ALU.max)
            dr()
            dve.reciprocal(r2, r2)
            dr()
            g3 = gates[:, :, :].rearrange("p t (h b) -> p t h b", b=3)
            tt(r2.rearrange("p (t h) -> p t h", t=TT), r2.rearrange("p (t h) -> p t h", t=TT), g3[:, :, :, 0], ALU.mult)
            dr()
            tt(sc2, sc2, bc(r2, NCMP), ALU.mult).then_inc(s["cs_ok"], 1)

            def maxima(i):
                st = steps[i]
                n, w = st["n"], st["n"] * P
                dve.wait_ge(s["sc_mm"], i + 1)
                if i >= 2:
                    dve.wait_ge(s["tp_mm"], i - 1)
                o = 1024 + 2 * (i % 2) * 512
                src = psum[:, o:o + REP * w].rearrange("p (a b) -> p a b", b=w)
                dst = st["S"][:, :, 0:w]
                if i < 8:
                    m = C[:, K_CAUSAL - (n - 1) * P:K_CAUSAL + P]
                    stt(dst, src, SCALE, mid(m, REP), ALU.mult, ALU.add).then_inc(s["sc_read"], 1)
                    dr()
                dve.tensor_reduce(smx[:, i % 2, :], dst if i < 8 else src, AX.X, ALU.max)
                dr()
                ts(smx[:, i % 2, :], smx[:, i % 2, :], -1.0 if i < 8 else -SCALE, ALU.mult).then_inc(s["mx_ok"], 1)

            def weights(i):
                st = steps[i]
                dst = st["S"][:, :, 0:st["n"] * P]
                r = ssum[:, i % 2, :]
                dve.wait_ge(s["ex_ok"], i + 1)
                dve.reciprocal(r, r)
                dr()
                if st["gate"] is not None:
                    tt(r, r, st["gate"][:, :, 0], ALU.mult)
                    dr()
                tt(dst, dst, bc(r, st["n"] * P), ALU.mult).then_inc(s["pn_ok"], 1)

            maxima(0)
            for i in range(8):
                if i < 7:
                    maxima(i + 1)
                weights(i)
            dve.wait_ge(s["mb_ok"], 1)
            tt(yaT, yaT, big[:, 24:32, :], ALU.mult)
            dve.wait_ge(s["proj_taken"], N_BB + 2)
            for n in range(N_BB, N_MIX):
                f = slice(2 * (n - N_BB), 2 * (n - N_BB) + 2)
                dve.wait_ge(s["proj_done"], n + 1)
                tt(flat2(mixT[:, f, :]), flat2(mb[:, f, :]), PB[n % 2], ALU.mult).then_inc(s["proj_taken"], 1)
                dr()
                tt(mixT[:, f, :], mixT[:, f, :], yaT[:, f, :], ALU.add).then_inc(s["mixed"], 1)

            def residual(n0, nth, t):
                for j in range(2):
                    if t == 0:
                        dve.wait_ge(s["res_mm"], 2 * nth + j + 1)
                    else:
                        dve.wait_ge(s["proj_done"], n0 + 2 * j + 2)
                    v = X[:, t, j * 512:(j + 1) * 512]
                    last = tt(v, v, PB[6 * t + j], ALU.add)
                    if t == 0:
                        last.then_inc(s["proj_taken"], 2)
                if t:
                    last.then_inc(s["res_ok"], 1)

            residual(N_MIX, 0, 0)
            scale_rows(2, 0, X, x2n)
            norm_out(2, 0, hT)
            residual(N_MIX, 0, 1)
            scale_rows(2, 1, X, x2n)
            norm_out(2, 1, hT)
            for j in range(2):
                maxima(8 + j)
                weights(8 + j)
            dve.memset(lwp[:, :, NE:], 3e38)
            residual(N_XO, 1, 0)
            scale_rows(3, 0, X, x3n)
            norm_out(3, 0, hT)
            residual(N_XO, 1, 1)

            def choose(t):
                dve.wait_ge(s["lg_mm"], t + 1)
                dve.tensor_copy(lg[:, t, :], PB[t][:, 0:NE])
                dve.tensor_copy(lwp[:, t, 0:NE], PB[t][:, 0:NE])
                dr()
                dve.max(top[:, t, :], lg[:, t, :])
                dr()
                ts(lw[:, t, :], lg[:, t, :], top[:, t, 0:1], ALU.subtract)
                dve.memset(top[:, t, TOPK:], 3e38)
                dr()
                dve.match_replace(left[:, t, :], top[:, t, :], lwp[:, t, :], -3e38)
                dr()
                return tt(msk[:, t, :], left[:, t, 0:NE], lg[:, t, :], ALU.is_lt)

            scale_rows(3, 1, X, x3n)
            choose(0)
            norm_out(3, 1, hT)
            choose(1).then_inc(s["lg_sub"], 1)
            dr().then_inc(s["lg_ok"], 1)
            dve.wait_ge(s["rk_mm"], 1)
            stt(cand.rearrange("p a b -> p (a b)"), PB[2][:, 0:TT * NE], 1.0, msk.rearrange("p a b -> p (a b)"), ALU.add, ALU.mult)
            dr()
            ts(rankT[:, 0:NE, :].rearrange("p e t -> p t e"), cand, 1.0, ALU.subtract)
            dr()
            def one_hot(t):
                for e in range(2):
                    for k in range(TT):
                        last = ts(Pg[:, k, e, :], C[:, K_IOTA:K_IOTA + CAP], rankT[:, bass.ds(2 * t + e, 1), k], ALU.is_equal)
                last.then_inc(s["pg_ok"], 1)

            def gated(t):
                for e in range(2):
                    for k in range(TT):
                        r, g = rankT[:, bass.ds(2 * t + e, 1), k], gateT[:, bass.ds(2 * t + e, 1), k]
                        last = ts(PGd[:, e, k, :], C[:, K_IOTA:K_IOTA + P], r, ALU.is_equal, g, ALU.mult)
                last.then_inc(s["pgd_ok"], 1)

            def selectors(t):
                for e in range(2):
                    last = dve.tensor_copy(bselv[0:B3, e * CAP:(e + 1) * CAP], selT[0:B3, bass.ds(2 * t + e, 1)].to_broadcast([B3, CAP]))
                last.then_inc(s["bsel_ok"], 1)

            def tokens(t):
                dve.wait_ge(s["gat_mm"], t + 1)
                g = gain(3)
                for i in range(2):
                    last = tt(xg[:, 4 * i:4 * i + 4, :, :].rearrange("p k e c -> p k (e c)"), PB[4 + i].rearrange("p (a b) -> p a b", b=P), bc(g[:, 4 * i:4 * i + 4], P), ALU.mult)
                last.then_inc(s["xg_ok"], 1)

            def swiglu(t, e):
                dve.wait_ge(s["gu_used"], 16 * t + 8 * (e + 1))
                ts(gg, PB[0], LIMIT, ALU.min).then_inc(s["act_g"], 1)
                ts(uu, PB[1], LIMIT, ALU.min, -LIMIT, ALU.max).then_inc(s["gu_taken"], 1)
                dr()
                stt(uu, uu, 1.0, gg, ALU.add, ALU.mult)
                dr()
                dve.wait_ge(s["act_s"], 2 * t + (e + 1))
                tt(hh, uu, sg, ALU.mult).then_inc(s["h_ok"], 1)

            def add_up(t, e):
                for k in range(TT):
                    dve.wait_ge(s["scat"], 4 * t + (2 * e + k + 1))
                    last = tt(X[:, k, :], X[:, k, :], psum[:, (4 + 2 * k) * 512:(6 + 2 * k) * 512], ALU.add)
                last.then_inc(s["acc_ok"], 1)

            def experts(t, first=False, carry=True):
                swiglu(t, 0)
                if carry and not first:
                    add_up(t - 1, 1)
                add_up(t, 0)
                dve.wait_ge(s["gat_mm"], t + 1)
                dve.wait_ge(s["pgt_mm"], t + 1)
                one_hot(t + 1)
                gated(t + 1)
                swiglu(t, 1)
                tokens(t + 1)
                dve.wait_ge(s["dn_used"], 16 * t + 16)
                selectors(t + 1)
                if not carry:
                    add_up(t, 1)

            dve.sem_inc(s["gu_taken"], 1)
            dve.sem_inc(s["acc_ok"], 1)
            one_hot(0)
            dve.wait_ge(s["lg_exp"], 1)
            dve.tensor_reduce(cmax[0:1, :], PB[2][0:1, 2 * NE:3 * NE], AX.X, ALU.max)
            tt(gate, gate, msk, ALU.mult)
            dr()
            dve.tensor_reduce(rsum, gate, AX.X, ALU.add)
            dve.tensor_copy(npass[0:1, 0:1], cmax[0:1, :]).then_inc(s["pass_ok"], 1)
            dr()
            dve.reciprocal(rsum, rsum)
            dr()
            tt(gate, gate, bc(rsum, NE), ALU.mult)
            dve.memset(rankT[:, PASSES * NE:, :], -1.0)
            dve.memset(gateT[:, PASSES * NE:, :], 0.0)
            dve.memset(selT[:, PASSES * NE:], 0.0)
            dve.tensor_copy(selT[:, 0:NE], C[:, K_SEL:K_SEL + NE])
            dr()
            dve.tensor_copy(gateT[:, 0:NE, :].rearrange("p e t -> p t e"), gate)
            selectors(0)
            dr()
            gated(0)
            tokens(0)
            for p in range(1, PASSES):
                e = slice(p * NE, (p + 1) * NE)
                ts(rankT[:, e, :].rearrange("p e t -> p t e"), cand, float(1 + p * CAP), ALU.subtract)
                dve.tensor_copy(gateT[:, e, :].rearrange("p e t -> p t e"), gate)
                dve.tensor_copy(selT[:, e], C[:, K_SEL:K_SEL + NE])
            dr()
            experts(0, True)
            with dve.Fori(1, NE // 2) as t:
                experts(t)
            add_up(NE // 2 - 1, 1)
            dve.wait_ge(s["pass_ok"], 1)
            many = dve.value_load(npass[0:1, 0:1], min_val=0, max_val=SEQ)
            with dve.If(many > CAP):
                with dve.Fori(NE // 2, PASSES * (NE // 2)) as t:
                    experts(t, carry=False)
            dr().then_inc(s["fin_acc"], 1)
            dve.wait_ge(s["fg_in"], 16)
            for t in range(TT):
                dve.wait_ge(s["rinv_n"], 9 + t)
                stt(X[:, t, :], X[:, t, :], stat[:, 4, 2, t:t + 1], fgb, ALU.mult, ALU.mult).then_inc(s["fin_ok"], 1)

        @block.gpsimd
        def _(pool):
            def tt(out, a0, a1, op=ALU.mult):
                return pool.tensor_tensor(out, a0, a1, op)

            gains_in(pool, ("gdn_conv_w", "attn_norm_g", "xattn_norm_g"), s["rows_in"])
            pool.dma_start(rowsB[0:32, :], a["cmp_pe_k"]).then_inc(s["rows_in"], 16)
            pool.dma_start(rowsB[32:64, :], a["cmp_pe_v"]).then_inc(s["rows_in"], 16)
            pool.dma_start(abias[:, 0:1], a["gdn_a_log"].rearrange("o h -> h o")).then_inc(s["ab_in"], 16)
            pool.dma_start(abias[:, 1:2], a["gdn_dt_bias"].rearrange("o h -> h o")).then_inc(s["ab_in"], 16)
            pool.sem_inc(s["mul_ok"], 2)
            pool.memset(raw, 0.0).then_inc(s["pads"], 1)
            with pool.Fori(0, 3) as it:
                for j in range(RING):
                    pool.wait_ge(s["sig_ok"], 4 * it + (j + 1))
                    tt(cT[:, bass.ds(8 * it + 2 * j, 2), :].rearrange("p a b -> p (a b)"), cy[:, j % 2, :], csg[:, j % 2, :]).then_inc(s["mul_ok"], 1)
            pool.drain()
            for i in range(HEADS):
                if i >= 2:
                    pool.wait_ge(s["ss_mm"], i - 1)
                f = flat2(cT[:, 2 * i:2 * i + 2, :])
                tt(flat2(sq[i % 2]), f, f).then_inc(s["sq_ok"], 1)
            pool.wait_ge(s["lv_in"], 16)
            for b in range(HEADS // 2):
                pool.wait_ge(s["u0_ok"], b + 1)
                for lv in range(1, LEVELS):
                    if lv > 1 or b:
                        pool.wait_ge(s["m1_mm"], 6 * b + lv - 1)
                    m = levels[:, lv * P:(lv + 1) * P]
                    tt(LT, AT[b % 2], m.unsqueeze(1).to_broadcast([P, 4, P])).then_inc(s["lt_ok"], 1)
            pool.wait_ge(s["oa_ok"], 4)
            pool.wait_ge(s["proj_taken"], N_XKV + 2)
            pool.tensor_copy(qr, big[:, 8:16, :]).then_inc(s["qcopy"], 1)
            pool.wait_ge(s["w1_act"], 2)
            for c in range(3):
                src = a["b_gate_up"][:, c * D:(c + 1) * D] if c < 2 else a["b_down"]
                bs = bspl[:, c * D:(c + 1) * D]
                for i in range(3):
                    pool.dma_start(btmp[i * NE:(i + 1) * NE, :], src).then_inc(s["bias_in"], 16)
                pool.wait_ge(s["bias_in"], 48 * (c + 1))
                pool.tensor_copy(bs, btmp)
                pool.drain()
                tt(btmp, btmp, bs, ALU.subtract)
                pool.drain()
                pool.tensor_copy(bmid, btmp)
                pool.drain()
                tt(btmp, btmp, bmid, ALU.subtract)
                pool.drain()
                pool.tensor_copy(bs[NE:2 * NE, :], bmid[NE:2 * NE, :])
                pool.drain()
                pool.tensor_copy(bs[2 * NE:3 * NE, :], btmp[2 * NE:3 * NE, :])
                pool.drain()
            pool.drain().then_inc(s["prep_ok"], 1)


_DEPTH = ["attn_norm_g", "w_in", "gdn_conv_w", "gdn_a_log", "gdn_dt_bias", "gdn_norm_g", "cmp_pe_k", "cmp_w1_k",
          "cmp_w2_k", "cmp_pe_v", "cmp_w1_v", "cmp_w2_v", "w_branch_a", "w_branch_b", "w_mix_out", "xattn_norm_g",
          "mem_norm_g", "xattn_w_q", "xattn_w_kv", "xattn_w_o", "ffn_norm_g", "router_w", "router_b", "w_gate_up",
          "b_gate_up", "w_down", "b_down"]
_ROWS = ("attn_norm_g", "xattn_norm_g", "mem_norm_g", "ffn_norm_g", "gdn_a_log", "gdn_dt_bias", "gdn_norm_g", "router_b")


def kernel(**inputs):
    import concourse.bacc as bacc
    from concourse.bass_utils import run_bass_kernel_spmd

    nc = bacc.Bacc("TRN2", target_bir_lowering=False, num_devices=1)
    arrays = {}
    for name in ["x", "mem", "final_norm_g"] + _DEPTH:
        v = np.ascontiguousarray(inputs[name])
        arrays[name] = v[0] if name in _DEPTH and name not in _ROWS else v
    arrays["tab"], arrays["levels"], arrays["rope"] = constants()
    aps = {n: nc.dram_tensor("in_" + n, v.shape, mybir.dt.from_np(v.dtype), kind="ExternalInput").ap() for n, v in arrays.items()}
    aps["out"] = nc.dram_tensor("out", (1, SEQ, D), mybir.dt.float32, kind="ExternalOutput").ap()
    build(nc, aps)
    r = run_bass_kernel_spmd(nc, [{"in_" + n: v for n, v in arrays.items()}], core_ids=[0])
    return r.results[0]["out"]
```
